# Optimizing a Trainium2 kernel written in Bass

```python
import math
import jax, jax.numpy as jnp
from jax import lax
import numpy as np

D_MODEL = 1024
BATCH = 1
SEQ = 512
DEPTH = 1

N_MIXERS = 3
NORM_EPS = 1e-6

RW_HEAD = 64
RW_HEADS = D_MODEL // RW_HEAD
RW_WIDTH = RW_HEADS * RW_HEAD
RW_DECAY_RANK = 64
RW_AAA_RANK = 64
RW_VRES_RANK = 32
RW_GN_EPS = 64e-5

SSD_EXPAND = 2
SSD_WIDTH = SSD_EXPAND * D_MODEL
SSD_HEAD = 64
SSD_HEADS = SSD_WIDTH // SSD_HEAD
SSD_GROUPS = 8
SSD_STATE = 128
SSD_CONV = 4
SSD_CHUNK = 128
SSD_CONV_DIM = SSD_WIDTH + 2 * SSD_GROUPS * SSD_STATE

SB_HEAD = 64
SB_HEADS = D_MODEL // SB_HEAD
SB_WIDTH = SB_HEADS * SB_HEAD
SB_BLOCK = 128
SB_SCALE = 1.0 / math.sqrt(SB_HEAD)


def rms_norm(u, g, eps=NORM_EPS):
    u32 = u.astype(jnp.float32)
    y = u32 * lax.rsqrt(jnp.mean(u32 * u32, axis=-1, keepdims=True) + eps)
    return (y * g.astype(jnp.float32)).astype(u.dtype)

def token_shift(h):
    return jnp.pad(h, ((0, 0), (1, 0), (0, 0)))[:, :-1]

def rwkv7_mixer(h, p, v_first):
    mu, w_in, w_up, w0, a_up, a0, k_k, k_a, r_k, gn_w, gn_b, w_out = p[:12]
    Bsz, T, _ = h.shape
    W, H, N = RW_WIDTH, RW_HEADS, RW_HEAD
    dx = token_shift(h) - h
    x_r, x_w, x_k, x_v, x_a, x_g = (h + dx * mu[i] for i in range(6))
    c = np.cumsum([0, W, W, W, W, RW_DECAY_RANK, RW_AAA_RANK])
    r = x_r @ w_in[:, c[0]:c[1]]
    k = x_k @ w_in[:, c[1]:c[2]]
    v = x_v @ w_in[:, c[2]:c[3]]
    g = jax.nn.silu(x_g @ w_in[:, c[3]:c[4]])
    w_lo = jnp.tanh(x_w @ w_in[:, c[4]:c[5]])
    a_lo = x_a @ w_in[:, c[5]:c[6]]
    f32 = jnp.float32
    w_raw = (w0 + w_lo @ w_up).astype(f32)
    log_decay = -jnp.exp(-jax.nn.softplus(-w_raw) - 0.5)
    a = jax.nn.sigmoid((a0 + a_lo @ a_up).astype(f32))
    if v_first is None:
        v_first = v
    else:
        v_up, v0 = p[12:]
        v_lo = x_v @ w_in[:, c[6]:]
        v = v + (v_first - v) * jax.nn.sigmoid(v0 + v_lo @ v_up)

    def heads(t):
        return t.astype(f32).reshape(Bsz, T, H, N)

    kk = heads(k * k_k)
    kk = kk / jnp.maximum(jnp.sqrt(jnp.sum(kk * kk, axis=-1, keepdims=True)), 1e-12)
    k = k.astype(f32) * (1.0 + (a - 1.0) * k_a.astype(f32))
    r_h, k_h, v_h, a_h = heads(r), heads(k), heads(v), heads(a)
    decay_h = jnp.exp(heads(log_decay))

    def step(S, inp):
        r_t, w_t, k_t, v_t, kk_t, a_t = inp
        sa = jnp.einsum('bhvk,bhk->bhv', S, -kk_t)
        S = (S * w_t[:, :, None, :]
             + sa[..., None] * (kk_t * a_t)[:, :, None, :]
             + v_t[..., None] * k_t[:, :, None, :])
        y_t = jnp.einsum('bhvk,bhk->bhv', S, r_t)
        return S, y_t

    tm = lambda t: jnp.moveaxis(t, 1, 0)
    S0 = jnp.zeros((Bsz, H, N, N), f32)
    _, y = lax.scan(step, S0, (tm(r_h), tm(decay_h), tm(k_h), tm(v_h), tm(kk), tm(a_h)))
    y = jnp.moveaxis(y, 0, 1)
    mean = jnp.mean(y, axis=-1, keepdims=True)
    var = jnp.mean(jnp.square(y - mean), axis=-1, keepdims=True)
    y = (y - mean) * lax.rsqrt(var + RW_GN_EPS)
    y = y * gn_w.astype(f32).reshape(H, N) + gn_b.astype(f32).reshape(H, N)
    y = y + jnp.sum(r_h * k_h * r_k.astype(f32), axis=-1, keepdims=True) * v_h
    y = y.reshape(Bsz, T, W).astype(h.dtype) * g
    return y @ w_out, v_first

def causal_depthwise_conv(u, w, b):
    out = lax.conv_general_dilated(
        u, w[:, None, :].astype(u.dtype), window_strides=(1,),
        padding=[(w.shape[0] - 1, 0)], dimension_numbers=('NWC', 'WIO', 'NWC'),
        feature_group_count=u.shape[-1])
    return out + b

def ssd_chunked(x, a, Bm, Cm):
    Bsz, T, H, P = x.shape
    G, R, l = SSD_GROUPS, H // SSD_GROUPS, SSD_CHUNK
    nc = T // l
    x = x.reshape(Bsz, nc, l, G, R, P)
    Bm = Bm.reshape(Bsz, nc, l, G, SSD_STATE)
    Cm = Cm.reshape(Bsz, nc, l, G, SSD_STATE)
    ac = jnp.cumsum(jnp.moveaxis(a.reshape(Bsz, nc, l, G, R), 2, -1), axis=-1)
    causal = jnp.tril(jnp.ones((l, l), bool))
    seg = ac[..., :, None] - ac[..., None, :]
    decay_in = jnp.exp(jnp.where(causal, seg, -jnp.inf))
    cb = jnp.einsum('bclgn,bcsgn->bcgls', Cm, Bm)
    y_diag = jnp.einsum('bcgrls,bcsgrp->bclgrp', cb[:, :, :, None] * decay_in, x)
    decay_states = jnp.moveaxis(jnp.exp(ac[..., -1:] - ac), -1, 2)
    states = jnp.einsum('bclgn,bclgrp->bcgrpn', Bm, x * decay_states[..., None])
    chunk_decay = ac[..., -1]

    def chunk_step(h_prev, inp):
        st, dec = inp
        return h_prev * jnp.exp(dec)[..., None, None] + st, h_prev

    h0 = jnp.zeros((Bsz, G, R, P, SSD_STATE), x.dtype)
    _, h_in = lax.scan(chunk_step, h0, (jnp.moveaxis(states, 1, 0), jnp.moveaxis(chunk_decay, 1, 0)))
    h_in = jnp.moveaxis(h_in, 0, 1)
    decay_out = jnp.moveaxis(jnp.exp(ac), -1, 2)
    y_off = jnp.einsum('bclgn,bcgrpn->bclgrp', Cm, h_in) * decay_out[..., None]
    return (y_diag + y_off).reshape(Bsz, T, H, P)

def mamba2_mixer(h, p):
    w_in, conv_w, conv_b, dt_bias, a_log, d_skip, gnorm_w, w_out = p
    Bsz, T, _ = h.shape
    f32 = jnp.float32
    proj = h @ w_in
    z = proj[..., :SSD_WIDTH]
    xbc = proj[..., SSD_WIDTH:SSD_WIDTH + SSD_CONV_DIM]
    dt_raw = proj[..., SSD_WIDTH + SSD_CONV_DIM:]
    xbc = jax.nn.silu(causal_depthwise_conv(xbc, conv_w, conv_b)).astype(f32)
    gn = SSD_GROUPS * SSD_STATE
    xs = xbc[..., :SSD_WIDTH].reshape(Bsz, T, SSD_HEADS, SSD_HEAD)
    Bm = xbc[..., SSD_WIDTH:SSD_WIDTH + gn].reshape(Bsz, T, SSD_GROUPS, SSD_STATE)
    Cm = xbc[..., SSD_WIDTH + gn:].reshape(Bsz, T, SSD_GROUPS, SSD_STATE)
    dt = jax.nn.softplus((dt_raw + dt_bias).astype(f32))
    A = -jnp.exp(a_log.astype(f32))
    y = ssd_chunked(xs * dt[..., None], dt * A, Bm, Cm)
    y = y + xs * d_skip.astype(f32)[:, None]
    y = y.reshape(Bsz, T, SSD_WIDTH) * jax.nn.silu(z.astype(f32))
    y = y.reshape(Bsz, T, SSD_GROUPS, SSD_WIDTH // SSD_GROUPS)
    y = y * lax.rsqrt(jnp.mean(y * y, axis=-1, keepdims=True) + NORM_EPS)
    y = y.reshape(Bsz, T, SSD_WIDTH) * gnorm_w.astype(f32)
    return y.astype(h.dtype) @ w_out

def stick_breaking_mixer(h, p):
    w_in, q_norm, k_norm, w_out = p
    Bsz, T, _ = h.shape
    f32 = jnp.float32
    proj = h @ w_in
    W = SB_WIDTH
    q = rms_norm(proj[..., :W].reshape(Bsz, T, SB_HEADS, SB_HEAD), q_norm).astype(f32)
    k = rms_norm(proj[..., W:2 * W].reshape(Bsz, T, SB_HEADS, SB_HEAD), k_norm).astype(f32)
    v = proj[..., 2 * W:3 * W].reshape(Bsz, T, SB_HEADS, SB_HEAD).astype(f32)
    g = jax.nn.silu(proj[..., 3 * W:])
    outs = []
    for blk in range(T // SB_BLOCK):
        start, end = blk * SB_BLOCK, (blk + 1) * SB_BLOCK
        qb, kb, vb = q[:, start:end], k[:, :end], v[:, :end]
        z = jnp.einsum('bthd,bshd->bhts', qb, kb) * SB_SCALE
        t_idx = start + jnp.arange(SB_BLOCK)
        s_idx = jnp.arange(end)
        strict = s_idx[None, :] < t_idx[:, None]
        log_beta = jax.nn.log_sigmoid(z)
        log_1m_beta = jnp.where(strict, log_beta - z, 0.0)
        tail = lax.cumsum(log_1m_beta, axis=3, reverse=True) - log_1m_beta
        att = jnp.where(strict, jnp.exp(log_beta + tail), 0.0)
        outs.append(jnp.einsum('bhts,bshd->bthd', att, vb))
    o = jnp.concatenate(outs, axis=1).reshape(Bsz, T, W).astype(h.dtype)
    return (o * g) @ w_out

def _normal(key, shape, scale):
    return scale * jax.random.normal(key, shape, jnp.float32)

def _rwkv_params(key, prefix, value_residual):
    ks = jax.random.split(key, 16)
    W = RW_WIDTH
    n_cols = 4 * W + RW_DECAY_RANK + RW_AAA_RANK + (RW_VRES_RANK if value_residual else 0)
    p = {
        prefix + "norm": 1.0 + _normal(ks[0], (D_MODEL,), 0.05),
        prefix + "mu": jax.random.uniform(ks[1], (6, D_MODEL), jnp.float32),
        prefix + "w_in": _normal(ks[2], (D_MODEL, n_cols), D_MODEL ** -0.5),
        prefix + "w_up": _normal(ks[3], (RW_DECAY_RANK, W), 0.5 * RW_DECAY_RANK ** -0.5),
        prefix + "w0": jax.random.uniform(ks[4], (W,), jnp.float32, -6.0, 1.0),
        prefix + "a_up": _normal(ks[5], (RW_AAA_RANK, W), 0.5 * RW_AAA_RANK ** -0.5),
        prefix + "a0": _normal(ks[6], (W,), 0.5),
        prefix + "k_k": 0.85 + _normal(ks[7], (W,), 0.05),
        prefix + "k_a": 1.0 + _normal(ks[8], (W,), 0.05),
        prefix + "r_k": _normal(ks[9], (RW_HEADS, RW_HEAD), 0.1),
        prefix + "gn_w": 1.0 + _normal(ks[10], (W,), 0.05),
        prefix + "gn_b": _normal(ks[11], (W,), 0.01),
        prefix + "w_out": _normal(ks[12], (W, D_MODEL), W ** -0.5),
    }
    if value_residual:
        p[prefix + "v_up"] = _normal(ks[13], (RW_VRES_RANK, W), 0.5 * RW_VRES_RANK ** -0.5)
        p[prefix + "v0"] = _normal(ks[14], (W,), 0.5)
    return p

def _mamba2_params(key, prefix):
    ks = jax.random.split(key, 10)
    n_cols = SSD_WIDTH + SSD_CONV_DIM + SSD_HEADS
    dt = jnp.exp(jax.random.uniform(ks[4], (SSD_HEADS,), jnp.float32, math.log(1e-3), math.log(1e-1)))
    return {
        prefix + "norm": 1.0 + _normal(ks[0], (D_MODEL,), 0.05),
        prefix + "w_in": _normal(ks[1], (D_MODEL, n_cols), D_MODEL ** -0.5),
        prefix + "conv_w": _normal(ks[2], (SSD_CONV, SSD_CONV_DIM), SSD_CONV ** -0.5),
        prefix + "conv_b": _normal(ks[3], (SSD_CONV_DIM,), 0.01),
        prefix + "dt_bias": dt + jnp.log(-jnp.expm1(-dt)),
        prefix + "a_log": jnp.log(jax.random.uniform(ks[5], (SSD_HEADS,), jnp.float32, 1.0, 16.0)),
        prefix + "d_skip": 1.0 + _normal(ks[6], (SSD_HEADS,), 0.05),
        prefix + "gnorm_w": 1.0 + _normal(ks[7], (SSD_WIDTH,), 0.05),
        prefix + "w_out": _normal(ks[8], (SSD_WIDTH, D_MODEL), SSD_WIDTH ** -0.5),
    }

def _stickbreak_params(key, prefix):
    ks = jax.random.split(key, 5)
    return {
        prefix + "norm": 1.0 + _normal(ks[0], (D_MODEL,), 0.05),
        prefix + "w_in": _normal(ks[1], (D_MODEL, 4 * SB_WIDTH), D_MODEL ** -0.5),
        prefix + "q_norm": 1.0 + _normal(ks[2], (SB_HEAD,), 0.05),
        prefix + "k_norm": 1.0 + _normal(ks[3], (SB_HEAD,), 0.05),
        prefix + "w_out": _normal(ks[4], (SB_WIDTH, D_MODEL), SB_WIDTH ** -0.5),
    }

def first_inputs(seed: int = 0) -> dict:
    key = jax.random.key(seed)
    kx, k0, k1, k2, k3 = jax.random.split(key, 5)
    inputs = {"x": jax.random.normal(kx, (BATCH, SEQ, D_MODEL), jnp.float32)}
    inputs.update(_rwkv_params(k0, "l0_", value_residual=False))
    inputs.update(_mamba2_params(k1, "l1_"))
    inputs.update(_stickbreak_params(k2, "l2_"))
    inputs.update(_rwkv_params(k3, "l3_", value_residual=True))
    return inputs

def first_block(x,
              l0_norm, l0_mu, l0_w_in, l0_w_up, l0_w0, l0_a_up, l0_a0, l0_k_k, l0_k_a, l0_r_k,
              l0_gn_w, l0_gn_b, l0_w_out,
              l1_norm, l1_w_in, l1_conv_w, l1_conv_b, l1_dt_bias, l1_a_log, l1_d_skip, l1_gnorm_w,
              l1_w_out,
              l2_norm, l2_w_in, l2_q_norm, l2_k_norm, l2_w_out,
              l3_norm, l3_mu, l3_w_in, l3_w_up, l3_w0, l3_a_up, l3_a0, l3_k_k, l3_k_a, l3_r_k,
              l3_gn_w, l3_gn_b, l3_w_out, l3_v_up, l3_v0):
    layer_params = [
        (l0_norm, (l0_mu, l0_w_in, l0_w_up, l0_w0, l0_a_up, l0_a0, l0_k_k, l0_k_a, l0_r_k,
                   l0_gn_w, l0_gn_b, l0_w_out)),
        (l1_norm, (l1_w_in, l1_conv_w, l1_conv_b, l1_dt_bias, l1_a_log, l1_d_skip, l1_gnorm_w,
                   l1_w_out)),
        (l2_norm, (l2_w_in, l2_q_norm, l2_k_norm, l2_w_out)),
        (l3_norm, (l3_mu, l3_w_in, l3_w_up, l3_w0, l3_a_up, l3_a0, l3_k_k, l3_k_a, l3_r_k,
                   l3_gn_w, l3_gn_b, l3_w_out, l3_v_up, l3_v0)),
    ]
    v_first = None
    for i in range(DEPTH):
        norm_g, p = layer_params[i]
        h = rms_norm(x, norm_g)
        kind = i % N_MIXERS
        if kind == 0:
            y, v_first = rwkv7_mixer(h, p, v_first)
        elif kind == 1:
            y = mamba2_mixer(h, p)
        else:
            y = stick_breaking_mixer(h, p)
        x = x + y.astype(x.dtype)
    return x


CTX_LEN = 256
GRID_W = 64
F_WIDTH = D_MODEL // 2
F_GROUPS = 4
F_GROUP_DIM = F_WIDTH // F_GROUPS
HEAD_DIM = 64
NA_WIDTH = D_MODEL - F_WIDTH
NA_HEADS = NA_WIDTH // HEAD_DIM
MIX_WIDTH = F_WIDTH + NA_WIDTH
IN_COLS = 2 * F_WIDTH + 4 * NA_WIDTH
WIN_ROWS_MAX = 8
WIN_COLS = 16
EPS = 1e-6
NEG_INF = -1e30


def _rms_norm(t, g):
    t32 = t.astype(jnp.float32)
    y = t32 * lax.rsqrt(jnp.mean(t32 * t32, axis=-1, keepdims=True) + EPS)
    return (y * g.astype(jnp.float32)).astype(t.dtype)

def _ada(cond, w_ada, b_ada):
    mod = jax.nn.silu(cond) @ w_ada + b_ada
    return jnp.split(mod, 3, axis=-1)

def _split_proj(p):
    f_in = p[..., :F_WIDTH]
    f_gate = p[..., F_WIDTH:2 * F_WIDTH]
    q, k, v, na_gate = jnp.split(p[..., 2 * F_WIDTH:], 4, axis=-1)
    return f_in, f_gate, q, k, v, na_gate

def _heads(t):
    return t.reshape(t.shape[0], t.shape[1], NA_HEADS, HEAD_DIM)

def _fourier(u, w_four):
    b, l, _ = u.shape
    ug = u.reshape(b, l, F_GROUPS, F_GROUP_DIM).astype(jnp.float32)
    y = jnp.real(jnp.fft.fft2(ug, axes=(1, 3))) * ((l * F_GROUP_DIM) ** -0.5)
    y = y.reshape(b, l, F_WIDTH).astype(u.dtype)
    return y @ w_four

def _ctx_attention(qc, kc, vc):
    s = jnp.einsum('bqhd,bkhd->bhqk', qc, kc, preferred_element_type=jnp.float32) * (HEAD_DIM ** -0.5)
    p = jax.nn.softmax(s, axis=-1).astype(vc.dtype)
    o = jnp.einsum('bhqk,bkhd->bqhd', p, vc)
    return o.reshape(o.shape[0], o.shape[1], NA_WIDTH)

def _neighbourhood_attention(q, k, v, kc, vc, rel_bias):
    b, l, h, d = q.shape
    rows = l // GRID_W
    wr = min(WIN_ROWS_MAX, rows)
    r_ar = jnp.arange(rows)
    rs = jnp.clip(r_ar - wr // 2, 0, rows - wr)
    row_idx = rs[:, None] + jnp.arange(wr)[None, :]
    col_ar = jnp.arange(GRID_W)
    cs = jnp.clip(col_ar - WIN_COLS // 2, 0, GRID_W - WIN_COLS)
    in_win = (col_ar[None, :] >= cs[:, None]) & (col_ar[None, :] < cs[:, None] + WIN_COLS)
    mask = jnp.broadcast_to(in_win[:, None, :], (GRID_W, wr, GRID_W)).reshape(GRID_W, wr * GRID_W)
    dr_idx = row_idx - r_ar[:, None] + (WIN_ROWS_MAX - 1)
    dc_idx = jnp.clip(col_ar[None, :] - col_ar[:, None], -(WIN_COLS - 1), WIN_COLS - 1) + (WIN_COLS - 1)
    bias = rel_bias[:, dr_idx[:, None, :, None], dc_idx[None, :, None, :]]
    bias = bias.reshape(h, rows, GRID_W, wr * GRID_W).astype(jnp.float32)
    qg = q.reshape(b, rows, GRID_W, h, d)
    k_rows = k.reshape(b, rows, GRID_W, h, d)[:, row_idx].reshape(b, rows, wr * GRID_W, h, d)
    v_rows = v.reshape(b, rows, GRID_W, h, d)[:, row_idx].reshape(b, rows, wr * GRID_W, h, d)
    scale = HEAD_DIM ** -0.5
    s_loc = jnp.einsum('brqhd,brkhd->bhrqk', qg, k_rows, preferred_element_type=jnp.float32) * scale
    s_loc = jnp.where(mask[None, None, None], s_loc + bias[None], NEG_INF)
    s_ctx = jnp.einsum('brqhd,bkhd->bhrqk', qg, kc, preferred_element_type=jnp.float32) * scale
    p = jax.nn.softmax(jnp.concatenate([s_loc, s_ctx], axis=-1), axis=-1).astype(v.dtype)
    n_loc = wr * GRID_W
    o = (jnp.einsum('bhrqk,brkhd->brqhd', p[..., :n_loc], v_rows)
         + jnp.einsum('bhrqk,bkhd->brqhd', p[..., n_loc:], vc))
    return o.reshape(b, l, NA_WIDTH)

def second_inputs(seed: int = 0) -> dict:
    key = jax.random.key(seed)
    ks = jax.random.split(key, 14)
    f32 = jnp.float32
    n = lambda k, shape: jax.random.normal(k, shape, f32)
    return {
        "x": n(ks[0], (BATCH, SEQ, D_MODEL)),
        "c": n(ks[1], (BATCH, D_MODEL)),
        "ctx": n(ks[2], (BATCH, CTX_LEN, D_MODEL)),
        "c_ctx": n(ks[3], (D_MODEL,)),
        "norm_g": 1.0 + 0.02 * n(ks[4], (DEPTH, D_MODEL)),
        "w_ada": n(ks[5], (DEPTH, D_MODEL, 3 * D_MODEL)) * D_MODEL ** -0.5,
        "b_ada": 0.02 * n(ks[6], (DEPTH, 3 * D_MODEL)),
        "w_in": n(ks[7], (DEPTH, D_MODEL, IN_COLS)) * D_MODEL ** -0.5,
        "w_four": n(ks[8], (DEPTH, F_WIDTH, F_WIDTH)) * F_WIDTH ** -0.5,
        "q_norm_g": 1.0 + 0.02 * n(ks[9], (DEPTH, HEAD_DIM)),
        "k_norm_g": 1.0 + 0.02 * n(ks[10], (DEPTH, HEAD_DIM)),
        "rel_bias": 0.02 * n(ks[11], (DEPTH, NA_HEADS, 2 * WIN_ROWS_MAX - 1, 2 * WIN_COLS - 1)),
        "w_out": n(ks[12], (DEPTH, MIX_WIDTH, D_MODEL)) * MIX_WIDTH ** -0.5,
    }

def second_block(x, c, ctx, c_ctx, norm_g, w_ada, b_ada, w_in, w_four, q_norm_g, k_norm_g, rel_bias, w_out):
    for l in range(DEPTH):
        last = l == DEPTH - 1
        sh_x, sc_x, g_x = [t[:, None, :] for t in _ada(c, w_ada[l], b_ada[l])]
        sh_c, sc_c, g_c = _ada(c_ctx, w_ada[l], b_ada[l])
        xn = _rms_norm(x, norm_g[l]) * (1.0 + sc_x) + sh_x
        cn = _rms_norm(ctx, norm_g[l]) * (1.0 + sc_c) + sh_c
        fx_in, fx_gate, qx, kx, vx, nx_gate = _split_proj(xn @ w_in[l])
        fc_in, fc_gate, qc, kc, vc, nc_gate = _split_proj(cn @ w_in[l])
        qx = _rms_norm(_heads(qx), q_norm_g[l])
        kx = _rms_norm(_heads(kx), k_norm_g[l])
        vx = _heads(vx)
        qc = _rms_norm(_heads(qc), q_norm_g[l])
        kc = _rms_norm(_heads(kc), k_norm_g[l])
        vc = _heads(vc)
        f_out = _fourier(fx_in, w_four[l]) * jax.nn.silu(fx_gate)
        na_out = _neighbourhood_attention(qx, kx, vx, kc, vc, rel_bias[l]) * jax.nn.silu(nx_gate)
        x_new = x + g_x * (jnp.concatenate([f_out, na_out], axis=-1) @ w_out[l])
        if not last:
            fc_out = _fourier(fc_in, w_four[l]) * jax.nn.silu(fc_gate)
            nc_out = _ctx_attention(qc, kc, vc) * jax.nn.silu(nc_gate)
            ctx = ctx + g_c * (jnp.concatenate([fc_out, nc_out], axis=-1) @ w_out[l])
        x = x_new
    return x


def setup_inputs(seed=0):
    out = dict(first_inputs(seed))
    for name, value in second_inputs(seed + 1).items():
        if name != "x":
            out[name + "_2"] = value
    return out


def reference(
    x, l0_norm, l0_mu, l0_w_in, l0_w_up, l0_w0, l0_a_up, l0_a0, l0_k_k, l0_k_a, l0_r_k, l0_gn_w,
    l0_gn_b, l0_w_out, l1_norm, l1_w_in, l1_conv_w, l1_conv_b, l1_dt_bias, l1_a_log, l1_d_skip,
    l1_gnorm_w, l1_w_out, l2_norm, l2_w_in, l2_q_norm, l2_k_norm, l2_w_out, l3_norm, l3_mu,
    l3_w_in, l3_w_up, l3_w0, l3_a_up, l3_a0, l3_k_k, l3_k_a, l3_r_k, l3_gn_w, l3_gn_b, l3_w_out,
    l3_v_up, l3_v0, c_2, ctx_2, c_ctx_2, norm_g_2, w_ada_2, b_ada_2, w_in_2, w_four_2,
    q_norm_g_2, k_norm_g_2, rel_bias_2, w_out_2,
):
    x = first_block(
        x, l0_norm, l0_mu, l0_w_in, l0_w_up, l0_w0, l0_a_up, l0_a0, l0_k_k, l0_k_a, l0_r_k,
        l0_gn_w, l0_gn_b, l0_w_out, l1_norm, l1_w_in, l1_conv_w, l1_conv_b, l1_dt_bias,
        l1_a_log, l1_d_skip, l1_gnorm_w, l1_w_out, l2_norm, l2_w_in, l2_q_norm, l2_k_norm,
        l2_w_out, l3_norm, l3_mu, l3_w_in, l3_w_up, l3_w0, l3_a_up, l3_a0, l3_k_k, l3_k_a,
        l3_r_k, l3_gn_w, l3_gn_b, l3_w_out, l3_v_up, l3_v0,
    )
    return second_block(
        x, c_2, ctx_2, c_ctx_2, norm_g_2, w_ada_2, b_ada_2, w_in_2, w_four_2, q_norm_g_2,
        k_norm_g_2, rel_bias_2, w_out_2,
    )


_drawn_inputs = setup_inputs


def setup_inputs(seed=0):
    import zlib

    import numpy as np

    out = dict(_drawn_inputs(seed))
    spreads = {}
    factors = {'l0_w_up': 5.234,
     'l0_k_k': 3.035,
     'l0_gn_b': 8.0,
     'norm_g_2': 7.303,
     'b_ada_2': 3.648,
     'q_norm_g_2': 8.0,
     'k_norm_g_2': 8.0,
     'rel_bias_2': 46.808}
    for name, (base, spread) in spreads.items():
        noise = np.random.default_rng([zlib.crc32(name.encode()), seed]).standard_normal(out[name].shape)
        drawn = base * np.exp(spread * noise) if base else spread * noise
        out[name] = __import__('jax').numpy.asarray(drawn.astype(out[name].dtype))
    for name, factor in factors.items():
        out[name] = (out[name] * factor).astype(out[name].dtype)
    return out
```

```python
import math
from contextlib import ExitStack

import numpy as np

import concourse.bass as bass
from concourse import mybir

T, D, P = 512, 1024, 128
KT, NT = D // P, T // P
PAIRS, HEADS, HD = 8, 16, 64
LEVELS = 7
GROUPS = NT * 4
CTX, NAH, GW, GH = 256, 8, 64, 8
WIN = 256
PADT = T + 2 * HD
KAPPA = math.exp(-0.5)
NORM_EPS, GN_EPS = 1e-6, 64e-5
RB = 15 * 31
RBW = 7 * 31 + 32
RBPAD = 8

CONST = {}
_at = 0
for _n, _w in [("ident", P), ("heads", P), ("gram", 2 * P), ("level", LEVELS * HD), ("ones", P),
               ("dft128", 2 * P), ("eps", 3)]:
    CONST[_n] = (_at, _w)
    _at += _w
CONST_W = _at
VEC = {n: KT * i for i, n in enumerate(
    ["norm", "mu_r", "mu_w", "mu_k", "mu_v", "mu_a", "mu_g", "w0", "a0", "k_k", "k_a", "r_k", "gn_w", "gn_b",
     "c", "c_ctx", "norm2", "b_shift", "b_scale"])}
VEC["q_gain"] = KT * len(VEC)
VEC["k_gain"] = VEC["q_gain"] + 1
VEC_W = VEC["k_gain"] + 1


def shape_constants():
    f = np.float32
    i, j = np.arange(P)[:, None], np.arange(P)[None, :]
    strict, incl = (i < j).astype(f), (i <= j).astype(f)
    c = np.zeros((P, CONST_W), f)

    def put(name, a):
        at, w = CONST[name]
        c[:, at:at + w] = a

    put("ident", np.eye(P, dtype=f))
    put("heads", (i // HD == j // HD).astype(f))
    put("gram", np.concatenate([strict, incl], 1))
    levels = []
    for l in range(LEVELS):
        b = 1 << l
        even = np.concatenate([np.arange(s, s + b) for s in range(0, P, 2 * b)])
        levels.append((i // b == even[None, :] // b + 1).astype(f))
    put("level", np.concatenate(levels, 1))
    put("ones", 1.0)
    cl, key = np.arange(P)[:, None] // GH, np.arange(WIN)[None, :] // GH
    near = []
    for tile in (0, 1, 3):
        q, k = 16 * tile + cl, 16 * tile - 8 + key
        first = np.clip(q - 8, 0, GW - 16)
        near.append(np.where((k >= first) & (k < first + 16), 0.0, -1e30).astype(f))
    w = 2 * np.pi * ((i * j) % P) / P
    put("dft128", np.concatenate([np.cos(w), np.sin(w)], 1) / 256.0)
    put("eps", np.array([[NORM_EPS, GN_EPS, HD * NORM_EPS]], f))
    order = np.array([r * GW + col for col in range(GW) for r in range(GH)])
    w = 2 * np.pi * ((order[:, None] * order[None, :]) % T) / T
    return c, np.cos(w).astype(f), (-np.sin(w)).astype(f), np.concatenate(near, 1)


def rwkv_then_grid_block(nc, x, vecs, consts, cos_t, nsin_t, near, ident_b, w_in, w_up, a_up, w_out,
                         ctx_x, w_ada, b_gate, w_in2, w_four, rel_bias, w_out2, out):
    f32, bf16 = mybir.dt.float32, mybir.dt.bfloat16
    ALU, ACT, AX = mybir.AluOpType, mybir.ActivationFunctionType, mybir.AxisListType
    MUL, ADD, SUB, MAX = ALU.mult, ALU.add, ALU.subtract, ALU.max

    stack = ExitStack()
    with stack:
        def sem(name):
            return stack.enter_context(nc.semaphore(name))

        arena = stack.enter_context(nc.sbuf_tensor("arena", [P, 52900], f32))
        idb = stack.enter_context(nc.sbuf_tensor("idb", [P, 4 * P], bf16))
        banks = [stack.enter_context(nc.psum_tensor(f"bank{b}", [P, 512], f32)) for b in range(8)]

        class Room:
            def __init__(self, at, end):
                self.at, self.end = at, end

            def take(self, width, parts=P):
                at = self.at
                self.at += width
                assert self.at <= self.end, (self.at, self.end)
                return arena[0:parts, at:at + width]

        fixed = Room(0, 52900)
        CON = fixed.take(CONST_W)
        VECS = fixed.take(VEC_W)
        NVEC = fixed.take(VEC_W)
        SMALL = fixed.take(700)
        WR = [fixed.take(2048) for _ in range(3)]

        def con(name):
            at, w = CONST[name]
            return CON[:, at:at + w]

        def vec(name, c, n=1):
            return VECS[:, VEC[name] + c:VEC[name] + c + n]

        def nvec(name, c, n=1):
            return NVEC[:, VEC[name] + c:VEC[name] + c + n]

        ident, heads1, gram_mask = con("ident"), con("heads"), con("gram")
        sm = Room(0, 700)

        def small(w):
            at = sm.at
            sm.at += w
            assert sm.at <= 700
            return SMALL[:, at:at + w]

        rstd = small(4)
        ssq = small(4)
        F = small(32).rearrange("p (c j) -> p c j", j=4)
        BON = small(64)
        RKB = small(16).rearrange("p (c h) -> p c h", h=2)
        MID = small(12)
        GST = small(64 * 3)
        SILC = small(16).rearrange("p (c k) -> p c k", k=2)
        SILT = small(32)
        MODS = small(32).rearrange("p (c k) -> p c k", k=2)
        GSC = small(16).rearrange("p (c k) -> p c k", k=2)
        CST = small(8)
        MXN = small(32)
        SUMS = small(80)
        NKA = small(KT)
        MXN2 = small(4)

        base = fixed.at
        roomA = Room(base, 52900)
        AR = roomA.take(8192).rearrange("p (s c t) -> p s c t", s=2, c=KT)
        KB = roomA.take(4096).rearrange("p (c t) -> p c t", c=KT)
        AB = roomA.take(4096).rearrange("p (c t) -> p c t", c=KT)
        V = roomA.take(4096).rearrange("p (t n) -> p t n", t=NT)
        HT_ = roomA.take(KT * 513)
        HT = HT_.rearrange("p (c t) -> p c t", c=KT)
        GT = HT_[:, 0:4096].rearrange("p (c t) -> p c t", c=KT)
        b0 = roomA.at
        DX = roomA.take(4096).rearrange("p (c t) -> p c t", c=KT)
        XI = [roomA.take(4096).rearrange("p (c t) -> p c t", c=KT) for _ in range(2)]
        b1 = roomA.at
        LOW = roomA.take(1024, 64).rearrange("p (s t) -> p s t", s=2)
        UPS = roomA.take(2048, 64).rearrange("p (s n) -> p s n", s=2)
        SIGW, CSUM, E2, KMOD = [roomA.take(512) for _ in range(4)]
        SQ2 = [roomA.take(512) for _ in range(2)]
        root_b = roomA.take(516)
        ROOT = [roomA.take(512), root_b[:, 0:512]]
        E1 = root_b.rearrange("p (j t) -> p j t", j=4)
        RKT = ROOT[0]

        roomB = Room(b0, b1)
        G = roomB.take(6144).rearrange("p (g u n) -> p g u n", g=3, u=4)
        XS = roomB.take(1024).rearrange("p (u s n) -> p u s n", u=4, s=2)
        XF = roomB.take(1024).rearrange("p (g u n) -> p g u n", g=2, u=4)
        YL = roomB.take(LEVELS * 512).rearrange("p (l u n) -> p l u n", l=LEVELS, u=4)
        roomB2 = Room(b1, 52900)
        YT = roomB2.take(4096).rearrange("p (t n) -> p t n", t=NT)
        BK = roomB2.take(1536).rearrange("p (g q n) -> p g q n", g=3, q=2)
        RH = roomB2.take(256).rearrange("p (q n) -> p q n", q=2)
        SA = roomB2.take(256).rearrange("p (q n) -> p q n", q=2)
        ST = roomB2.take(1024).rearrange("p (c n) -> p c n", c=PAIRS)
        STMP = roomB2.take(256).rearrange("p (q n) -> p q n", q=2)

        roomC = Room(base, base + 16384)
        SQ = roomC.take(4096).rearrange("p (t n) -> p t n", t=NT)
        BV = roomC.take(4096).rearrange("p (t n) -> p t n", t=NT)
        YG = roomC.take(4096).rearrange("p (c t) -> p c t", c=KT)
        GX = roomC.take(1024)
        SCB = roomC.take(1024).rearrange("p (c m) -> p c m", c=KT)
        BGX = roomC.take(1024)
        XR = arena[:, b0:b0 + 4096].rearrange("p (t n) -> p t n", t=NT)
        X1 = arena[:, b0 + 4096:b0 + 8192].rearrange("p (t n) -> p t n", t=NT)
        gx_at, x1_at = base + 12288, b0 + 4096

        dlo = Room(base, gx_at)
        XNP = dlo.take(KT * PADT).rearrange("p (c t) -> p c t", c=KT)
        MIX = XNP[:, :, 0:T]
        xn_flat = dlo.take(4096)
        XN = xn_flat.rearrange("p (t n) -> p t n", t=NT)
        UC = xn_flat.rearrange("p (t s n) -> p t s n", t=NT, s=2)
        OUTB = [xn_flat[:, 512 * i:512 * i + 512].rearrange("p (j n) -> p j n", j=2) for i in range(4)]
        QT_flat = dlo.take(2048)
        QT = QT_flat.rearrange("p (c t) -> p c t", c=4)
        CK = dlo.take(1024).rearrange("p (c t) -> p c t", c=4)
        dmid = Room(gx_at + 1024, x1_at)
        KTP = dmid.take(4 * PADT).rearrange("p (c t) -> p c t", c=4)
        VP = dmid.take(7 * 512).rearrange("p (t n) -> p t n", t=7)
        gate_flat = dmid.take(4096)
        GATE = gate_flat.rearrange("p (c t) -> p c t", c=8)
        CX = gate_flat[:, 0:2048].rearrange("p (t n) -> p t n", t=2)
        UT = dmid.take(2048).rearrange("p (c t) -> p c t", c=4)
        YF = UT
        CNT = dmid.take(2048).rearrange("p (c t) -> p c t", c=KT)
        CNJ = QT_flat[:, 0:D]
        DROOT = [dmid.take(512) for _ in range(2)]
        dhi = Room(x1_at + 4096, 52900)
        BM = dhi.take(3 * NAH * WIN).rearrange("p (v h n) -> p v h n", v=3, h=NAH)
        pr = dhi.at
        REL = dhi.take(NAH * RBW)
        DTMP = [dhi.take(512) for _ in range(2)]
        NEAR = dhi.take(3 * WIN)
        datt = Room(pr, 52900)
        PB = [datt.take(512) for _ in range(3)]
        PT = [datt.take(512) for _ in range(3)]
        ON = datt.take(512)

        bank_full = [sem(f"bank_full{b}") for b in range(8)]
        bank_free = [sem(f"bank_free{b}") for b in range(8)]
        weights_here = [sem(f"weights_here{s}") for s in range(3)]
        consts_here, x_here, ups_here, x_again, ctx_here, rel_here, bgate_here = [
            sem(n) for n in ("consts_here", "x_here", "ups_here", "x_again", "ctx_here", "rel_here", "bgate_here")]
        out_stored = [sem(f"out_stored{i}") for i in range(4)]
        act_steps, dve_steps, pool_steps = sem("act_steps"), sem("dve_steps"), sem("pool_steps")
        act_phase, dve_phase, pool_phase = sem("act_phase"), sem("dve_phase"), sem("pool_phase")
        x_squared, x_scaled, mixed = sem("x_squared"), sem("x_scaled"), sem("mixed")
        k_scaled, k_squared, k_root, kk_done = sem("k_scaled"), sem("k_squared"), sem("k_root"), sem("kk_done")
        csum_ready, decays_ready, a_ready, kmod_ready, rk_ready, kappa_ready, bonus_done = [
            sem(n) for n in ("csum_ready", "decays_ready", "a_ready", "kmod_ready", "rk_ready", "kappa_ready",
                             "bonus_done")]
        vectors_ready, gate_exp, c_exp, silu_c_ready = [
            sem(n) for n in ("vectors_ready", "gate_exp", "c_exp", "silu_c_ready")]
        y_zeroed = sem("y_zeroed")
        mods_block, pv_done = sem("mods_block"), sem("pv_done")
        z_ready, y_ready, x_grown, x_copied = [[sem(f"{n}{h}") for h in range(2)] for n in
                                               ("z_ready", "y_ready", "x_grown", "x_copied")]
        rhs_ready, rhs_copied, sa_ready, sa_copied, ys_ready, s_updated, y_copied = [
            [sem(f"{n}{h}") for h in range(2)] for n in
            ("rhs_ready", "rhs_copied", "sa_ready", "sa_copied", "ys_ready", "s_updated", "y_copied")]
        centred, gn_squared, gn_sums, gn_root, y_normed, bv_ready, y_gated = [
            sem(n) for n in ("centred", "gn_squared", "gn_sums", "gn_root", "y_normed", "bv_ready", "y_gated")]
        n2_root, cn_ready, xn_ready, mods_ready, pads_ready = [
            sem(n) for n in ("n2_root", "cn_ready", "xn_ready", "mods_ready", "pads_ready")]
        qk_squared, qk_root, qk_done = sem("qk_squared"), sem("qk_root"), sem("qk_done")
        gate2_exp, bm_ready, masked, out_ready = [sem(n) for n in ("gate2_exp", "bm_ready", "masked", "out_ready")]

        def cols(w, a, n):
            return w.rearrange("(k p) n -> p k n", p=P)[:, :, a:a + n], w.shape[0] // P, n

        stream = [cols(w_in, 4 * D, P)]
        for first in (D, 0, 2 * D, 3 * D):
            stream += [cols(w_in, first + 256 * b, 256) for b in range(4)]
        stream += [cols(w_ada, 256 * b, 256) for b in range(12)]
        stream += [cols(w_out, 256 * b, 256) for b in range(4)]
        stream += [cols(w_in2, a + 256 * b, 256) for a in (1024, 1536, 2048, 0, 512, 2560) for b in range(2)]
        stream += [cols(cos_t, 0, 512), cols(nsin_t, 0, 512), cols(w_four, 0, 512)]
        stream += [cols(w_out2, 256 * b, 256) for b in range(4)]

        def block_view(n):
            _, k, w = stream[n]
            return WR[n % 3][:, 0:k * w].rearrange("p (k n) -> p k n", k=k)

        class Steps:

            def __init__(self, eng, s):
                self.eng, self.s, self.n = eng, s, 0

            def did(self, ins):
                ins.then_inc(self.s, 1)
                self.n += 1

            def wait(self):
                self.eng.wait_ge(self.s, self.n)

            def own(self, ins):
                self.did(ins)
                self.wait()

        where, uses = {}, [0] * 8
        block_key = {}

        def arrived(eng, key):
            b, n = where[key]
            eng.wait_ge(bank_full[b], n)
            return banks[b]

        def free(ins, key):
            ins.then_inc(bank_free[where[key][0]], 1)

        def stored(eng, key):
            b, n = where[key]
            eng.wait_ge(bank_free[b], n)

        def others_done(eng, n, mine):
            for s in (act_phase, dve_phase, pool_phase):
                if s is not mine:
                    eng.wait_ge(s, n)

        def halves(ap, b, s):
            v = ap.rearrange("p (m s b) -> p m s b", s=2, b=b)
            return v[:, :, s, :]

        def halves2(ap, b, s):
            v = ap.rearrange("p u (m s b) -> p u m s b", s=2, b=b)
            return v[:, :, :, s, :]

        last_of_mix = [("low", 0), ("low", 1), ("k", 7), ("r", 7)]
        ITEMS = [("q", c) for c in range(4)] + [("kk", c) for c in range(4)] + [("ck", c) for c in range(4)]
        block = stack.enter_context(nc.Block())

        @block.tensor
        def _(pe):
            mm = nc.tensor.matmul
            taken = [0]

            def weights():
                n = taken[0]
                taken[0] += 1
                pe.wait_ge(weights_here[n % 3], 16 * (n // 3 + 1))
                return block_view(n)

            def out_bank(key, b):
                if uses[b]:
                    pe.wait_ge(bank_free[b], uses[b])
                uses[b] += 1
                where[key] = (b, uses[b])
                return banks[b]

            turn = [0]

            def next_bank(key, n=6):
                turn[0] = (turn[0] + 1) % n
                return out_bank(key, turn[0])

            def full(ins, key):
                ins.then_inc(bank_full[where[key][0]], 1)
                block_key[taken[0] - 1] = key

            def accumulate(o, lhs, rhs, n=KT):
                for k in range(n):
                    last = mm(o, lhs(k), rhs(k), start=(k == 0), stop=(k == n - 1))
                return last

            pe.wait_ge(consts_here, 64)
            pe.wait_ge(x_scaled, NT)
            for c in range(KT):
                o = next_bank(("hT", c))
                for t in range(NT):
                    last = nc.tensor.transpose(o[:, t * P:(t + 1) * P], V[:, t, c * P:(c + 1) * P], ident)
                full(last, ("hT", c))
            w = weights()
            for m in range(2):
                o = next_bank(("low", m))
                for k in range(KT):
                    pe.wait_ge(mixed, KT * m + k + 1)
                    last = mm(o[0:64, :], w[:, k, 64 * m:64 * m + 64], XI[m][:, k, :], start=(k == 0), stop=(k == KT - 1))
                full(last, ("low", m))
            for m, name in ((2, "k"), (3, "r")):
                pe.wait_ge(mixed, KT * (m + 1))
                for nb in range(4):
                    w = weights()
                    for h in range(2):
                        c = 2 * nb + h
                        o = next_bank((name, c))
                        full(accumulate(o[:, :], lambda k: w[:, k, h * P:(h + 1) * P], lambda k: XI[m % 2][:, k, :]),
                             (name, c))
                        if m == 3:
                            pe.wait_ge(k_squared, c + 1)
                            o = next_bank(("kss", c))
                            ins = mm(o[:, :], heads1, SQ2[c % 2], start=True, stop=True)
                            ins.then_inc(bank_full[where["kss", c][0]], 1)
            stored(pe, ("low", 0))
            stored(pe, ("low", 1))
            pe.wait_ge(ups_here, 32)
            pe.wait_ge(vectors_ready, 1)
            bonus_bank = out_bank("bonus", 7)

            def bonus(c):
                pe.wait_ge(rk_ready, c + 1)
                for t in range(NT):
                    last = mm(bonus_bank[:, t * 16 + 2 * c:t * 16 + 2 * c + 2], RKT[:, t * P:(t + 1) * P],
                              RKB[:, c, :], start=True, stop=True, skip_group_check=True)
                if c < KT - 1:
                    last.then_inc(bonus_done, 1)
                else:
                    full(last, "bonus")

            for c in range(KT):
                for s, name in ((0, "w"), (1, "a")):
                    o = next_bank((name, c))
                    mm(o[:, :], UPS[:, s, c * P:(c + 1) * P], LOW[:, s, :], start=True, stop=True)\
                        .then_inc(bank_full[where[name, c][0]], 1)
                w = weights()
                pe.wait_ge(mixed, KT * (5 if c < 4 else 6))
                for h in range(2):
                    if c < 4:
                        o = next_bank(("v", c, h))
                        for i in range(2):
                            t = 2 * h + i
                            last = accumulate(o[:, i * 256:(i + 1) * 256], lambda k: XI[0][:, k, t * P:(t + 1) * P],
                                              lambda k: w[:, k, :])
                        full(last, ("v", c, h))
                    else:
                        cc = 2 * (c - 4) + h
                        o = next_bank(("g", cc))
                        full(accumulate(o[:, :], lambda k: w[:, k, h * P:(h + 1) * P], lambda k: XI[1][:, k, :]),
                             ("g", cc))
                if c >= 1:
                    bonus(c - 1)
            bonus(KT - 1)
            for b in range(8):
                if uses[b]:
                    pe.wait_ge(bank_free[b], uses[b])
            others_done(pe, 1, None)

            gram_n = [0]

            def gram_bank(key):
                b = 4 + gram_n[0] % 2
                gram_n[0] += 1
                return out_bank(key, b)

            def gram(g, u):
                j, cc = divmod(g, 4)
                c, lo = 2 * cc + u // 2, HD * (u % 2)
                o = gram_bank(("gram", g, u))
                at = slice(j * P, (j + 1) * P)
                mm(o[:, 0:256], AB[lo:lo + HD, c, at], AR[lo:lo + HD, :, c, at], start=True, stop=True,
                   skip_group_check=True)
                mm(o[:, 256:512], KB[lo:lo + HD, c, at], AR[lo:lo + HD, :, c, at], start=True, stop=True,
                   skip_group_check=True).then_inc(bank_full[where["gram", g, u][0]], 1)

            def turned(g):
                j, cc = divmod(g, 4)
                o = gram_bank(("turn", g))
                for q in range(2):
                    for s, src in enumerate((AB, KB)):
                        last = nc.tensor.transpose(o[:, (2 * q + s) * P:(2 * q + s + 1) * P],
                                                   src[:, 2 * cc + q, j * P:(j + 1) * P], ident)
                last.then_inc(bank_full[where["turn", g][0]], 1)

            def seed(g, hf):
                if g:
                    pe.wait_ge(x_copied[hf], LEVELS * g)
                mm(banks[hf][:, :], idb[:, 0:P], idb[:, :], start=True, stop=False, skip_group_check=True)

            def off_product(g, l, hf):
                n = LEVELS * g + l
                if l:
                    pe.wait_ge(x_copied[hf], n)
                if n:
                    pe.wait_ge(y_ready[hf], n)
                for i in range(2):
                    u = 2 * hf + i
                    if l == 0:
                        stored(pe, ("gram", g, u))
                    rhs = ident if l == 0 else XS[:, u, 0, :]
                    last = mm(banks[2 + hf][:, i * HD:(i + 1) * HD], G[:, g % 3, u, 0:P], halves(rhs, 1 << l, 0),
                              start=True, stop=True, skip_group_check=True)
                last.then_inc(z_ready[hf], 1)

            def grow(g, l, hf):
                pe.wait_ge(y_ready[hf], LEVELS * g + l + 1)
                for i in range(2):
                    u = 2 * hf + i
                    xt = ident if l == 0 else XS[:, u, 1, :]
                    o = banks[hf][:, i * 256:(i + 1) * 256]
                    y = YL[:, l, u, :]
                    if l < LEVELS - 1:
                        mm(halves(o[:, 0:P], 1 << l, 0), xt, halves(y, 1 << l, 0), start=False, stop=False,
                           skip_group_check=True)
                    last = mm(halves(o[:, P:256], 1 << l, 1), y, halves(xt, 1 << l, 1), start=False,
                              stop=(l == LEVELS - 1), skip_group_check=True)
                last.then_inc(x_grown[hf], 1)

            def scan_rhs(g, q):
                j, cc = divmod(g, 4)
                c = 2 * cc + q
                o = banks[6 + q][:, 0:P]
                if g:
                    pe.wait_ge(y_copied[q], g)
                    pe.wait_ge(s_updated[q], min(g, GROUPS - 4))
                for i in range(2):
                    stored(pe, ("gram", g, 2 * q + i))
                if j:
                    mm(o, AR[:, 0, c, j * P:(j + 1) * P], ST[:, c, :], start=True, stop=False, skip_group_check=True)
                for i in range(2):
                    last = mm(o[:, i * HD:(i + 1) * HD], G[:, g % 3, 2 * q + i, 2 * P:3 * P],
                              V[:, j, c * P + i * HD:c * P + (i + 1) * HD], start=(j == 0 and i == 0), stop=(i == 1),
                              skip_group_check=True)
                last.then_inc(rhs_ready[q], 1)

            def scan_sa(g, q):
                pe.wait_ge(rhs_copied[q], g + 1)
                pe.wait_ge(x_copied[q], LEVELS * (g + 1))
                for i in range(2):
                    last = mm(banks[6 + q][:, P + i * HD:P + (i + 1) * HD], XF[:, g % 2, 2 * q + i, :],
                              RH[:, q, i * HD:(i + 1) * HD], start=True, stop=True, skip_group_check=True)
                last.then_inc(sa_ready[q], 1)

            def scan_out(g, q):
                j, cc = divmod(g, 4)
                c = 2 * cc + q
                pe.wait_ge(sa_copied[q], g + 1)
                o = banks[6 + q][:, 2 * P:3 * P]
                if j:
                    mm(o, AR[:, 1, c, j * P:(j + 1) * P], ST[:, c, :], start=True, stop=False, skip_group_check=True)
                for i in range(2):
                    gm = G[:, g % 3, 2 * q + i, :]
                    mm(o[:, i * HD:(i + 1) * HD], gm[:, P:2 * P], SA[:, q, i * HD:(i + 1) * HD],
                       start=(j == 0 and i == 0), stop=False, skip_group_check=True)
                    last = mm(o[:, i * HD:(i + 1) * HD], gm[:, 3 * P:4 * P],
                              V[:, j, c * P + i * HD:c * P + (i + 1) * HD], start=False, stop=(i == 1),
                              skip_group_check=True)
                if j < NT - 1:
                    stored(pe, ("turn", g))
                    s = banks[6 + q][:, 3 * P:4 * P]
                    mm(s, BK[:, g % 3, q, 0:P], SA[:, q, :], start=True, stop=False, skip_group_check=True)
                    last = mm(s, BK[:, g % 3, q, P:2 * P], V[:, j, c * P:(c + 1) * P], start=False, stop=True,
                              skip_group_check=True)
                last.then_inc(ys_ready[q], 1)

            for u in range(4):
                gram(0, u)
            turned(0)
            pe.wait_ge(y_zeroed, 1)
            for g in range(GROUPS + 1):
                now, nxt, old = g < GROUPS, g + 1 < GROUPS, g > 0
                if now:
                    seed(g, 0)
                    seed(g, 1)
                for l in range(LEVELS):
                    if now:
                        off_product(g, l, 0)
                        off_product(g, l, 1)
                    if nxt and l < 3:
                        gram(g + 1, l)
                    if old and l == 3:
                        scan_out(g - 1, 1)
                    if nxt and l == 4:
                        turned(g + 1)
                    if now:
                        grow(g, l, 0)
                        grow(g, l, 1)
                    if old and l == 0:
                        scan_rhs(g - 1, 0)
                        scan_rhs(g - 1, 1)
                    if old and l == 1:
                        scan_sa(g - 1, 0)
                        scan_sa(g - 1, 1)
                    if old and l == 2:
                        scan_out(g - 1, 0)
                    if nxt and l == 3:
                        gram(g + 1, 3)

            others_done(pe, 2, None)
            pe.wait_ge(silu_c_ready, 1)
            o = out_bank("mods", 7)
            for nb in range(8):
                w = weights()
                for h in range(2):
                    col = 4 * nb + 2 * h
                    for k in range(KT):
                        last = mm(o[:, col:col + 2], w[:, k, h * P:(h + 1) * P], SILC[:, k, :],
                                  start=(k == 0), stop=(k == KT - 1), skip_group_check=True)
                if nb < 7:
                    last.then_inc(mods_block, 1)
                    block_key[taken[0] - 1] = nb + 1
                else:
                    full(last, "mods")
            for gb in range(2):
                o = next_bank(("gx", gb))
                for h in range(2):
                    w = weights()
                    last = accumulate(o[:, h * 256:(h + 1) * 256], lambda k: SCB[:, k, :], lambda k: w[:, k, :])
                    if h == 0:
                        last.then_inc(mods_block, 1)
                        block_key[taken[0] - 1] = 8 + gb
                full(last, ("gx", gb))
            for t in range(NT):
                pe.wait_ge(y_normed, t + 1)
                pe.wait_ge(bv_ready, t + 1)
                for h in range(2):
                    for name, src in (("yT", YT), ("bT", BV)):
                        o = next_bank((name, t, h))
                        for i in range(4):
                            last = nc.tensor.transpose(o[:, i * P:(i + 1) * P],
                                                       src[:, t, (4 * h + i) * P:(4 * h + i + 1) * P], ident)
                        last.then_inc(bank_full[where[name, t, h][0]], 1)
            for nb in range(4):
                w = weights()
                for th in range(2):
                    o = next_bank(("o", nb, th))
                    for i in range(2):
                        t = 2 * th + i
                        if nb == 0:
                            pe.wait_ge(y_gated, 2 * (t + 1))
                        last = accumulate(o[:, i * 256:(i + 1) * 256], lambda k: YG[:, k, t * P:(t + 1) * P],
                                          lambda k: w[:, k, :])
                    full(last, ("o", nb, th))
            pe.wait_ge(cn_ready, 2)
            for h in range(4):
                o = next_bank(("cT", h))
                for i in range(2):
                    for t in range(2):
                        c = 2 * h + i
                        last = nc.tensor.transpose(o[:, i * 256 + t * P:i * 256 + (t + 1) * P],
                                                   CX[:, t, c * P:(c + 1) * P], ident)
                last.then_inc(bank_full[where["cT", h][0]], 1)
            pe.wait_ge(xn_ready, NT)
            for c in range(KT):
                o = next_bank(("xT", c))
                for t in range(NT):
                    last = nc.tensor.transpose(o[:, t * P:(t + 1) * P], XN[:, t, c * P:(c + 1) * P], ident)
                last.then_inc(bank_full[where["xT", c][0]], 1)
            for h in range(4):
                stored(pe, ("cT", h))
            for c in range(KT):
                stored(pe, ("xT", c))
            pe.wait_ge(pads_ready, 1)
            tok = slice(HD, HD + T)

            def head_norm(i):
                n = CTX if ITEMS[i][0] == "ck" else T
                pe.wait_ge(qk_squared, i + 1)
                o = next_bank(("ss", i))
                mm(o[:, 0:n], heads1, DTMP[i % 2][:, 0:n], start=True, stop=True)\
                    .then_inc(bank_full[where["ss", i][0]], 1)

            items = []

            def qk_output(name, c, w, h, rhs, n):
                o = next_bank((name, c))
                full(accumulate(o[:, 0:n], lambda k: w[:, k, h * P:(h + 1) * P], rhs), (name, c))
                items.append((name, c))
                if len(items) > 1:
                    head_norm(len(items) - 2)

            for nb in range(2):
                w = weights()
                for h in range(2):
                    qk_output("q", 2 * nb + h, w, h, lambda k: XNP[:, k, tok], T)
            kw = []
            for nb in range(2):
                w = weights()
                kw.append(w)
                for h in range(2):
                    qk_output("kk", 2 * nb + h, w, h, lambda k: XNP[:, k, tok], T)
            for nb in range(2):
                for h in range(2):
                    qk_output("ck", 2 * nb + h, kw[nb], h, lambda k: CNT[:, k, :], CTX)
                    block_key[taken[0] - 2 + nb] = ("ck", 2 * nb + h)
            block_key[taken[0] - 1] = ("ck", 3)
            head_norm(len(items) - 1)
            for nb in range(2):
                w = weights()
                for b4 in range(4):
                    o = next_bank(("vv", nb, b4))
                    for i in range(2):
                        t = 2 * b4 + i
                        if t < 7:
                            last = accumulate(o[:, i * 256:(i + 1) * 256],
                                              (lambda k: XNP[:, k, t * P:(t + 1) * P]) if t < 5 else
                                              (lambda k: CNT[:, k, (t - 5) * P:(t - 4) * P]), lambda k: w[:, k, :])
                    full(last, ("vv", nb, b4))
            for name, n0 in (("f", 0), ("g2", 0), ("g2", 4)):
                for nb in range(2):
                    w = weights()
                    for h in range(2):
                        key = (name, n0 + 2 * nb + h)
                        o = next_bank(key)
                        full(accumulate(o[:, :], lambda k: w[:, k, h * P:(h + 1) * P], lambda k: XNP[:, k, tok]), key)
            for t in range(NT):
                for gp in range(2):
                    stored(pe, ("f", 2 * gp))
                    stored(pe, ("f", 2 * gp + 1))
                    o = next_bank(("uc", t, gp))
                    for i in range(2):
                        last = mm(o[:, i * 256:(i + 1) * 256], UT[:, 2 * gp + i, t * P:(t + 1) * P], con("dft128"),
                                  start=True, stop=True)
                    last.then_inc(bank_full[where["uc", t, gp][0]], 1)
            dft = [weights(), weights()]
            for g in range(4):
                o = next_bank(("yf", g))
                for s in range(2):
                    for t in range(NT):
                        stored(pe, ("uc", t, g // 2))
                        last = mm(o[:, :], UC[:, t, s, g * P:(g + 1) * P], dft[s][:, t, :], start=(s == 0 and t == 0),
                                  stop=(s == 1 and t == NT - 1))
                full(last, ("yf", g))
            block_key[taken[0] - 2] = ("yf", 3)
            w = weights()
            for n in range(4):
                o = next_bank(("fo", n))
                for k in range(4):
                    stored(pe, ("yf", k))
                full(accumulate(o[:, :], lambda k: w[:, k, n * P:(n + 1) * P], lambda k: YF[:, k, :], 4), ("fo", n))

            def scores(n):
                qt, h = divmod(n, NAH)
                lo = HD * (h % 2)
                o = out_bank(("s", n), n % 2)
                q = QT[lo:lo + HD, h // 2, qt * P:(qt + 1) * P]
                mm(o[:, 0:WIN], q, KTP[lo:lo + HD, h // 2, qt * P:qt * P + WIN], start=True, stop=True,
                   skip_group_check=True)
                mm(o[:, WIN:WIN + CTX], q, CK[lo:lo + HD, h // 2, :], start=True, stop=True, skip_group_check=True)\
                    .then_inc(bank_full[n % 2], 1)

            def turn_probs(n):
                stored(pe, ("s", n))
                o = out_bank(("pt", n), 2 + n % 2)
                for i in range(4):
                    last = nc.tensor.transpose(o[:, i * P:(i + 1) * P], PB[n % 3][:, i * P:(i + 1) * P], ident)
                last.then_inc(bank_full[2 + n % 2], 1)

            def take_values(n):
                qt, h = divmod(n, NAH)
                stored(pe, ("pt", n))
                o = out_bank(("at", qt), 4) if h == 0 else banks[4]
                for i in range(4):
                    v = VP[:, qt + i if i < 2 else 3 + i, h * HD:(h + 1) * HD]
                    last = mm(o[:, h * HD:(h + 1) * HD], PT[n % 3][:, i * P:(i + 1) * P], v, start=(i == 0),
                              stop=(i == 3), skip_group_check=True)
                last.then_inc(bank_full[4], 1) if h == NAH - 1 else last.then_inc(pv_done, 1)

            def turn_out(qt):
                stored(pe, ("at", qt))
                o = out_bank(("oT", qt), 5)
                for i in range(4):
                    last = nc.tensor.transpose(o[:, i * P:(i + 1) * P], ON[:, i * P:(i + 1) * P], ident)
                last.then_inc(bank_full[5], 1)

            pe.wait_ge(qk_done, len(ITEMS))
            for nb in range(2):
                for b4 in range(4):
                    stored(pe, ("vv", nb, b4))
            NU = NT * NAH
            for n in range(NU + 5):
                if n < NU:
                    scores(n)
                if 1 <= n < NU + 1:
                    turn_probs(n - 1)
                if 2 <= n < NU + 2:
                    take_values(n - 2)
                if n >= NAH + 4 and (n - NAH - 4) % NAH == 0:
                    turn_out((n - NAH - 4) // NAH)
            for nb in range(4):
                w = weights()
                for th in range(2):
                    o = next_bank(("z", nb, th))
                    if nb == 0 and th == 0:
                        for n in range(4):
                            stored(pe, ("fo", n))
                            stored(pe, ("oT", n))
                    for i in range(2):
                        t = 2 * th + i
                        last = accumulate(o[:, i * 256:(i + 1) * 256], lambda k: MIX[:, k, t * P:(t + 1) * P],
                                          lambda k: w[:, k, :])
                    full(last, ("z", nb, th))

        @block.sync
        def _(sp):
            x_t = x.rearrange("(t p) n -> p t n", p=P)
            sp.dma_start(V, x_t).then_inc(x_here, 16)
            sp.dma_start(CON, consts).then_inc(consts_here, 16)
            sp.dma_start(VECS, vecs).then_inc(consts_here, 16)
            for i in range(4):
                if i < 2:
                    sp.dma_start(idb[:, 2 * i * P:(2 * i + 2) * P], ident_b).then_inc(consts_here, 16)
            sp.dma_start(UPS[:, 0, :], w_up).then_inc(ups_here, 16)
            sp.dma_start(UPS[:, 1, :], a_up).then_inc(ups_here, 16)
            for n, (src, k, w) in enumerate(stream):
                if n >= 3:
                    key = block_key[n - 3]
                    if isinstance(key, int):
                        sp.wait_ge(mods_block, key)
                    else:
                        arrived(sp, key)
                sp.dma_start(block_view(n), src).then_inc(weights_here[n % 3], 16)
                if n == 19:
                    others_done(sp, 2, None)
                    sp.dma_start(XR, x_t).then_inc(x_again, 16)
                    sp.dma_start(BGX, b_gate.partition_broadcast(P)).then_inc(bgate_here, 16)
                if n == 32:
                    others_done(sp, 3, None)
                    sp.dma_start(CX, ctx_x.rearrange("(t p) n -> p t n", p=P)).then_inc(ctx_here, 16)
                    sp.dma_start(NEAR, near).then_inc(rel_here, 16)
                    for cl in range(16):
                        sp.dma_start(REL[cl * GH:(cl + 1) * GH, :],
                                     bass.AP(rel_bias.tensor, RBPAD + 7 - cl, [[31, GH], [RB + 2 * RBPAD, NAH], [1, RBW]])).then_inc(rel_here, 16)
            for i in range(8):
                nb, th = divmod(i, 2)
                sp.wait_ge(out_ready, i + 1)
                sp.dma_start(out.rearrange("(t p) n -> p t n", p=P)[:, 2 * th:2 * th + 2, 256 * nb:256 * nb + 256],
                             OUTB[i % 4]).then_inc(out_stored[i % 4], 16)
            for s in out_stored:
                sp.wait_ge(s, 32)

        @block.scalar
        def _(act):
            A = nc.scalar.activation
            own = Steps(act, act_steps)
            eps, gn_eps, eps64 = [con("eps")[:, i:i + 1] for i in range(3)]
            act.wait_ge(consts_here, 64)
            act.wait_ge(x_here, 16)
            for t in range(NT):
                own.did(A(XI[0][:, 2 * t:2 * t + 2, :], V[:, t, :].rearrange("p (a b) -> p a b", a=2), ACT.Square,
                          accum_out=ssq[:, t:t + 1]))
            own.wait()
            A(rstd, ssq, ACT.Sqrt, bias=eps, scale=1.0 / D).then_inc(x_squared, 1)
            act.wait_ge(vectors_ready, 1)
            A(SILT[:, 0:16], VECS[:, VEC["c"]:VEC["c"] + 16], ACT.Exp, scale=-1.0).then_inc(c_exp, 1)
            for c in range(KT):
                o = arrived(act, ("hT", c))
                free(A(HT[:, c, 1:T + 1], o[:, :], ACT.Copy, scale=vec("norm", c)), ("hT", c))
            free(A(LOW[:, 0, :], arrived(act, ("low", 0))[0:64, :], ACT.Tanh), ("low", 0))
            free(A(LOW[:, 1, :], arrived(act, ("low", 1))[0:64, :], ACT.Copy), ("low", 1))
            for c in range(KT):
                free(A(KB[:, c, :], arrived(act, ("k", c))[:, :], ACT.Copy), ("k", c))

            def square_k(c):
                act.wait_ge(k_scaled, c + 1)
                if c >= 2:
                    arrived(act, ("kss", c - 2))
                A(SQ2[c % 2], AR[:, 0, c, :], ACT.Square).then_inc(k_squared, 1)

            square_k(0)
            for c in range(KT):
                if c + 1 < KT:
                    square_k(c + 1)
                free(A(AR[:, 1, c, :], arrived(act, ("r", c))[:, :], ACT.Copy), ("r", c))
                o = arrived(act, ("kss", c))
                if c >= 2:
                    act.wait_ge(kk_done, c - 1)
                free(A(ROOT[c % 2], o[:, :], ACT.Sqrt), ("kss", c))
            for c in range(KT):
                o = arrived(act, ("w", c))
                if c:
                    act.wait_ge(csum_ready, c)
                free(A(SIGW, o[:, :], ACT.Exp, scale=-1.0, bias=nvec("w0", c)), ("w", c))
                free(A(AB[:, c, :], arrived(act, ("a", c))[:, :], ACT.Exp, scale=-1.0, bias=nvec("a0", c)), ("a", c))
                act.wait_ge(csum_ready, c + 1)
                if c:
                    act.wait_ge(kappa_ready, c)
                csum = CSUM.rearrange("p (j t) -> p j t", j=4)
                A(E1[:, :, 1:P + 1], csum, ACT.Exp, scale=-KAPPA)
                A(E2, CSUM, ACT.Exp, scale=KAPPA)
                A(E1[:, :, 0], MID[:, 0:4], ACT.Exp, scale=KAPPA)
                A(MID[:, 4:8], MID[:, 0:4], ACT.Exp, scale=-KAPPA).then_inc(decays_ready, 1)
                for h in range(2):
                    if c < 4:
                        o = arrived(act, ("v", c, h))
                        free(A(V[:, 2 * h:2 * h + 2, c * 256:(c + 1) * 256], o.rearrange("p (i n) -> p i n", i=2),
                               ACT.Copy), ("v", c, h))
                    else:
                        cc = 2 * (c - 4) + h
                        o = arrived(act, ("g", cc))
                        if cc >= 2:
                            stored(act, ("g", cc - 2))
                        A(SQ2[cc % 2], o[:, :], ACT.Exp, scale=-1.0).then_inc(gate_exp, 1)
            A(CST[:, 0:1], CST[:, 4:5], ACT.Copy).then_inc(act_phase, 1)
            others_done(act, 1, act_phase)
            arrived(act, "bonus")

            def copy_turned(g):
                free(A(BK[:, g % 3, :, :], arrived(act, ("turn", g)).rearrange("p (q n) -> p q n", q=2), ACT.Copy),
                     ("turn", g))

            def copy_x(g, l, hf):
                act.wait_ge(x_grown[hf], LEVELS * g + l + 1)
                o = banks[hf].rearrange("p (u s n) -> p u s n", u=2, s=2)
                u = slice(2 * hf, 2 * hf + 2)
                if l == LEVELS - 1:
                    ins = A(XF[:, g % 2, u, :], o[:, :, 1, :], ACT.Copy)
                elif l == 0:
                    ins = A(XS[:, u, :, :], o, ACT.Copy)
                else:
                    A(halves2(XS[:, u, 0, :], 1 << l, 0), halves2(o[:, :, 0, :], 1 << l, 0), ACT.Copy)
                    ins = A(halves2(XS[:, u, 1, :], 1 << l, 1), halves2(o[:, :, 1, :], 1 << l, 1), ACT.Copy)
                ins.then_inc(x_copied[hf], 1)

            def copy_y(g, q):
                j, cc = divmod(g, 4)
                c = 2 * cc + q
                act.wait_ge(ys_ready[q], g + 1)
                if j < NT - 1:
                    act.wait_ge(s_updated[q], g + 1)
                A(YT[:, j, c * P:(c + 1) * P], banks[6 + q][:, 2 * P:3 * P], ACT.Copy).then_inc(y_copied[q], 1)

            copy_turned(0)
            for g in range(GROUPS + 1):
                now, nxt, old = g < GROUPS, g + 1 < GROUPS, g > 0
                for l in range(LEVELS):
                    if nxt and l == 4:
                        copy_turned(g + 1)
                    if now:
                        copy_x(g, l, 0)
                        copy_x(g, l, 1)
                    if old and l == 3:
                        copy_y(g - 1, 0)
                        copy_y(g - 1, 1)
            A(CST[:, 0:1], CST[:, 4:5], ACT.Copy).then_inc(act_phase, 1)
            others_done(act, 2, act_phase)
            for t in range(NT):
                act.wait_ge(centred, t + 1)
                A(SQ[:, t, :], YT[:, t, :], ACT.Square).then_inc(gn_squared, 1)
            act.wait_ge(gn_sums, 1)
            A(GST[:, 128:192], GST[:, 64:128], ACT.Sqrt, bias=gn_eps, scale=1.0 / HD).then_inc(gn_root, 1)
            for t in range(NT):
                for h in range(2):
                    o = arrived(act, ("yT", t, h))
                    for i in range(4):
                        c = 4 * h + i
                        ins = A(YG[:, c, t * P:(t + 1) * P], o[:, i * P:(i + 1) * P], ACT.Identity,
                                bias=vec("gn_b", c), scale=vec("gn_w", c))
                    free(ins, ("yT", t, h))
            A(CST[:, 0:1], CST[:, 4:5], ACT.Copy).then_inc(act_phase, 1)
            others_done(act, 3, act_phase)
            for t in range(NT):
                own.did(A(XN[:, t, :], X1[:, t, :], ACT.Square, accum_out=ssq[:, t:t + 1]))
            act.wait_ge(ctx_here, 16)
            for t in range(2):
                own.own(A(CNJ, CX[:, t, :], ACT.Square, accum_out=SUMS[:, t:t + 1]))
            own.wait()
            A(rstd, ssq, ACT.Sqrt, bias=eps, scale=1.0 / D).then_inc(n2_root, 1)
            A(SUMS[:, 2:4], SUMS[:, 0:2], ACT.Sqrt, bias=eps, scale=1.0 / D).then_inc(n2_root, 1)
            act.wait_ge(mods_ready, 1)
            for h in range(4):
                o = arrived(act, ("cT", h))
                for i in range(2):
                    c = 2 * h + i
                    ins = A(CNT[:, c, :], o[:, i * 256:(i + 1) * 256], ACT.Identity, bias=MODS[:, c, 1:2],
                            scale=GSC[:, c, 1:2])
                free(ins, ("cT", h))
            for c in range(KT):
                o = arrived(act, ("xT", c))
                dst = XNP[:, c, HD:HD + T].rearrange("p (col r) -> p r col", r=GH)
                free(A(dst, o.rearrange("p (r col) -> p r col", r=GH), ACT.Identity, bias=MODS[:, c, 0:1],
                       scale=GSC[:, c, 0:1]), ("xT", c))

            def root(i):
                n = CTX if ITEMS[i][0] == "ck" else T
                o = arrived(act, ("ss", i))
                if i >= 2:
                    act.wait_ge(qk_done, i - 1)
                q = ITEMS[i][0] == "q"
                free(A(DROOT[i % 2][:, 0:n], o[:, 0:n], ACT.Sqrt, bias=eps64 if q else eps,
                       scale=1.0 if q else 1.0 / HD), ("ss", i))

            for i, key in enumerate(ITEMS):
                n = CTX if key[0] == "ck" else T
                o = arrived(act, key)
                if i >= 2:
                    arrived(act, ("ss", i - 2))
                A(DTMP[i % 2][:, 0:n], o[:, 0:n], ACT.Square).then_inc(qk_squared, 1)
                if i:
                    root(i - 1)
            root(len(ITEMS) - 1)
            for nb in range(2):
                for b4 in range(4):
                    o = arrived(act, ("vv", nb, b4)).rearrange("p (i n) -> p i n", i=2)
                    w = 2 if b4 < 3 else 1
                    free(A(VP[:, 2 * b4:2 * b4 + w, nb * 256:(nb + 1) * 256], o[:, 0:w, :], ACT.Copy), ("vv", nb, b4))
            for c in range(4):
                free(A(UT[:, c, :], arrived(act, ("f", c))[:, :], ACT.Copy), ("f", c))
            for c in range(8):
                A(GATE[:, c, :], arrived(act, ("g2", c))[:, :], ACT.Exp, scale=-1.0).then_inc(gate2_exp, 1)
            for t in range(NT):
                for gp in range(2):
                    o = arrived(act, ("uc", t, gp)).rearrange("p (g s n) -> p g s n", g=2, s=2)
                    dst = UC[:, t, :, gp * 256:(gp + 1) * 256].rearrange("p s (g n) -> p g s n", g=2)
                    free(A(dst, o, ACT.Copy), ("uc", t, gp))
            for g in range(4):
                free(A(YF[:, g, :], arrived(act, ("yf", g))[:, :], ACT.Copy), ("yf", g))
            for n in range(NT * NAH):
                act.wait_ge(masked, n + 1)
                nm = MXN2[:, n % 4:n % 4 + 1]
                A(PB[n % 3][:, 0:WIN], PB[n % 3][:, 0:WIN], ACT.Exp, bias=nm, accum_out=SUMS[:, 8 + n:9 + n])
                free(A(PB[n % 3][:, WIN:512], banks[n % 2][:, WIN:512], ACT.Exp, bias=nm,
                       accum_out=SUMS[:, 40 + n:41 + n]), ("s", n))

        @block.vector
        def _(dve):
            TT, TS, STT = nc.vector.tensor_tensor, nc.vector.tensor_scalar, nc.vector.scalar_tensor_tensor
            own = Steps(dve, dve_steps)
            own.did(nc.vector.memset(CST, 0.0))
            own.did(nc.vector.memset(HT[:, :, 0:1], 0.0))
            dve.wait_ge(consts_here, 64)
            own.did(TS(NVEC, VECS, -1.0, None, MUL))
            own.did(TS(NKA, VECS[:, VEC["k_a"]:VEC["k_a"] + KT], -1.0, 1.0, MUL, ADD))
            TT(RKB, VECS[:, VEC["r_k"]:VEC["r_k"] + KT].unsqueeze(2).broadcast_to([P, KT, 2]),
               heads1[:, 0:P:HD].unsqueeze(1).broadcast_to([P, KT, 2]), MUL).then_inc(vectors_ready, 1)
            dve.wait_ge(x_squared, 1)
            own.own(nc.vector.reciprocal(rstd, rstd))
            dve.wait_ge(x_here, 16)
            for t in range(NT):
                TS(V[:, t, :], V[:, t, :], rstd[:, t:t + 1], None, MUL).then_inc(x_scaled, 1)
            dve.wait_ge(c_exp, 1)
            own.own(TS(SILT[:, 0:16], SILT[:, 0:16], 1.0, None, ADD))
            own.own(nc.vector.reciprocal(SILT[:, 16:32], SILT[:, 0:16]))
            own.did(TT(SILC.rearrange("p c k -> p k c"), SILT[:, 16:32].rearrange("p (k c) -> p k c", k=2),
                       VECS[:, VEC["c"]:VEC["c"] + 16].rearrange("p (k c) -> p k c", k=2), MUL))
            for c in range(KT):
                stored(dve, ("hT", c))
                own.did(TT(DX[:, c, :], HT[:, c, 0:T], HT[:, c, 1:T + 1], SUB))
            own.wait()

            def mix(m):
                if m >= 2:
                    arrived(dve, last_of_mix[m - 2])
                for c in range(KT):
                    STT(XI[m % 2][:, c, :], DX[:, c, :], vec("mu_" + "wakrvg"[m], c), HT[:, c, 1:T + 1], MUL, ADD)\
                        .then_inc(mixed, 1)

            for m in range(4):
                mix(m)
            for c in range(KT):
                stored(dve, ("k", c))
                TS(AR[:, 0, c, :], KB[:, c, :], vec("k_k", c), None, MUL).then_inc(k_scaled, 1)
            mix(4)
            for c in range(KT):
                stored(dve, ("kss", c))
                own.own(TS(ROOT[c % 2], ROOT[c % 2], 1e-12, None, MAX))
                own.own(nc.vector.reciprocal(ROOT[c % 2], ROOT[c % 2]))
                TT(AR[:, 0, c, :], AR[:, 0, c, :], ROOT[c % 2], MUL).then_inc(kk_done, 1)
            mix(5)

            def gate(cc):
                dve.wait_ge(gate_exp, cc + 1)
                e = SQ2[cc % 2]
                own.own(TS(e, e, 1.0, None, ADD))
                own.own(nc.vector.reciprocal(e, e))
                free(TT(GT[:, cc, :], arrived(dve, ("g", cc))[:, :], e, MUL), ("g", cc))

            dve.wait_ge(mixed, KT * 6)
            dve.wait_ge(kk_done, KT)
            for c in range(KT):
                stored(dve, ("w", c))
                own.own(TS(SIGW, SIGW, 1.0, None, ADD))
                own.own(nc.vector.reciprocal(SIGW, SIGW))
                for j in range(4):
                    at = slice(j * P, (j + 1) * P)
                    own.did(nc.vector.tensor_tensor_scan(CSUM[:, at], con("ones"), SIGW[:, at], 0.0, MUL, ADD))
                own.wait()
                csum = CSUM.rearrange("p (j t) -> p j t", j=4)
                if c:
                    dve.wait_ge(decays_ready, c)
                own.own(nc.vector.tensor_copy(MID[:, 0:4], csum[:, :, HD - 1]))
                TT(csum, csum, MID[:, 0:4].unsqueeze(2).broadcast_to([P, 4, P]), SUB).then_inc(csum_ready, 1)
                stored(dve, ("a", c))
                own.own(TS(AB[:, c, :], AB[:, c, :], 1.0, None, ADD))
                nc.vector.reciprocal(AB[:, c, :], AB[:, c, :]).then_inc(a_ready, 1)
                dve.wait_ge(a_ready, c + 1)
                dve.wait_ge(kmod_ready, c + 1)
                own.own(TT(AB[:, c, :], AB[:, c, :], AR[:, 0, c, :], MUL))
                dve.wait_ge(decays_ready, c + 1)
                own.did(TT(AB[:, c, :], AB[:, c, :], E2, MUL))
                a4 = AR[:, 0, c, :].rearrange("p (j t) -> p j t", j=4)
                own.did(STT(a4, a4, -1.0, E1[:, :, 0:P], MUL, MUL))
                own.did(TT(F[:, c, 0:3], E1[:, 0:3, P], MID[:, 5:8], MUL))
                dve.wait_ge(rk_ready, c + 1)
                r4 = AR[:, 1, c, :].rearrange("p (j t) -> p j t", j=4)
                own.own(TT(r4, r4, E1[:, :, 1:P + 1], MUL))
                if c >= 4:
                    gate(2 * (c - 4))
                    gate(2 * (c - 4) + 1)
            free(nc.vector.tensor_copy(BON, arrived(dve, "bonus")[:, 0:64]), "bonus")
            nc.vector.tensor_copy(CST[:, 1:2], CST[:, 5:6]).then_inc(dve_phase, 1)
            others_done(dve, 1, dve_phase)

            def mask_gram(g, u):
                o = arrived(dve, ("gram", g, u)).rearrange("p (s n) -> p s n", s=2)
                free(TT(G[:, g % 3, u, :].rearrange("p (s n) -> p s n", s=2), o,
                        gram_mask.unsqueeze(1).broadcast_to([P, 2, 2 * P]), MUL), ("gram", g, u))

            def mask_z(g, l, hf):
                dve.wait_ge(z_ready[hf], LEVELS * g + l + 1)
                b = 1 << l
                m = con("level")[:, l * HD:(l + 1) * HD].rearrange("p (m b) -> p m b", b=b)
                z = banks[2 + hf][:, 0:P].rearrange("p (u m b) -> p u m b", u=2, b=b)
                TT(halves2(YL[:, l, 2 * hf:2 * hf + 2, :], b, 0), z, m.unsqueeze(1).broadcast_to([P, 2, HD // b, b]),
                   MUL).then_inc(y_ready[hf], 1)

            def copy_rhs(g, q):
                dve.wait_ge(rhs_ready[q], g + 1)
                nc.vector.tensor_copy(RH[:, q, :], banks[6 + q][:, 0:P]).then_inc(rhs_copied[q], 1)

            def copy_sa(g, q):
                dve.wait_ge(sa_ready[q], g + 1)
                nc.vector.tensor_copy(SA[:, q, :], banks[6 + q][:, P:2 * P]).then_inc(sa_copied[q], 1)

            def update(g, q):
                j, cc = divmod(g, 4)
                c = 2 * cc + q
                if j == NT - 1:
                    return
                dve.wait_ge(ys_ready[q], g + 1)
                s = banks[6 + q][:, 3 * P:4 * P]
                if j == 0:
                    STT(ST[:, c, :], s, F[:, c, j:j + 1], heads1, MUL, MUL).then_inc(s_updated[q], 1)
                else:
                    own.own(STT(STMP[:, q, :], s, F[:, c, j:j + 1], heads1, MUL, MUL))
                    STT(ST[:, c, :], ST[:, c, :], F[:, c, j:j + 1], STMP[:, q, :], MUL, ADD).then_inc(s_updated[q], 1)

            arrived(dve, "bonus")
            for u in range(4):
                mask_gram(0, u)
            dve.wait_ge(y_zeroed, 1)
            for g in range(GROUPS + 1):
                now, nxt, old = g < GROUPS, g + 1 < GROUPS, g > 0
                for l in range(LEVELS):
                    if now:
                        mask_z(g, l, 0)
                        mask_z(g, l, 1)
                    if nxt and l < 3:
                        mask_gram(g + 1, l)
                    if old and l == 3:
                        update(g - 1, 1)
                    if old and l == 0:
                        copy_rhs(g - 1, 0)
                        copy_rhs(g - 1, 1)
                    if old and l == 1:
                        copy_sa(g - 1, 0)
                        copy_sa(g - 1, 1)
                    if old and l == 2:
                        update(g - 1, 0)
                    if nxt and l == 3:
                        mask_gram(g + 1, 3)
            nc.vector.tensor_copy(CST[:, 1:2], CST[:, 5:6]).then_inc(dve_phase, 1)
            others_done(dve, 2, dve_phase)
            heads_of = YT.rearrange("p t (h n) -> p t h n", n=HD)
            sq_heads = SQ.rearrange("p t (h n) -> p t h n", n=HD)
            stat = lambda i, t: GST[:, 64 * i + 16 * t:64 * i + 16 * t + 16]
            bc = lambda a: a.unsqueeze(2).broadcast_to([P, HEADS, HD])
            for t in range(NT):
                own.own(nc.vector.tensor_reduce(stat(0, t), heads_of[:, t], AX.X, ADD))
                own.own(TS(stat(0, t), stat(0, t), 1.0 / HD, None, MUL))
                TT(heads_of[:, t], heads_of[:, t], bc(stat(0, t)), SUB).then_inc(centred, 1)
            own.did(TT(SCB, SILC[:, :, 0:1].broadcast_to([P, KT, P]),
                       con("ones").unsqueeze(1).broadcast_to([P, KT, P]), MUL))
            own.wait()
            nc.vector.tensor_copy(CST[:, 2:3], CST[:, 5:6]).then_inc(silu_c_ready, 1)
            for t in range(NT):
                dve.wait_ge(gn_squared, t + 1)
                last = nc.vector.tensor_reduce(stat(1, t), sq_heads[:, t], AX.X, ADD)
                if t < NT - 1:
                    own.did(last)
            last.then_inc(gn_sums, 1)
            dve.wait_ge(gn_root, 1)
            own.own(nc.vector.reciprocal(GST[:, 128:192], GST[:, 128:192]))
            for t in range(NT):
                dve.wait_ge(centred, t + 1)
                TT(heads_of[:, t], heads_of[:, t], bc(stat(2, t)), MUL).then_inc(y_normed, 1)
            o = arrived(dve, "mods")
            mods = o[:, 0:32].rearrange("p (c k) -> p c k", k=2)
            b2 = VECS[:, VEC["b_shift"]:VEC["b_shift"] + 16].unsqueeze(2).broadcast_to([P, 16, 2])
            free(TT(MODS, mods, b2, ADD), "mods")
            stored(dve, "mods")
            own.own(TS(GSC, MODS[:, 8:16, :], 1.0, None, ADD))
            TT(GSC, GSC, VECS[:, VEC["norm2"]:VEC["norm2"] + 8].unsqueeze(2).broadcast_to([P, 8, 2]), MUL)\
                .then_inc(mods_ready, 1)
            dve.wait_ge(bgate_here, 16)
            for gb in range(2):
                o = arrived(dve, ("gx", gb))
                free(TT(GX[:, gb * 512:(gb + 1) * 512], o[:, :], BGX[:, gb * 512:(gb + 1) * 512], ADD), ("gx", gb))
            for t in range(NT):
                for h in range(2):
                    stored(dve, ("yT", t, h))
                    o = arrived(dve, ("bT", t, h))
                    y = YG[:, 4 * h:4 * h + 4, t * P:(t + 1) * P]
                    free(TT(y, y, o.rearrange("p (c n) -> p c n", c=4), ADD), ("bT", t, h))
                    stored(dve, ("bT", t, h))
                    TT(y, y, GT[:, 4 * h:4 * h + 4, t * P:(t + 1) * P], MUL).then_inc(y_gated, 1)
            dve.wait_ge(x_again, 16)
            for nb in range(4):
                for th in range(2):
                    o = arrived(dve, ("o", nb, th)).rearrange("p (i n) -> p i n", i=2)
                    at = slice(nb * 256, (nb + 1) * 256)
                    free(TT(X1[:, 2 * th:2 * th + 2, at], o, XR[:, 2 * th:2 * th + 2, at], ADD), ("o", nb, th))
            nc.vector.tensor_copy(CST[:, 1:2], CST[:, 5:6]).then_inc(dve_phase, 1)
            others_done(dve, 3, dve_phase)
            dve.wait_ge(n2_root, 2)
            own.did(nc.vector.reciprocal(rstd, rstd))
            own.own(nc.vector.reciprocal(SUMS[:, 2:4], SUMS[:, 2:4]))
            for t in range(2):
                TS(CX[:, t, :], CX[:, t, :], SUMS[:, 2 + t:3 + t], None, MUL).then_inc(cn_ready, 1)
            for t in range(NT):
                TS(XN[:, t, :], X1[:, t, :], rstd[:, t:t + 1], None, MUL).then_inc(xn_ready, 1)

            def head_dst(i):
                name, c = ITEMS[i]
                return {"q": QT[:, c, :], "kk": KTP[:, c, HD:HD + T], "ck": CK[:, c, :]}[name]

            def scale_heads(i):
                n = CTX if ITEMS[i][0] == "ck" else T
                stored(dve, ("ss", i))
                r = DROOT[i % 2][:, 0:n]
                own.own(nc.vector.reciprocal(r, r))
                stored(dve, ITEMS[i])
                TT(head_dst(i), head_dst(i), r, MUL).then_inc(qk_done, 1)

            for i, key in enumerate(ITEMS):
                n = CTX if key[0] == "ck" else T
                dve.wait_ge(qk_squared, i + 1)
                g = VECS[:, VEC["q_gain"]:VEC["q_gain"] + 1] if key[0] == "q" else \
                    VECS[:, VEC["k_gain"]:VEC["k_gain"] + 1]
                free(TS(head_dst(i), arrived(dve, key)[:, 0:n], g, None, MUL), key)
                if i:
                    scale_heads(i - 1)
            scale_heads(len(ITEMS) - 1)
            for c in range(8):
                dve.wait_ge(gate2_exp, c + 1)
                e = GATE[:, c, :]
                own.own(TS(e, e, 1.0, None, ADD))
                own.own(nc.vector.reciprocal(e, e))
                free(TT(e, arrived(dve, ("g2", c))[:, :], e, MUL), ("g2", c))
            for n in range(4):
                o = arrived(dve, ("fo", n)).rearrange("p (col r) -> p col r", r=GH)
                free(TT(MIX[:, n, :].rearrange("p (r col) -> p col r", r=GH), o,
                        GATE[:, n, :].rearrange("p (col r) -> p col r", r=GH), MUL), ("fo", n))

            def mask_scores(n):
                qt, h = divmod(n, NAH)
                o = arrived(dve, ("s", n))
                if n >= 3:
                    arrived(dve, ("pt", n - 3))
                if n >= 4:
                    stored(dve, ("s", n - 4))
                m = MXN[:, 2 * (n % 4):2 * (n % 4) + 1]
                m2 = MXN[:, 2 * (n % 4) + 1:2 * (n % 4) + 2]
                own.own(nc.vector.tensor_reduce(m, o[:, WIN:512], AX.X, MAX))
                own.own(nc.vector.tensor_tensor_reduce(
                    out=PB[n % 3][:, 0:WIN], in0=o[:, 0:WIN], in1=BM[:, (0, 1, 1, 2)[qt], h, :], scale=1.0, scalar=m,
                    op0=ADD, op1=MAX, accum_out=m2))
                TS(MXN2[:, n % 4:n % 4 + 1], m2, -1.0, None, MUL).then_inc(masked, 1)

            def copy_turned_probs(n):
                o = arrived(dve, ("pt", n))
                if n >= 3:
                    k = n - 3
                    if k % NAH == NAH - 1:
                        arrived(dve, ("at", k // NAH))
                    else:
                        dve.wait_ge(pv_done, (k // NAH) * (NAH - 1) + k % NAH + 1)
                free(nc.vector.tensor_copy(PT[n % 3], o[:, :]), ("pt", n))

            def scale_out(qt):
                s1, s2 = SUMS[:, 8 + 8 * qt:16 + 8 * qt], SUMS[:, 40 + 8 * qt:48 + 8 * qt]
                own.own(TT(s1, s1, s2, ADD))
                own.own(nc.vector.reciprocal(s1, s1))
                o = arrived(dve, ("at", qt)).rearrange("p (h n) -> p h n", h=NAH)
                if qt:
                    arrived(dve, ("oT", qt - 1))
                free(TT(ON.rearrange("p (h n) -> p h n", h=NAH), o, s1.unsqueeze(2).broadcast_to([P, NAH, HD]), MUL),
                     ("at", qt))

            def gate_out(qt):
                o = arrived(dve, ("oT", qt)).rearrange("p (c col r) -> p c col r", c=4, r=GH)
                g = GATE[:, 4:8, qt * P:(qt + 1) * P].rearrange("p c (col r) -> p c col r", r=GH)
                dst = MIX[:, 4:8, :].rearrange("p c (r col) -> p c col r", r=GH)[:, :, 16 * qt:16 * qt + 16, :]
                for i in range(4):
                    ins = TT(dst[:, i], o[:, i], g[:, i], MUL)
                    if i < 3:
                        own.did(ins)
                free(ins, ("oT", qt))

            dve.wait_ge(bm_ready, 1)
            NU = NT * NAH
            for n in range(NU + 5):
                if n < NU:
                    mask_scores(n)
                if 1 <= n < NU + 1:
                    copy_turned_probs(n - 1)
                if n >= NAH + 2 and (n - NAH - 2) % NAH == 0:
                    scale_out((n - NAH - 2) // NAH)
                if n >= NAH + 4 and (n - NAH - 4) % NAH == 0:
                    gate_out((n - NAH - 4) // NAH)
            for i in range(8):
                nb, th = divmod(i, 2)
                o = arrived(dve, ("z", nb, th)).rearrange("p (j n) -> p j n", j=2)
                if i >= 4:
                    dve.wait_ge(out_stored[i % 4], 16)
                free(TT(OUTB[i % 4], o, GX[:, nb * 256:(nb + 1) * 256].unsqueeze(1).broadcast_to([P, 2, 256]), MUL),
                     ("z", nb, th))

        @block.gpsimd
        def _(pool):
            TT, TS = nc.gpsimd.tensor_tensor, nc.gpsimd.tensor_scalar
            own = Steps(pool, pool_steps)
            pool.wait_ge(vectors_ready, 1)
            for c in range(KT):
                pool.wait_ge(a_ready, c + 1)
                TS(KMOD, AB[:, c, :], vec("k_a", c), NKA[:, c:c + 1], MUL, ADD).then_inc(kmod_ready, 1)
                pool.wait_ge(kmod_ready, c + 1)
                stored(pool, ("k", c))
                own.own(TT(KB[:, c, :], KB[:, c, :], KMOD, MUL))
                stored(pool, ("r", c))
                if c:
                    pool.wait_ge(bonus_done, c)
                TT(RKT, KB[:, c, :], AR[:, 1, c, :], MUL).then_inc(rk_ready, 1)
                pool.wait_ge(decays_ready, c + 1)
                pool.wait_ge(rk_ready, c + 1)
                TT(KB[:, c, :], KB[:, c, :], E2, MUL).then_inc(kappa_ready, 1)
            pool.wait_ge(kappa_ready, KT)
            TT(CST[:, 3:4], CST[:, 6:7], CST[:, 6:7], ADD).then_inc(pool_phase, 1)
            others_done(pool, 1, pool_phase)
            arrived(pool, "bonus")
            nc.gpsimd.memset(YL, 0.0).then_inc(y_zeroed, 1)
            pool.wait_ge(y_copied[1], GROUPS)
            pool.wait_ge(y_zeroed, 1)
            TT(CST[:, 3:4], CST[:, 6:7], CST[:, 6:7], ADD).then_inc(pool_phase, 1)
            others_done(pool, 2, pool_phase)
            for t in range(NT):
                TT(BV[:, t, :].rearrange("p (h n) -> p h n", n=HD), V[:, t, :].rearrange("p (h n) -> p h n", n=HD),
                   BON[:, 16 * t:16 * t + 16].unsqueeze(2).broadcast_to([P, HEADS, HD]), MUL).then_inc(bv_ready, 1)
            pool.wait_ge(bv_ready, NT)
            stored(pool, ("o", 3, 1))
            TT(CST[:, 3:4], CST[:, 6:7], CST[:, 6:7], ADD).then_inc(pool_phase, 1)
            others_done(pool, 3, pool_phase)
            own.did(nc.gpsimd.memset(XNP[:, :, 0:HD], 0.0))
            own.did(nc.gpsimd.memset(XNP[:, :, HD + T:PADT], 0.0))
            own.did(nc.gpsimd.memset(KTP[:, :, 0:HD], 0.0))
            nc.gpsimd.memset(KTP[:, :, HD + T:PADT], 0.0).then_inc(pads_ready, 1)
            pool.wait_ge(rel_here, 16 * 17)
            near_v = NEAR.rearrange("p (v a b) -> p v a b", v=3, b=GH)
            for v in range(3):
                for h in range(NAH):
                    r = REL[:, h * RBW:h * RBW + 1]
                    bias = bass.AP(r.tensor, r.offset + 7 * 31, [list(r.ap[0]), [1, 32], [-31, GH]])
                    ins = TT(BM[:, v, h, :].rearrange("p (a b) -> p a b", b=GH), bias, near_v[:, v], ADD)
                    if (v, h) != (2, NAH - 1):
                        own.did(ins)
            ins.then_inc(bm_ready, 1)
            for i in range(8):
                nb, th = divmod(i, 2)
                stored(pool, ("z", nb, th))
                at = slice(nb * 256, (nb + 1) * 256)
                TT(OUTB[i % 4], OUTB[i % 4], X1[:, 2 * th:2 * th + 2, at], ADD).then_inc(out_ready, 1)


_OUT = (1, T, D)


def kernel(**inputs):
    import concourse.bacc as bacc
    from concourse.bass_utils import run_bass_kernel_spmd as run
    import ml_dtypes

    g = {k: np.ascontiguousarray(v) for k, v in inputs.items()}
    f = np.float32

    def rows(a):
        return a.reshape(-1, P).T

    mu = g["l0_mu"]
    parts = [rows(g["l0_norm"])] + [rows(mu[i]) for i in range(6)]
    parts += [rows(g["l0_" + n]) for n in ("w0", "a0", "k_k", "k_a", "r_k", "gn_w", "gn_b")]
    parts += [rows(g["c_2"]), rows(g["c_ctx_2"]), rows(g["norm_g_2"]), rows(g["b_ada_2"][0, :2 * D])]
    parts += [np.tile(g["q_norm_g_2"][0], 2)[:, None], np.tile(g["k_norm_g_2"][0], 2)[:, None]]
    consts, cos_t, nsin_t, near = shape_constants()
    arrays = {
        "x": g["x"][0], "vecs": np.concatenate(parts, 1), "consts": consts, "cos_t": cos_t, "nsin_t": nsin_t,
        "near": near,
        "ident_b": np.concatenate([np.eye(P)] * 2, 1).astype(ml_dtypes.bfloat16),
        "w_in": g["l0_w_in"], "w_up": g["l0_w_up"], "a_up": g["l0_a_up"], "w_out": g["l0_w_out"],
        "ctx_x": g["ctx_2"][0], "w_ada": g["w_ada_2"][0], "b_gate": g["b_ada_2"][0, 2 * D:],
        "w_in2": g["w_in_2"][0], "w_four": g["w_four_2"][0],
        "rel_bias": np.pad(g["rel_bias_2"][0][:, ::-1].reshape(NAH, RB), ((0, 0), (RBPAD, RBPAD))),
        "w_out2": g["w_out_2"][0],
    }
    arrays = {k: np.ascontiguousarray(v) for k, v in arrays.items()}
    nc = bacc.Bacc("TRN2", target_bir_lowering=False, num_devices=1)
    args = [nc.dram_tensor(k, v.shape, mybir.dt.from_np(v.dtype), kind="ExternalInput").ap()
            for k, v in arrays.items()]
    out = nc.dram_tensor("out", (T, D), mybir.dt.float32, kind="ExternalOutput").ap()
    rwkv_then_grid_block(nc, *args, out)
    r = run(nc, [arrays], core_ids=[0])
    return r.results[0]["out"].reshape(_OUT)
```

```python
import math
from contextlib import ExitStack

import numpy as np

import concourse.bass as bass
from concourse import mybir

T, D, P = 512, 1024, 128
KT, NT = D // P, T // P
PAIRS, HEADS, HD = 8, 16, 64
BLK = 16
LEVELS = 3
BATCHES, UNITS = 4, 16
GROUPS = NT * 4
CTX, NAH, GW, GH = 256, 8, 64, 8
WIN = 256
PADT = T + 2 * HD
KAPPA = math.exp(-0.5)
NORM_EPS, GN_EPS = 1e-6, 64e-5
RB = 15 * 31
RBW = 7 * 31 + 32
RBPAD = 8

CONST = {}
_at = 0
for _n, _w in [("ident", P), ("heads", P), ("gram", 2 * P), ("level", LEVELS * HD), ("ones", P), ("blocks", P),
               ("dft128", 2 * P), ("eps", 3)]:
    CONST[_n] = (_at, _w)
    _at += _w
CONST_W = _at
VEC = {n: KT * i for i, n in enumerate(
    ["norm", "mu_r", "mu_w", "mu_k", "mu_v", "mu_a", "mu_g", "w0", "a0", "k_k", "k_a", "r_k", "gn_w", "gn_b",
     "c", "c_ctx", "norm2", "b_shift", "b_scale",
     "b_gate"])}
VEC["q_gain"] = KT * len(VEC)
VEC["k_gain"] = VEC["q_gain"] + 1
VEC_W = VEC["k_gain"] + 1


def shape_constants():
    f = np.float32
    i, j = np.arange(P)[:, None], np.arange(P)[None, :]
    strict, incl = (i < j).astype(f), (i <= j).astype(f)
    c = np.zeros((P, CONST_W), f)

    def put(name, a):
        at, w = CONST[name]
        c[:, at:at + w] = a

    put("ident", np.eye(P, dtype=f))
    put("heads", (i // HD == j // HD).astype(f))
    put("gram", np.concatenate([strict, incl], 1))
    levels = []
    for l in range(LEVELS):
        b = BLK << l
        even = np.concatenate([np.arange(s, s + b) for s in range(0, P, 2 * b)])
        levels.append((i // b == even[None, :] // b + 1).astype(f))
    put("level", np.concatenate(levels, 1))
    put("ones", 1.0)
    put("blocks", (i // BLK == j // BLK).astype(f))
    cl, key = np.arange(P)[:, None] // GH, np.arange(WIN)[None, :] // GH
    near = []
    for tile in (0, 1, 3):
        q, k = 16 * tile + cl, 16 * tile - 8 + key
        first = np.clip(q - 8, 0, GW - 16)
        near.append(np.where((k >= first) & (k < first + 16), 0.0, -1e30).astype(f))
    w = 2 * np.pi * ((i * j) % P) / P
    put("dft128", np.concatenate([np.cos(w), np.sin(w)], 1) / 256.0)
    put("eps", np.array([[NORM_EPS, GN_EPS, HD * NORM_EPS]], f))
    order = np.array([r * GW + col for col in range(GW) for r in range(GH)])
    w = 2 * np.pi * ((order[:, None] * order[None, :]) % T) / T
    return c, np.cos(w).astype(f), (-np.sin(w)).astype(f), np.concatenate(near, 1)


def rwkv_then_grid_block(nc, x, vecs, consts, cos_t, nsin_t, near, w_in, w_up, a_up, w_out,
                         ctx_x, w_ada, w_in2, w_four, rel_bias, w_out2, out, lt_dram, inv_dram):
    f32 = mybir.dt.float32
    ALU, ACT, AX = mybir.AluOpType, mybir.ActivationFunctionType, mybir.AxisListType
    MUL, ADD, SUB, MAX = ALU.mult, ALU.add, ALU.subtract, ALU.max

    stack = ExitStack()
    with stack:
        def sem(name):
            return stack.enter_context(nc.semaphore(name))

        END, SMALL_W = 53207, 612
        arena = stack.enter_context(nc.sbuf_tensor("arena", [P, END], f32))
        banks = [stack.enter_context(nc.psum_tensor(f"bank{b}", [P, 512], f32)) for b in range(8)]

        class Room:
            def __init__(self, at, end):
                self.at, self.end = at, end

            def take(self, width, parts=P):
                at = self.at
                self.at += width
                assert self.at <= self.end, (self.at, self.end)
                return arena[0:parts, at:at + width]

        fixed = Room(0, END)
        CON = fixed.take(CONST_W)
        VECS = fixed.take(VEC_W)
        MROW = fixed.take(256, 2)
        SMALL = fixed.take(SMALL_W)
        WR = [fixed.take(2048) for _ in range(3)]

        def con(name):
            at, w = CONST[name]
            return CON[:, at:at + w]

        def vec(name, c, n=1):
            return VECS[:, VEC[name] + c:VEC[name] + c + n]

        def half_vec(name, c, n=1):
            at = {"w0": 0, "a0": KT}[name] + c
            return HVEC[:, at:at + n]

        ident, heads1, gram_mask = con("ident"), con("heads"), con("gram")
        sm = Room(0, SMALL_W)

        def small(w):
            at = sm.at
            sm.at += w
            assert sm.at <= SMALL_W
            return SMALL[:, at:at + w]

        rstd = small(4)
        ssq = small(4)
        F = small(32).rearrange("p (c j) -> p c j", j=4)
        BON = small(64)
        RKB = small(16).rearrange("p (c h) -> p c h", h=2)
        MID = small(12)
        GST = small(64 * 3)
        SILC = small(16).rearrange("p (c k) -> p c k", k=2)
        SILT = small(32)
        MODS = small(48).rearrange("p (c k) -> p c k", k=2)
        GSC = small(16).rearrange("p (c k) -> p c k", k=2)
        CST = small(8)
        MXN = small(32)
        SUMS = small(80)
        HVEC = small(2 * KT)
        NKA = small(KT)
        MXN2 = small(4)

        base = fixed.at
        roomA = Room(base, END)
        AR = roomA.take(8192).rearrange("p (s c t) -> p s c t", s=2, c=KT)
        KB = roomA.take(4096).rearrange("p (c t) -> p c t", c=KT)
        AB = roomA.take(4096).rearrange("p (c t) -> p c t", c=KT)
        V = roomA.take(4096).rearrange("p (t n) -> p t n", t=NT)
        HT_ = roomA.take(KT * 513)
        HT = HT_.rearrange("p (c t) -> p c t", c=KT)
        GT = HT_[:, 0:4096].rearrange("p (c t) -> p c t", c=KT)
        b0 = roomA.at
        DX = roomA.take(4096).rearrange("p (c t) -> p c t", c=KT)
        XI = [roomA.take(4096).rearrange("p (c t) -> p c t", c=KT) for _ in range(2)]
        b1 = roomA.at
        LOW = roomA.take(1024, 64).rearrange("p (s t) -> p s t", s=2)
        UPS = roomA.take(2048, 64).rearrange("p (s n) -> p s n", s=2)
        SIGW, CSUM, E2, KMOD = [roomA.take(512) for _ in range(4)]
        SQ2 = [roomA.take(512) for _ in range(2)]
        root_b = roomA.take(516)
        ROOT = [roomA.take(512), root_b[:, 0:512]]
        E1 = root_b.rearrange("p (j t) -> p j t", j=4)
        RKT = ROOT[0]

        xi0, xi1 = b0 + 4096, b0 + 8192
        XST = arena[:, xi0:xi0 + 2048].rearrange("p (q s u n) -> p q s u n", q=BATCHES, s=2, u=UNITS)
        LTS = [arena[:, xi0 + 2048 + 512 * i:xi0 + 2560 + 512 * i] for i in range(2)]
        LTB = arena[:, xi0 + 3072:xi0 + 3328].rearrange("p (a b) -> p a b", a=BLK)
        XO = arena[:, xi0 + 3328:xi0 + 3840].rearrange("p (s a b) -> p s a b", s=2, a=BLK)
        XTMP = arena[:, xi0 + 3840:xi0 + 4096]
        SQ = arena[:, xi0 + 3072:xi0 + 4096]
        GM = [arena[:, at:at + 2048].rearrange("p (u n) -> p u n", u=4) for at in (b0, b0 + 2048, xi1)]
        XS = arena[:, xi1 + 2048:xi1 + 4096].rearrange("p (g u s n) -> p g u s n", g=2, u=4, s=2)
        roomB2 = Room(b1, END)
        yt3 = roomB2.take(3072)
        YT = [yt3[:, 1024 * i:1024 * i + 1024] for i in range(3)] + [arena[:, xi0 + 2048:xi0 + 3072]]
        YG = [y.rearrange("p (c t) -> p c t", c=KT) for y in YT]
        BK = roomB2.take(1536).rearrange("p (g q n) -> p g q n", g=3, q=2)
        RH = roomB2.take(256).rearrange("p (q n) -> p q n", q=2)
        SA = roomB2.take(256).rearrange("p (q n) -> p q n", q=2)
        ST = roomB2.take(1024).rearrange("p (c n) -> p c n", c=PAIRS)
        STMP = roomB2.take(256).rearrange("p (q n) -> p q n", q=2)
        YL_ = roomB2.take(LEVELS * 512)
        YL = YL_.rearrange("p (l u n) -> p l u n", l=LEVELS, u=4)

        def corner(hf, w):
            return banks[hf][:, 2 * P:4 * P].rearrange("p (u w n) -> p u w n", u=2, w=2)[:, :, w, :]

        dlo = Room(base, base + 16384)
        XNP = dlo.take(KT * PADT).rearrange("p (c t) -> p c t", c=KT)
        MIX = XNP[:, :, 0:T]
        xn_flat = dlo.take(4096)
        XN = xn_flat.rearrange("p (t n) -> p t n", t=NT)
        UC = xn_flat.rearrange("p (t s n) -> p t s n", t=NT, s=2)
        OUTB = [xn_flat[:, 512 * i:512 * i + 512].rearrange("p (j n) -> p j n", j=2) for i in range(4)]
        xr_at = dlo.at
        XR = arena[:, xr_at:xr_at + 4096].rearrange("p (t n) -> p t n", t=NT)
        WX = arena[:, xr_at + 4096:xr_at + 6144].rearrange("p (k n) -> p k n", k=KT)
        QT = dlo.take(2048).rearrange("p (c t) -> p c t", c=4)
        CK = dlo.take(1024).rearrange("p (c t) -> p c t", c=4)
        KTP = dlo.take(4 * PADT).rearrange("p (c t) -> p c t", c=4)
        GX = dlo.take(1024)
        gate_flat = HT_[:, 0:4096]
        GATE = gate_flat.rearrange("p (c t) -> p c t", c=8)
        CX = gate_flat[:, 0:2048].rearrange("p (t n) -> p t n", t=2)
        CNT = gate_flat[:, 2048:4096].rearrange("p (c t) -> p c t", c=KT)
        CNJ = gate_flat[:, 2048:3072]
        X1 = arena[:, b0:b0 + 4096].rearrange("p (t n) -> p t n", t=NT)
        dhi = Room(b0 + 4096, END)
        VP = dhi.take(7 * 512).rearrange("p (t n) -> p t n", t=7)
        UT = dhi.take(2048).rearrange("p (c t) -> p c t", c=4)
        YF = UT
        BM = dhi.take(3 * NAH * WIN).rearrange("p (v h n) -> p v h n", v=3, h=NAH)
        pr = dhi.at
        REL = dhi.take(NAH * RBW)
        NEAR = dhi.take(3 * WIN)
        GDIAG = [xn_flat[:, 512 * i:512 * i + 512] for i in range(2)]
        DTMP = [dhi.take(512) for _ in range(2)]
        DROOT = [GX[:, 0:512], dlo.take(512)]
        datt = Room(pr, END)
        PB = [datt.take(512) for _ in range(4)]
        PT = [datt.take(512) for _ in range(3)]
        ON = datt.take(512)

        bank_full = [sem(f"bank_full{b}") for b in range(8)]
        bank_free = [sem(f"bank_free{b}") for b in range(8)]
        weights_here = [sem(f"weights_here{s}") for s in range(3)]
        consts_here, x_here, ups_here, x_again, ctx_here, rel_here, wx_here = [
            sem(n) for n in ("consts_here", "x_here", "ups_here", "x_again", "ctx_here", "rel_here", "wx_here")]
        out_stored = [sem(f"out_stored{i}") for i in range(4)]
        act_steps, dve_steps, pool_steps = sem("act_steps"), sem("dve_steps"), sem("pool_steps")
        act_phase, dve_phase, pool_phase = sem("act_phase"), sem("dve_phase"), sem("pool_phase")
        x_squared, x_scaled, mixed = sem("x_squared"), sem("x_scaled"), sem("mixed")
        k_scaled, k_squared, k_root, kk_done = sem("k_scaled"), sem("k_squared"), sem("k_root"), sem("kk_done")
        csum_ready, decays_ready, a_ready, kmod_ready, rk_ready, kappa_ready, bonus_done = [
            sem(n) for n in ("csum_ready", "decays_ready", "a_ready", "kmod_ready", "rk_ready", "kappa_ready",
                             "bonus_done")]
        vectors_ready, gate_tanh, c_tanh = [sem(n) for n in ("vectors_ready", "gate_tanh", "c_tanh")]
        y_zeroed, ab_ready, inverted, expanded = [sem(n) for n in ("y_zeroed", "ab_ready", "inverted", "expanded")]
        lt_copied, lt_back, inv_out = sem("lt_copied"), sem("lt_back"), sem("inv_out")
        lt_out = [sem(f"lt_out{i}") for i in range(2)]
        inv_back = [sem(f"inv_back{q}") for q in range(BATCHES)]
        mods_block, pv_done = sem("mods_block"), sem("pv_done")
        mods_copied = sem("mods_copied")
        z_ready, y_ready, x_grown, x_added = [[sem(f"{n}{h}") for h in range(2)] for n in
                                              ("z_ready", "y_ready", "x_grown", "x_added")]
        rhs_ready, rhs_copied, sa_ready, sa_copied, ys_ready, s_updated, y_copied = [
            [sem(f"{n}{h}") for h in range(2)] for n in
            ("rhs_ready", "rhs_copied", "sa_ready", "sa_copied", "ys_ready", "s_updated", "y_copied")]
        centred, gn_squared, gn_sums, gn_root, y_normed, bv_ready, y_gated = [
            sem(n) for n in ("centred", "gn_squared", "gn_sums", "gn_root", "y_normed", "bv_ready", "y_gated")]
        n2_root, cn_root, cn_ready, xn_ready, mods_ready, pads_ready, gdiag_ready = [
            sem(n) for n in ("n2_root", "cn_root", "cn_ready", "xn_ready", "mods_ready", "pads_ready", "gdiag_ready")]
        qk_squared, qk_root, qk_done = sem("qk_squared"), sem("qk_root"), sem("qk_done")
        gate2_tanh, bm_ready, masked, out_ready = [sem(n) for n in ("gate2_tanh", "bm_ready", "masked", "out_ready")]

        def cols(w, a, n):
            return w.rearrange("(k p) n -> p k n", p=P)[:, :, a:a + n], w.shape[0] // P, n

        stream = [cols(w_in, 4 * D, P)]
        for first in (D, 0, 2 * D, 3 * D):
            stream += [cols(w_in, first + 256 * b, 256) for b in range(4)]
        stream += [cols(w_ada, 256 * b, 256) for b in range(12)]
        stream += [cols(w_out, 256 * b, 256) for b in range(3)]
        stream += [cols(w_in2, a + 256 * b, 256) for a in (1536, 1024, 2048, 0, 512, 2560) for b in range(2)]
        stream += [cols(cos_t, 0, 512), cols(nsin_t, 0, 512), cols(w_four, 0, 512)]
        stream += [cols(w_out2, 256 * b, 256) for b in range(4)]

        def block_view(n):
            _, k, w = stream[n]
            return WR[n % 3][:, 0:k * w].rearrange("p (k n) -> p k n", k=k)

        class Steps:

            def __init__(self, eng, s):
                self.eng, self.s, self.n = eng, s, 0

            def did(self, ins):
                ins.then_inc(self.s, 1)
                self.n += 1

            def wait(self):
                self.eng.wait_ge(self.s, self.n)

            def own(self, ins):
                self.did(ins)
                self.wait()

        where, uses = {}, [0] * 8
        block_key = {}

        def arrived(eng, key):
            b, n = where[key]
            eng.wait_ge(bank_full[b], n)
            return banks[b]

        def free(ins, key):
            ins.then_inc(bank_free[where[key][0]], 1)

        def stored(eng, key):
            b, n = where[key]
            eng.wait_ge(bank_free[b], n)

        def others_done(eng, n, mine):
            for s in (act_phase, dve_phase, pool_phase):
                if s is not mine:
                    eng.wait_ge(s, n)

        def halves(ap, b, s):
            v = ap.rearrange("p (m s b) -> p m s b", s=2, b=b)
            return v[:, :, s, :]

        def halves2(ap, b, s):
            v = ap.rearrange("p u (m s b) -> p u m s b", s=2, b=b)
            return v[:, :, :, s, :]

        last_of_mix = [("low", 0), ("low", 1), ("k", 7), ("r", 7)]
        ITEMS = [("ck", c) for c in range(4)] + [("kk", c) for c in range(4)] + [("q", c) for c in range(4)]
        block = stack.enter_context(nc.Block())

        @block.tensor
        def _(pe):
            mm = nc.tensor.matmul
            taken = [0]

            def weights():
                n = taken[0]
                taken[0] += 1
                pe.wait_ge(weights_here[n % 3], 16 * (n // 3 + 1))
                return block_view(n)

            def out_bank(key, b):
                if uses[b]:
                    pe.wait_ge(bank_free[b], uses[b])
                uses[b] += 1
                where[key] = (b, uses[b])
                return banks[b]

            turn = [0]

            def next_bank(key, n=6):
                turn[0] = (turn[0] + 1) % n
                return out_bank(key, turn[0])

            def full(ins, key):
                ins.then_inc(bank_full[where[key][0]], 1)
                block_key[taken[0] - 1] = key

            def accumulate(o, lhs, rhs, n=KT):
                for k in range(n):
                    last = mm(o, lhs(k), rhs(k), start=(k == 0), stop=(k == n - 1))
                return last

            pe.wait_ge(consts_here, 32)
            pe.wait_ge(x_scaled, NT)
            for c in range(KT):
                o = next_bank(("hT", c))
                for t in range(NT):
                    last = nc.tensor.transpose(o[:, t * P:(t + 1) * P], V[:, t, c * P:(c + 1) * P], ident)
                full(last, ("hT", c))
            w = weights()
            for m in range(2):
                o = next_bank(("low", m))
                for k in range(KT):
                    pe.wait_ge(mixed, KT * m + k + 1)
                    last = mm(o[0:64, :], w[:, k, 64 * m:64 * m + 64], XI[m][:, k, :], start=(k == 0), stop=(k == KT - 1))
                full(last, ("low", m))
            for m, name in ((2, "k"), (3, "r")):
                pe.wait_ge(mixed, KT * (m + 1))
                for nb in range(4):
                    w = weights()
                    for h in range(2):
                        c = 2 * nb + h
                        o = next_bank((name, c))
                        full(accumulate(o[:, :], lambda k: w[:, k, h * P:(h + 1) * P], lambda k: XI[m % 2][:, k, :]),
                             (name, c))
                        if m == 3:
                            pe.wait_ge(k_squared, c + 1)
                            o = next_bank(("kss", c))
                            ins = mm(o[:, :], heads1, SQ2[c % 2], start=True, stop=True)
                            ins.then_inc(bank_full[where["kss", c][0]], 1)
            stored(pe, ("low", 0))
            stored(pe, ("low", 1))
            pe.wait_ge(ups_here, 32)
            pe.wait_ge(vectors_ready, 1)
            bonus_bank = out_bank("bonus", 7)

            def bonus(c):
                pe.wait_ge(rk_ready, c + 1)
                for t in range(NT):
                    last = mm(bonus_bank[:, t * 16 + 2 * c:t * 16 + 2 * c + 2], RKT[:, t * P:(t + 1) * P],
                              RKB[:, c, :], start=True, stop=True, skip_group_check=True)
                if c < KT - 1:
                    last.then_inc(bonus_done, 1)
                else:
                    full(last, "bonus")

            def first_l(c):
                pe.wait_ge(ab_ready, c + 1)
                for h in range(2):
                    o = next_bank(("lt", c, h))
                    lo = HD * h
                    for j in range(NT):
                        at = slice(j * P, (j + 1) * P)
                        last = mm(o[:, at], AB[lo:lo + HD, c, at], AR[lo:lo + HD, 0, c, at], start=True, stop=True,
                                  skip_group_check=True)
                    last.then_inc(bank_full[where["lt", c, h][0]], 1)

            for c in range(KT):
                for s, name in ((0, "w"), (1, "a")):
                    o = next_bank((name, c))
                    mm(o[:, :], UPS[:, s, c * P:(c + 1) * P], LOW[:, s, :], start=True, stop=True)\
                        .then_inc(bank_full[where[name, c][0]], 1)
                w = weights()
                pe.wait_ge(mixed, KT * (5 if c < 4 else 6))
                for h in range(2):
                    if c < 4:
                        o = next_bank(("v", c, h))
                        for i in range(2):
                            t = 2 * h + i
                            last = accumulate(o[:, i * 256:(i + 1) * 256], lambda k: XI[0][:, k, t * P:(t + 1) * P],
                                              lambda k: w[:, k, :])
                        full(last, ("v", c, h))
                    else:
                        cc = 2 * (c - 4) + h
                        o = next_bank(("g", cc))
                        full(accumulate(o[:, :], lambda k: w[:, k, h * P:(h + 1) * P], lambda k: XI[1][:, k, :]),
                             ("g", cc))
                if c >= 1:
                    bonus(c - 1)
                if c == KT - 1:
                    bonus(c)
                if c >= 4:
                    first_l(2 * (c - 4))
                    first_l(2 * (c - 4) + 1)
            for b in range(8):
                if uses[b]:
                    pe.wait_ge(bank_free[b], uses[b])
            others_done(pe, 1, None)

            gram_n = [0]

            def gram_bank(key):
                b = 4 + gram_n[0] % 2
                gram_n[0] += 1
                return out_bank(key, b)

            def gram(g, u):
                j, cc = divmod(g, 4)
                c, lo = 2 * cc + u // 2, HD * (u % 2)
                o = gram_bank(("gram", g, u))
                at = slice(j * P, (j + 1) * P)
                mm(o[:, 0:256], AB[lo:lo + HD, c, at], AR[lo:lo + HD, :, c, at], start=True, stop=True,
                   skip_group_check=True)
                mm(o[:, 256:512], KB[lo:lo + HD, c, at], AR[lo:lo + HD, :, c, at], start=True, stop=True,
                   skip_group_check=True).then_inc(bank_full[where["gram", g, u][0]], 1)

            def turned(g):
                j, cc = divmod(g, 4)
                o = gram_bank(("turn", g))
                for q in range(2):
                    for s, src in enumerate((AB, KB)):
                        last = nc.tensor.transpose(o[:, (2 * q + s) * P:(2 * q + s + 1) * P],
                                                   src[:, 2 * cc + q, j * P:(j + 1) * P], ident)
                last.then_inc(bank_full[where["turn", g][0]], 1)

            def off_product(g, l, hf):
                n = LEVELS * g + l
                if l == 0:
                    pe.wait_ge(expanded, g + 1)
                if n:
                    pe.wait_ge(x_added[hf], n)
                for i in range(2):
                    u = 2 * hf + i
                    if l == 0:
                        stored(pe, ("gram", g, u))
                    last = mm(banks[hf][:, i * P:(i + 1) * P], GM[g % 3][:, u, 0:P], XS[:, g % 2, u, 0, :],
                              start=True, stop=True, skip_group_check=True)
                last.then_inc(z_ready[hf], 1)

            def grow(g, l, hf):
                pe.wait_ge(y_ready[hf], LEVELS * g + l + 1)
                for i in range(2):
                    u = 2 * hf + i
                    xt = XS[:, g % 2, u, 1, :]
                    o = banks[hf][:, (2 + i) * P:(3 + i) * P]
                    y = YL[:, l, u, :]
                    if l < LEVELS - 1:
                        mm(o[:, 0:HD], xt, halves(y, BLK << l, 0), start=True, stop=True, skip_group_check=True)
                    last = mm(o[:, HD:P], y, halves(xt, BLK << l, 1), start=True, stop=True, skip_group_check=True)
                last.then_inc(x_grown[hf], 1)

            def scan_rhs(g, q):
                j, cc = divmod(g, 4)
                c = 2 * cc + q
                o = banks[6 + q][:, 0:P]
                if g:
                    pe.wait_ge(y_copied[q], g)
                    pe.wait_ge(s_updated[q], min(g, GROUPS - 4))
                for i in range(2):
                    stored(pe, ("gram", g, 2 * q + i))
                if j:
                    mm(o, AR[:, 0, c, j * P:(j + 1) * P], ST[:, c, :], start=True, stop=False, skip_group_check=True)
                for i in range(2):
                    last = mm(o[:, i * HD:(i + 1) * HD], GM[g % 3][:, 2 * q + i, 2 * P:3 * P],
                              V[:, j, c * P + i * HD:c * P + (i + 1) * HD], start=(j == 0 and i == 0), stop=(i == 1),
                              skip_group_check=True)
                last.then_inc(rhs_ready[q], 1)

            def scan_sa(g, q):
                pe.wait_ge(rhs_copied[q], g + 1)
                pe.wait_ge(x_added[q], LEVELS * (g + 1))
                for i in range(2):
                    last = mm(banks[6 + q][:, P + i * HD:P + (i + 1) * HD], XS[:, g % 2, 2 * q + i, 1, :],
                              RH[:, q, i * HD:(i + 1) * HD], start=True, stop=True, skip_group_check=True)
                last.then_inc(sa_ready[q], 1)

            def scan_out(g, q):
                j, cc = divmod(g, 4)
                c = 2 * cc + q
                pe.wait_ge(sa_copied[q], g + 1)
                o = banks[6 + q][:, 2 * P:3 * P]
                if j:
                    mm(o, AR[:, 1, c, j * P:(j + 1) * P], ST[:, c, :], start=True, stop=False, skip_group_check=True)
                for i in range(2):
                    gm = GM[g % 3][:, 2 * q + i, :]
                    mm(o[:, i * HD:(i + 1) * HD], gm[:, P:2 * P], SA[:, q, i * HD:(i + 1) * HD],
                       start=(j == 0 and i == 0), stop=False, skip_group_check=True)
                    last = mm(o[:, i * HD:(i + 1) * HD], gm[:, 3 * P:4 * P],
                              V[:, j, c * P + i * HD:c * P + (i + 1) * HD], start=False, stop=(i == 1),
                              skip_group_check=True)
                if j < NT - 1:
                    stored(pe, ("turn", g))
                    s = banks[6 + q][:, 3 * P:4 * P]
                    mm(s, BK[:, g % 3, q, 0:P], SA[:, q, :], start=True, stop=False, skip_group_check=True)
                    last = mm(s, BK[:, g % 3, q, P:2 * P], V[:, j, c * P:(c + 1) * P], start=False, stop=True,
                              skip_group_check=True)
                last.then_inc(ys_ready[q], 1)

            def modulation(n):
                w = weights()
                if n == 0:
                    out_bank("mods", 2)
                last = accumulate(banks[2][0:2, 0:256], lambda k: SILC[:, k, :], lambda k: w[:, k, :])
                last.then_inc(mods_block, 1)
                block_key[taken[0] - 1] = n + 1

            def turn_mods(n):
                pe.wait_ge(mods_copied, n + 1)
                for h in range(2):
                    at = 256 + 4 * n + 2 * h
                    last = nc.tensor.transpose(banks[2][:, at:at + 2], MROW[:, h * P:(h + 1) * P], ident[0:2, 0:2])
                if n == 11:
                    last.then_inc(bank_full[2], 1)

            def turn_y(j, piece):
                h = piece // 2
                if piece == 0:
                    pe.wait_ge(y_normed, j + 1)
                    pe.wait_ge(bv_ready, j + 1)
                name, src = ("yT", YT[j]) if piece % 2 == 0 else ("bT", V[:, j, :])
                o = out_bank((name, j, h), 3)
                for i in range(4):
                    last = nc.tensor.transpose(o[:, i * P:(i + 1) * P], src[:, (4 * h + i) * P:(4 * h + i + 1) * P],
                                               ident)
                last.then_inc(bank_full[3], 1)

            for u in range(4):
                gram(0, u)
            turned(0)
            pe.wait_ge(y_zeroed, 1)
            for g in range(GROUPS + 4):
                now, nxt, old = g < GROUPS, g + 1 < GROUPS, 0 < g <= GROUPS
                mod = g - 1 if 1 <= g <= 12 else None
                turning = g in (8, 12, 16)
                if g == 13:
                    turn_mods(11)
                for l in range(LEVELS):
                    if now:
                        off_product(g, l, 0)
                        off_product(g, l, 1)
                    if nxt:
                        gram(g + 1, l)
                    if old and l == 0:
                        scan_rhs(g - 1, 0)
                        scan_rhs(g - 1, 1)
                    if old and l == 1:
                        scan_out(g - 1, 0)
                    if old and l == 2:
                        scan_out(g - 1, 1)
                    if mod is not None and l == 0:
                        if mod:
                            turn_mods(mod - 1)
                        modulation(mod)
                    if now:
                        grow(g, l, 0)
                        grow(g, l, 1)
                    if old and l == 0:
                        scan_sa(g - 1, 0)
                        scan_sa(g - 1, 1)
                    if nxt and l == 1:
                        gram(g + 1, 3)
                    if nxt and l == 2:
                        turned(g + 1)
                    if turning:
                        turn_y(g // 4 - 2, l)
                if turning:
                    turn_y(g // 4 - 2, 3)

            wo = [weights(), weights()]

            def project_y(t, h):
                pe.wait_ge(y_gated, 2 * (t + 1))
                if (t, h) == (0, 1):
                    wo.extend([weights(), WX])
                    pe.wait_ge(wx_here, 16)
                o = next_bank(("o", t, h))
                for i in range(2):
                    last = accumulate(o[:, i * 256:(i + 1) * 256], lambda k: YG[t][:, k, :],
                                      lambda k: wo[2 * h + i][:, k, :])
                last.then_inc(bank_full[where["o", t, h][0]], 1)

            def turn_x1(t):
                pe.wait_ge(xn_ready, t + 1)
                for h in range(2):
                    o = next_bank(("xT", t, h))
                    for i in range(4):
                        last = nc.tensor.transpose(o[:, i * P:(i + 1) * P], XN[:, t, (4 * h + i) * P:(4 * h + i + 1) * P],
                                                   ident)
                    last.then_inc(bank_full[where["xT", t, h][0]], 1)

            for t in range(3):
                project_y(t, 0)
            for piece in range(4):
                turn_y(3, piece)
            project_y(3, 0)
            block_key[taken[0] - 2] = block_key[taken[0] - 1] = ("o", 3, 0)
            project_y(0, 1)
            pe.wait_ge(cn_ready, 2)
            for h in range(4):
                o = next_bank(("cT", h))
                for i in range(2):
                    for t in range(2):
                        c = 2 * h + i
                        last = nc.tensor.transpose(o[:, i * 256 + t * P:i * 256 + (t + 1) * P],
                                                   CX[:, t, c * P:(c + 1) * P], ident)
                last.then_inc(bank_full[where["cT", h][0]], 1)
            items, kw = [], []
            tok = slice(HD, HD + T)

            def head_norm(i):
                n = CTX if ITEMS[i][0] == "ck" else T
                pe.wait_ge(qk_squared, i + 1)
                o = next_bank(("ss", i))
                mm(o[:, 0:n], heads1, DTMP[i % 2][:, 0:n], start=True, stop=True)\
                    .then_inc(bank_full[where["ss", i][0]], 1)

            def qk_output(name, c, w, h, rhs, n):
                o = next_bank((name, c))
                last = accumulate(o[:, 0:n], lambda k: w[:, k, h * P:(h + 1) * P], rhs)
                last.then_inc(bank_full[where[name, c][0]], 1)
                items.append((name, c))
                if len(items) > 1:
                    head_norm(len(items) - 2)

            project_y(1, 1)
            project_y(2, 1)
            turn_x1(0)
            project_y(3, 1)
            block_key[taken[0] - 1] = ("o", 3, 1)
            turn_x1(1)
            for h in range(4):
                stored(pe, ("cT", h))
            for nb in range(2):
                kw.append(weights())
                for h in range(2):
                    qk_output("ck", 2 * nb + h, kw[nb], h, lambda k: CNT[:, k, :], CTX)
                turn_x1(2 + nb)
            for t in range(NT):
                stored(pe, ("xT", t, 0))
                stored(pe, ("xT", t, 1))
            pe.wait_ge(pads_ready, 1)
            for nb in range(2):
                for h in range(2):
                    qk_output("kk", 2 * nb + h, kw[nb], h, lambda k: XNP[:, k, tok], T)
                block_key[taken[0] - 2 + nb] = ("kk", 2 * nb + 1)
            for nb in range(2):
                w = weights()
                for h in range(2):
                    qk_output("q", 2 * nb + h, w, h, lambda k: XNP[:, k, tok], T)
                block_key[taken[0] - 1] = ("q", 2 * nb + 1)
            head_norm(len(items) - 1)
            for nb in range(2):
                w = weights()
                for b4 in range(4):
                    o = next_bank(("vv", nb, b4))
                    for i in range(2):
                        t = 2 * b4 + i
                        if t < 7:
                            last = accumulate(o[:, i * 256:(i + 1) * 256],
                                              (lambda k: XNP[:, k, t * P:(t + 1) * P]) if t < 5 else
                                              (lambda k: CNT[:, k, (t - 5) * P:(t - 4) * P]), lambda k: w[:, k, :])
                    full(last, ("vv", nb, b4))
            for name, n0 in (("f", 0), ("g2", 0), ("g2", 4)):
                for nb in range(2):
                    w = weights()
                    for h in range(2):
                        key = (name, n0 + 2 * nb + h)
                        o = next_bank(key)
                        full(accumulate(o[:, :], lambda k: w[:, k, h * P:(h + 1) * P], lambda k: XNP[:, k, tok]), key)
            for t in range(NT):
                for gp in range(2):
                    stored(pe, ("f", 2 * gp))
                    stored(pe, ("f", 2 * gp + 1))
                    o = next_bank(("uc", t, gp))
                    for i in range(2):
                        last = mm(o[:, i * 256:(i + 1) * 256], UT[:, 2 * gp + i, t * P:(t + 1) * P], con("dft128"),
                                  start=True, stop=True)
                    last.then_inc(bank_full[where["uc", t, gp][0]], 1)
            dft = [weights(), weights()]
            for g in range(4):
                o = next_bank(("yf", g))
                for s in range(2):
                    for t in range(NT):
                        stored(pe, ("uc", t, g // 2))
                        last = mm(o[:, :], UC[:, t, s, g * P:(g + 1) * P], dft[s][:, t, :], start=(s == 0 and t == 0),
                                  stop=(s == 1 and t == NT - 1))
                full(last, ("yf", g))
            block_key[taken[0] - 2] = ("yf", 3)
            w = weights()
            for n in range(4):
                o = next_bank(("fo", n))
                for k in range(4):
                    stored(pe, ("yf", k))
                full(accumulate(o[:, :], lambda k: w[:, k, n * P:(n + 1) * P], lambda k: YF[:, k, :], 4), ("fo", n))

            for h in range(2):
                pe.wait_ge(gdiag_ready, h + 1)
                o = next_bank(("gx", h))
                full_ins = mm(o[:, :], con("ones"), GDIAG[h], start=True, stop=True)
                full_ins.then_inc(bank_full[where["gx", h][0]], 1)

            def scores(n):
                qt, h = divmod(n, NAH)
                lo = HD * (h % 2)
                o = out_bank(("s", n), (0, 1, 6)[n % 3])
                q = QT[lo:lo + HD, h // 2, qt * P:(qt + 1) * P]
                mm(o[:, 0:WIN], q, KTP[lo:lo + HD, h // 2, qt * P:qt * P + WIN], start=True, stop=True,
                   skip_group_check=True)
                mm(o[:, WIN:WIN + CTX], q, CK[lo:lo + HD, h // 2, :], start=True, stop=True, skip_group_check=True)\
                    .then_inc(bank_full[where["s", n][0]], 1)

            def turn_probs(n):
                stored(pe, ("s", n))
                o = out_bank(("pt", n), 2 + n % 2)
                for i in range(4):
                    last = nc.tensor.transpose(o[:, i * P:(i + 1) * P], PB[n % 4][:, i * P:(i + 1) * P], ident)
                last.then_inc(bank_full[2 + n % 2], 1)

            def take_values(n):
                qt, h = divmod(n, NAH)
                stored(pe, ("pt", n))
                b = 4 if qt % 2 == 0 else 7
                o = out_bank(("at", qt), b) if h == 0 else banks[b]
                for i in range(4):
                    v = VP[:, qt + i if i < 2 else 3 + i, h * HD:(h + 1) * HD]
                    last = mm(o[:, h * HD:(h + 1) * HD], PT[n % 3][:, i * P:(i + 1) * P], v, start=(i == 0),
                              stop=(i == 3), skip_group_check=True)
                last.then_inc(bank_full[b], 1) if h == NAH - 1 else last.then_inc(pv_done, 1)

            def turn_out(qt):
                stored(pe, ("at", qt))
                o = out_bank(("oT", qt), 5)
                for i in range(4):
                    last = nc.tensor.transpose(o[:, i * P:(i + 1) * P], ON[:, i * P:(i + 1) * P], ident)
                last.then_inc(bank_full[5], 1)

            pe.wait_ge(qk_done, len(ITEMS))
            for nb in range(2):
                for b4 in range(4):
                    stored(pe, ("vv", nb, b4))
            NU = NT * NAH
            for n in range(NU + 6):
                if n < NU:
                    scores(n)
                if 2 <= n < NU + 2:
                    turn_probs(n - 2)
                if 3 <= n < NU + 3:
                    take_values(n - 3)
                if n >= NAH + 5 and (n - NAH - 5) % NAH == 0:
                    turn_out((n - NAH - 5) // NAH)
            for nb in range(4):
                w = weights()
                for th in range(2):
                    o = next_bank(("z", nb, th))
                    if nb == 0 and th == 0:
                        for n in range(4):
                            stored(pe, ("fo", n))
                            stored(pe, ("oT", n))
                    for i in range(2):
                        t = 2 * th + i
                        last = accumulate(o[:, i * 256:(i + 1) * 256], lambda k: MIX[:, k, t * P:(t + 1) * P],
                                          lambda k: w[:, k, :])
                    full(last, ("z", nb, th))

        @block.sync
        def _(sp):
            x_t = x.rearrange("(t p) n -> p t n", p=P)
            sp.dma_start(V, x_t).then_inc(x_here, 16)
            sp.dma_start(CON, consts).then_inc(consts_here, 16)
            sp.dma_start(VECS, vecs).then_inc(consts_here, 16)
            for n, (src, k, w) in enumerate(stream):
                if n >= 3:
                    key = block_key[n - 3]
                    if isinstance(key, int):
                        sp.wait_ge(mods_block, key)
                    else:
                        arrived(sp, key)
                sp.dma_start(block_view(n), src).then_inc(weights_here[n % 3], 16)
                if n == 0:
                    sp.dma_start(UPS[:, 0, :], w_up).then_inc(ups_here, 16)
                    sp.dma_start(UPS[:, 1, :], a_up).then_inc(ups_here, 16)
                if n == 31:
                    sp.wait_ge(ys_ready[0], GROUPS)
                    sp.wait_ge(ys_ready[1], GROUPS)
                    sp.dma_start(XR, x_t).then_inc(x_again, 16)
                    sp.dma_start(WX, cols(w_out, 768, 256)[0]).then_inc(wx_here, 16)
                    sp.wait_ge(y_gated, 2 * NT)
                    sp.dma_start(CX, ctx_x.rearrange("(t p) n -> p t n", p=P)).then_inc(ctx_here, 16)
                if n == 34:
                    sp.dma_start(NEAR, near).then_inc(rel_here, 16)
                    for cl in range(16):
                        src = bass.AP(rel_bias.tensor, RBPAD + 7 - cl, [[31, GH], [RB + 2 * RBPAD, NAH], [1, RBW]])
                        sp.dma_start(REL[cl * GH:(cl + 1) * GH, :], src).then_inc(rel_here, 16)
            for i in range(8):
                nb, th = divmod(i, 2)
                sp.wait_ge(out_ready, i + 1)
                sp.dma_start(out.rearrange("(t p) n -> p t n", p=P)[:, 2 * th:2 * th + 2, 256 * nb:256 * nb + 256],
                             OUTB[i % 4]).then_inc(out_stored[i % 4], 16)
            for s in out_stored:
                sp.wait_ge(s, 32)

        @block.scalar
        def _(act):
            A = nc.scalar.activation
            own = Steps(act, act_steps)
            eps, gn_eps, eps64 = [con("eps")[:, i:i + 1] for i in range(3)]
            act.wait_ge(consts_here, 32)
            act.wait_ge(x_here, 16)
            for t in range(NT):
                own.did(A(XI[0][:, 2 * t:2 * t + 2, :], V[:, t, :].rearrange("p (a b) -> p a b", a=2), ACT.Square,
                          accum_out=ssq[:, t:t + 1]))
            own.wait()
            A(rstd, ssq, ACT.Sqrt, bias=eps, scale=1.0 / D).then_inc(x_squared, 1)
            act.wait_ge(vectors_ready, 1)
            A(SILT[:, 0:16], VECS[:, VEC["c"]:VEC["c"] + 16], ACT.Tanh, scale=0.5).then_inc(c_tanh, 1)
            for c in range(KT):
                o = arrived(act, ("hT", c))
                free(A(HT[:, c, 1:T + 1], o[:, :], ACT.Copy, scale=vec("norm", c)), ("hT", c))
            free(A(LOW[:, 0, :], arrived(act, ("low", 0))[0:64, :], ACT.Tanh), ("low", 0))
            free(A(LOW[:, 1, :], arrived(act, ("low", 1))[0:64, :], ACT.Copy), ("low", 1))
            for c in range(KT):
                free(A(KB[:, c, :], arrived(act, ("k", c))[:, :], ACT.Copy), ("k", c))

            def square_k(c):
                act.wait_ge(k_scaled, c + 1)
                if c >= 2:
                    arrived(act, ("kss", c - 2))
                A(SQ2[c % 2], AR[:, 0, c, :], ACT.Square).then_inc(k_squared, 1)

            square_k(0)
            for c in range(KT):
                if c + 1 < KT:
                    square_k(c + 1)
                free(A(AR[:, 1, c, :], arrived(act, ("r", c))[:, :], ACT.Copy), ("r", c))
                o = arrived(act, ("kss", c))
                if c >= 2:
                    act.wait_ge(kk_done, c - 1)
                free(A(ROOT[c % 2], o[:, :], ACT.Sqrt), ("kss", c))
            def copy_l(q):
                for i in range(4):
                    k, (c, h) = 4 * q + i, (2 * q + i // 2, i % 2)
                    o = arrived(act, ("lt", c, h))
                    if k >= 2:
                        act.wait_ge(lt_out[k % 2], 16 * (k // 2))
                    free(A(LTS[k % 2], o[:, :], ACT.Copy), ("lt", c, h))
                    stored(act, ("lt", c, h))
                    dst = bass.AP(lt_dram.tensor, k * NT * P * (P + 1), [[P, P], [P * (P + 1), NT], [1, P]])
                    act.dma_start(dst, LTS[k % 2].rearrange("p (j t) -> p j t", j=NT)).then_inc(lt_out[k % 2], 16)

            def fetch_blocks(q):
                for i in range(2):
                    act.wait_ge(lt_out[i], 32 * (q + 1))
                if q:
                    act.wait_ge(inverted, q)
                src = bass.AP(lt_dram.tensor, q * UNITS * P * (P + 1), [[BLK * (P + 1), P], [P, BLK], [1, BLK]])
                act.dma_start(LTB, src).then_inc(lt_back, 16)

            def store_inverse(q):
                act.wait_ge(inverted, q + 1)
                dst = bass.AP(inv_dram.tensor, q * 2 * P * BLK * BLK, [[BLK * BLK, P], [P * BLK * BLK, 2], [1, BLK * BLK]])
                act.dma_start(dst, XO.rearrange("p s a b -> p s (a b)")).then_inc(inv_out, 16)

            def fetch_inverse(q):
                act.wait_ge(inv_out, 16 * (q + 1))
                for s in range(2):
                    src = bass.AP(inv_dram.tensor, (2 * q + s) * P * BLK * BLK, [[BLK, P], [P * BLK, UNITS], [1, BLK]])
                    act.dma_start(XST[:, q, s], src).then_inc(inv_back[q], 16)

            for c in range(KT):
                o = arrived(act, ("w", c))
                if c:
                    act.wait_ge(csum_ready, c)
                free(A(SIGW, o[:, :], ACT.Tanh, scale=0.5, bias=half_vec("w0", c)), ("w", c))
                free(A(AB[:, c, :], arrived(act, ("a", c))[:, :], ACT.Tanh, scale=0.5, bias=half_vec("a0", c)), ("a", c))
                act.wait_ge(csum_ready, c + 1)
                if c:
                    act.wait_ge(kappa_ready, c)
                csum = CSUM.rearrange("p (j t) -> p j t", j=4)
                A(E1[:, :, 1:P + 1], csum, ACT.Exp, scale=-KAPPA)
                A(E2, CSUM, ACT.Exp, scale=KAPPA)
                A(E1[:, :, 0], MID[:, 0:4], ACT.Exp, scale=KAPPA)
                A(MID[:, 4:8], MID[:, 0:4], ACT.Exp, scale=-KAPPA).then_inc(decays_ready, 1)
                for h in range(2):
                    if c < 4:
                        o = arrived(act, ("v", c, h))
                        free(A(V[:, 2 * h:2 * h + 2, c * 256:(c + 1) * 256], o.rearrange("p (i n) -> p i n", i=2),
                               ACT.Copy), ("v", c, h))
                    else:
                        cc = 2 * (c - 4) + h
                        o = arrived(act, ("g", cc))
                        if cc >= 2:
                            stored(act, ("g", cc - 2))
                        A(SQ2[cc % 2], o[:, :], ACT.Tanh, scale=0.5).then_inc(gate_tanh, 1)
                if c >= 7:
                    fetch_inverse(c - 7)
                if c >= 6:
                    store_inverse(c - 6)
                if c >= 5:
                    fetch_blocks(c - 5)
                if c >= 4:
                    copy_l(c - 4)
            A(CST[:, 0:1], CST[:, 4:5], ACT.Copy).then_inc(act_phase, 1)
            fetch_inverse(1)
            store_inverse(2)
            fetch_blocks(3)
            fetch_inverse(2)
            others_done(act, 1, act_phase)
            arrived(act, "bonus")

            def copy_turned(g):
                free(A(BK[:, g % 3, :, :], arrived(act, ("turn", g)).rearrange("p (q n) -> p q n", q=2), ACT.Copy),
                     ("turn", g))

            def copy_rhs(g, q):
                act.wait_ge(rhs_ready[q], g + 1)
                A(RH[:, q, :], banks[6 + q][:, 0:P], ACT.Copy).then_inc(rhs_copied[q], 1)

            def copy_sa(g, q):
                act.wait_ge(sa_ready[q], g + 1)
                A(SA[:, q, :], banks[6 + q][:, P:2 * P], ACT.Copy).then_inc(sa_copied[q], 1)

            def copy_y(g, q):
                j, cc = divmod(g, 4)
                c = 2 * cc + q
                act.wait_ge(ys_ready[q], g + 1)
                if j < NT - 1:
                    act.wait_ge(s_updated[q], g + 1)
                A(YT[j][:, c * P:(c + 1) * P], banks[6 + q][:, 2 * P:3 * P], ACT.Copy).then_inc(y_copied[q], 1)

            def take_y(j, h):
                o = arrived(act, ("yT", j, h))
                for i in range(4):
                    c = 4 * h + i
                    ins = A(YG[j][:, c, :], o[:, i * P:(i + 1) * P], ACT.Identity, bias=vec("gn_b", c),
                            scale=vec("gn_w", c))
                free(ins, ("yT", j, h))

            copy_turned(0)
            for g in range(GROUPS + 4):
                nxt, old = g + 1 < GROUPS, 0 < g <= GROUPS
                turning = g in (8, 12, 16)
                if old:
                    for q in range(2):
                        copy_rhs(g - 1, q)
                mod = g - 1 if 1 <= g <= 12 else None
                if mod is not None:
                    act.wait_ge(mods_block, mod + 1)
                    A(MROW, banks[2][0:2, 0:256], ACT.Copy).then_inc(mods_copied, 1)
                if old:
                    for q in range(2):
                        copy_sa(g - 1, q)
                if turning:
                    take_y(g // 4 - 2, 0)
                if old:
                    for q in range(2):
                        copy_y(g - 1, q)
                if nxt:
                    copy_turned(g + 1)
                if turning:
                    take_y(g // 4 - 2, 1)
                j = g // 4 - 1
                if g >= 5 and g % 4 == 1:
                    act.wait_ge(centred, j + 1)
                    if j:
                        act.wait_ge(gn_sums, j)
                    A(SQ, YT[j], ACT.Square).then_inc(gn_squared, 1)
                if g >= 6 and g % 4 == 2:
                    act.wait_ge(gn_sums, j + 1)
                    A(GST[:, 128 + 16 * j:144 + 16 * j], GST[:, 64 + 16 * j:80 + 16 * j], ACT.Sqrt, bias=gn_eps,
                      scale=1.0 / HD).then_inc(gn_root, 1)
                if g == 0:
                    store_inverse(3)
                if g == 1:
                    fetch_inverse(3)
            take_y(3, 0)
            take_y(3, 1)
            act.wait_ge(ctx_here, 16)
            for t in range(2):
                own.own(A(CNJ, CX[:, t, :], ACT.Square, accum_out=SUMS[:, t:t + 1]))
            A(SUMS[:, 2:4], SUMS[:, 0:2], ACT.Sqrt, bias=eps, scale=1.0 / D).then_inc(cn_root, 1)

            def square_x1(t):
                for h in range(2):
                    stored(act, ("o", t, h))
                own.own(A(XN[:, t, :], X1[:, t, :], ACT.Square, accum_out=ssq[:, t:t + 1]))
                A(rstd[:, t:t + 1], ssq[:, t:t + 1], ACT.Sqrt, bias=eps, scale=1.0 / D).then_inc(n2_root, 1)

            def take_x1(t):
                for h in range(2):
                    o = arrived(act, ("xT", t, h))
                    for i in range(4):
                        c = 4 * h + i
                        dst = XNP[:, c, HD:HD + T].rearrange("p (col r) -> p r col", r=GH)[:, 2 * t:2 * t + 2, :]
                        ins = A(dst, o[:, i * P:(i + 1) * P].rearrange("p (r col) -> p r col", r=2), ACT.Identity,
                                bias=MODS[:, c, 0:1], scale=GSC[:, c, 0:1])
                    free(ins, ("xT", t, h))

            act.wait_ge(mods_ready, 1)
            square_x1(0)
            for h in range(4):
                o = arrived(act, ("cT", h))
                for i in range(2):
                    c = 2 * h + i
                    ins = A(CNT[:, c, :], o[:, i * 256:(i + 1) * 256], ACT.Identity, bias=MODS[:, c, 1:2],
                            scale=GSC[:, c, 1:2])
                free(ins, ("cT", h))
            square_x1(1)
            square_x1(2)
            take_x1(0)
            square_x1(3)
            take_x1(1)

            def root(i):
                n = CTX if ITEMS[i][0] == "ck" else T
                o = arrived(act, ("ss", i))
                if i >= 2:
                    act.wait_ge(qk_done, i - 1)
                q = ITEMS[i][0] == "q"
                free(A(DROOT[i % 2][:, 0:n], o[:, 0:n], ACT.Sqrt, bias=eps64 if q else eps,
                       scale=1.0 if q else 1.0 / HD), ("ss", i))

            for i, key in enumerate(ITEMS):
                if i in (2, 4):
                    take_x1(1 + i // 2)
                n = CTX if key[0] == "ck" else T
                o = arrived(act, key)
                if i >= 2:
                    arrived(act, ("ss", i - 2))
                A(DTMP[i % 2][:, 0:n], o[:, 0:n], ACT.Square).then_inc(qk_squared, 1)
                if i:
                    root(i - 1)
            root(len(ITEMS) - 1)
            for nb in range(2):
                for b4 in range(4):
                    o = arrived(act, ("vv", nb, b4)).rearrange("p (i n) -> p i n", i=2)
                    w = 2 if b4 < 3 else 1
                    free(A(VP[:, 2 * b4:2 * b4 + w, nb * 256:(nb + 1) * 256], o[:, 0:w, :], ACT.Copy), ("vv", nb, b4))
            for c in range(4):
                free(A(UT[:, c, :], arrived(act, ("f", c))[:, :], ACT.Copy), ("f", c))
            for c in range(8):
                A(GATE[:, c, :], arrived(act, ("g2", c))[:, :], ACT.Tanh, scale=0.5).then_inc(gate2_tanh, 1)
            for t in range(NT):
                for gp in range(2):
                    o = arrived(act, ("uc", t, gp)).rearrange("p (g s n) -> p g s n", g=2, s=2)
                    dst = UC[:, t, :, gp * 256:(gp + 1) * 256].rearrange("p s (g n) -> p g s n", g=2)
                    free(A(dst, o, ACT.Copy), ("uc", t, gp))
            for g in range(4):
                free(A(YF[:, g, :], arrived(act, ("yf", g))[:, :], ACT.Copy), ("yf", g))
            for n in range(NT * NAH):
                act.wait_ge(masked, n + 1)
                nm = MXN2[:, n % 4:n % 4 + 1]
                A(PB[n % 4][:, 0:WIN], PB[n % 4][:, 0:WIN], ACT.Exp, bias=nm, accum_out=SUMS[:, 8 + n:9 + n])
                free(A(PB[n % 4][:, WIN:512], banks[where["s", n][0]][:, WIN:512], ACT.Exp, bias=nm,
                       accum_out=SUMS[:, 40 + n:41 + n]), ("s", n))

        @block.vector
        def _(dve):
            TT, TS, STT = nc.vector.tensor_tensor, nc.vector.tensor_scalar, nc.vector.scalar_tensor_tensor
            own = Steps(dve, dve_steps)
            own.did(nc.vector.memset(CST, 0.0))
            own.did(nc.vector.memset(HT[:, :, 0:1], 0.0))
            dve.wait_ge(consts_here, 32)
            own.did(TS(HVEC, VECS[:, VEC["w0"]:VEC["w0"] + 2 * KT], 0.5, None, MUL))
            own.did(TS(NKA, VECS[:, VEC["k_a"]:VEC["k_a"] + KT], -1.0, 1.0, MUL, ADD))
            TT(RKB, VECS[:, VEC["r_k"]:VEC["r_k"] + KT].unsqueeze(2).broadcast_to([P, KT, 2]),
               heads1[:, 0:P:HD].unsqueeze(1).broadcast_to([P, KT, 2]), MUL).then_inc(vectors_ready, 1)
            dve.wait_ge(x_squared, 1)
            own.own(nc.vector.reciprocal(rstd, rstd))
            dve.wait_ge(x_here, 16)
            for t in range(NT):
                TS(V[:, t, :], V[:, t, :], rstd[:, t:t + 1], None, MUL).then_inc(x_scaled, 1)
            dve.wait_ge(c_tanh, 1)
            own.own(TS(SILT[:, 16:32], SILT[:, 0:16], 0.5, 0.5, MUL, ADD))
            own.did(TT(SILC.rearrange("p c k -> p k c"), SILT[:, 16:32].rearrange("p (k c) -> p k c", k=2),
                       VECS[:, VEC["c"]:VEC["c"] + 16].rearrange("p (k c) -> p k c", k=2), MUL))
            for c in range(KT):
                stored(dve, ("hT", c))
                own.did(TT(DX[:, c, :], HT[:, c, 0:T], HT[:, c, 1:T + 1], SUB))
            own.wait()

            def mix(m):
                if m >= 2:
                    arrived(dve, last_of_mix[m - 2])
                for c in range(KT):
                    STT(XI[m % 2][:, c, :], DX[:, c, :], vec("mu_" + "wakrvg"[m], c), HT[:, c, 1:T + 1], MUL, ADD)\
                        .then_inc(mixed, 1)

            for m in range(4):
                mix(m)
            for c in range(KT):
                stored(dve, ("k", c))
                TS(AR[:, 0, c, :], KB[:, c, :], vec("k_k", c), None, MUL).then_inc(k_scaled, 1)
            mix(4)
            for c in range(KT):
                stored(dve, ("kss", c))
                own.own(TS(ROOT[c % 2], ROOT[c % 2], 1e-12, None, MAX))
                own.own(nc.vector.reciprocal(ROOT[c % 2], ROOT[c % 2]))
                TT(AR[:, 0, c, :], AR[:, 0, c, :], ROOT[c % 2], MUL).then_inc(kk_done, 1)
            mix(5)

            def gate(cc):
                dve.wait_ge(gate_tanh, cc + 1)
                free(STT(GT[:, cc, :], SQ2[cc % 2], 1.0, arrived(dve, ("g", cc))[:, :], ADD, MUL), ("g", cc))

            def solve(q):
                if q:
                    dve.wait_ge(inv_out, 16 * q)
                own.own(nc.vector.memset(XO[:, 0], 0.0))
                own.did(nc.vector.memset(XO[:, 0].rearrange("p a b -> p (a b)")[:, 0:BLK * BLK:BLK + 1], 1.0))
                dve.wait_ge(lt_back, 16 * (q + 1))
                own.wait()
                for i in range(1, BLK):
                    tmp = XTMP[:, 0:i * i].rearrange("p (k j) -> p k j", k=i)
                    own.own(TT(tmp, XO[:, 0, 0:i, 0:i].rearrange("p j k -> p k j"),
                               LTB[:, 0:i, i].unsqueeze(1).broadcast_to([P, i, i]), MUL))
                    own.own(nc.vector.tensor_reduce(XO[:, 0, i, 0:i], tmp, AX.X, ADD))
                nc.vector.tensor_copy(XO[:, 1], XO[:, 0].rearrange("p a b -> p b a")).then_inc(inverted, 1)

            dve.wait_ge(mixed, KT * 6)
            dve.wait_ge(kk_done, KT)
            for c in range(KT):
                stored(dve, ("w", c))
                own.own(TS(SIGW, SIGW, 0.5, 0.5, MUL, ADD))
                for j in range(4):
                    at = slice(j * P, (j + 1) * P)
                    own.did(nc.vector.tensor_tensor_scan(CSUM[:, at], con("ones"), SIGW[:, at], 0.0, MUL, ADD))
                own.wait()
                csum = CSUM.rearrange("p (j t) -> p j t", j=4)
                if c:
                    dve.wait_ge(decays_ready, c)
                own.own(nc.vector.tensor_copy(MID[:, 0:4], csum[:, :, HD - 1]))
                TT(csum, csum, MID[:, 0:4].unsqueeze(2).broadcast_to([P, 4, P]), SUB).then_inc(csum_ready, 1)
                stored(dve, ("a", c))
                TS(AB[:, c, :], AB[:, c, :], 0.5, 0.5, MUL, ADD).then_inc(a_ready, 1)
                dve.wait_ge(a_ready, c + 1)
                dve.wait_ge(kmod_ready, c + 1)
                own.own(TT(AB[:, c, :], AB[:, c, :], AR[:, 0, c, :], MUL))
                dve.wait_ge(decays_ready, c + 1)
                own.did(TT(AB[:, c, :], AB[:, c, :], E2, MUL))
                a4 = AR[:, 0, c, :].rearrange("p (j t) -> p j t", j=4)
                own.did(STT(a4, a4, -1.0, E1[:, :, 0:P], MUL, MUL))
                own.did(TT(F[:, c, 0:3], E1[:, 0:3, P], MID[:, 5:8], MUL))
                dve.wait_ge(rk_ready, c + 1)
                r4 = AR[:, 1, c, :].rearrange("p (j t) -> p j t", j=4)
                TT(r4, r4, E1[:, :, 1:P + 1], MUL).then_inc(ab_ready, 1)
                if c >= 4:
                    gate(2 * (c - 4))
                    gate(2 * (c - 4) + 1)
                if c >= 5:
                    solve(c - 5)
            free(nc.vector.tensor_copy(BON, arrived(dve, "bonus")[:, 0:64]), "bonus")
            nc.vector.tensor_copy(CST[:, 1:2], CST[:, 5:6]).then_inc(dve_phase, 1)
            others_done(dve, 1, dve_phase)

            def mask_gram(g, u):
                o = arrived(dve, ("gram", g, u)).rearrange("p (s n) -> p s n", s=2)
                free(TT(GM[g % 3][:, u, :].rearrange("p (s n) -> p s n", s=2), o,
                        gram_mask.unsqueeze(1).broadcast_to([P, 2, 2 * P]), MUL), ("gram", g, u))

            def mask_z(g, l, hf):
                dve.wait_ge(z_ready[hf], LEVELS * g + l + 1)
                b = BLK << l
                m = con("level")[:, l * HD:(l + 1) * HD].rearrange("p (m b) -> p m b", b=b)
                z = halves2(banks[hf][:, 0:2 * P].rearrange("p (u n) -> p u n", u=2), b, 0)
                TT(halves2(YL[:, l, 2 * hf:2 * hf + 2, :], b, 0), z, m.unsqueeze(1).broadcast_to([P, 2, HD // b, b]),
                   MUL).then_inc(y_ready[hf], 1)

            def add_x(g, l, hf):
                dve.wait_ge(x_grown[hf], LEVELS * g + l + 1)
                b = BLK << l
                for w in range(0 if l < LEVELS - 1 else 1, 2):
                    x = halves2(XS[:, g % 2, 2 * hf:2 * hf + 2, w, :], b, w)
                    ins = TT(x, x, corner(hf, w).rearrange("p u (m b) -> p u m b", b=b), ADD)
                ins.then_inc(x_added[hf], 1)

            def update(g, q):
                j, cc = divmod(g, 4)
                c = 2 * cc + q
                if j == NT - 1:
                    return
                dve.wait_ge(ys_ready[q], g + 1)
                s = banks[6 + q][:, 3 * P:4 * P]
                if j == 0:
                    STT(ST[:, c, :], s, F[:, c, j:j + 1], heads1, MUL, MUL).then_inc(s_updated[q], 1)
                else:
                    own.own(STT(STMP[:, q, :], s, F[:, c, j:j + 1], heads1, MUL, MUL))
                    STT(ST[:, c, :], ST[:, c, :], F[:, c, j:j + 1], STMP[:, q, :], MUL, ADD).then_inc(s_updated[q], 1)

            arrived(dve, "bonus")
            for u in range(4):
                mask_gram(0, u)
            dve.wait_ge(y_zeroed, 1)
            def centre(j):
                for q in range(2):
                    dve.wait_ge(y_copied[q], 4 * (j + 1))
                own.own(nc.vector.tensor_reduce(stat(0, j), heads_of(YT[j]), AX.X, ADD))
                own.own(TS(stat(0, j), stat(0, j), 1.0 / HD, None, MUL))
                TT(heads_of(YT[j]), heads_of(YT[j]), bc(stat(0, j)), SUB).then_inc(centred, 1)

            def finish_y(j, h):
                stored(dve, ("yT", j, h))
                o = arrived(dve, ("bT", j, h))
                y = YG[j][:, 4 * h:4 * h + 4, :]
                free(TT(y, y, o.rearrange("p (c n) -> p c n", c=4), ADD), ("bT", j, h))
                stored(dve, ("bT", j, h))
                STT(y, y, 0.5, GT[:, 4 * h:4 * h + 4, j * P:(j + 1) * P], MUL, MUL).then_inc(y_gated, 1)

            def take_mods():
                o = arrived(dve, "mods")
                b2 = VECS[:, VEC["b_shift"]:VEC["b_shift"] + 24].unsqueeze(2).broadcast_to([P, 24, 2])
                free(TT(MODS, o[:, 256:304].rearrange("p (c k) -> p c k", k=2), b2, ADD), "mods")
                stored(dve, "mods")
                own.own(TS(GSC, MODS[:, 8:16, :], 1.0, None, ADD))
                TT(GSC, GSC, VECS[:, VEC["norm2"]:VEC["norm2"] + 8].unsqueeze(2).broadcast_to([P, 8, 2]), MUL)\
                    .then_inc(mods_ready, 1)

            stat = lambda i, j: GST[:, 64 * i + 16 * j:64 * i + 16 * j + 16]
            bc = lambda a: a.unsqueeze(2).broadcast_to([P, HEADS, HD])
            heads_of = lambda a: a.rearrange("p (h n) -> p h n", n=HD)
            for g in range(GROUPS + 4):
                now, nxt, old = g < GROUPS, g + 1 < GROUPS, 0 < g <= GROUPS
                turning = g in (8, 12, 16)
                for l in range(LEVELS):
                    if now:
                        mask_z(g, l, 0)
                        mask_z(g, l, 1)
                    if nxt:
                        mask_gram(g + 1, l)
                    if now:
                        add_x(g, l, 0)
                        add_x(g, l, 1)
                    if old and l == 1:
                        update(g - 1, 0)
                    if nxt and l == 1:
                        mask_gram(g + 1, 3)
                    if turning and l == 1:
                        finish_y(g // 4 - 2, 0)
                    if old and l == 2:
                        update(g - 1, 1)
                if turning:
                    finish_y(g // 4 - 2, 1)
                j = g // 4 - 1
                if g >= 5 and g % 4 == 1:
                    centre(j)
                if g >= 6 and g % 4 == 2:
                    dve.wait_ge(gn_squared, j + 1)
                    nc.vector.tensor_reduce(stat(1, j), heads_of(SQ), AX.X, ADD).then_inc(gn_sums, 1)
                if g >= 7 and g % 4 == 3:
                    dve.wait_ge(gn_root, j + 1)
                    own.own(nc.vector.reciprocal(stat(2, j), stat(2, j)))
                    TT(heads_of(YT[j]), heads_of(YT[j]), bc(stat(2, j)), MUL).then_inc(y_normed, 1)
                if g == 0:
                    solve(BATCHES - 1)
                if g == 13:
                    take_mods()
            dve.wait_ge(x_again, 16)

            def make_x1(t, h):
                at = slice(512 * h, 512 * h + 512)
                free(TT(X1[:, t, at], arrived(dve, ("o", t, h))[:, :], XR[:, t, at], ADD), ("o", t, h))

            for t in range(3):
                make_x1(t, 0)
            finish_y(3, 0)
            finish_y(3, 1)
            make_x1(3, 0)
            dve.wait_ge(cn_root, 1)
            own.own(nc.vector.reciprocal(SUMS[:, 2:4], SUMS[:, 2:4]))
            for t in range(2):
                TS(CX[:, t, :], CX[:, t, :], SUMS[:, 2 + t:3 + t], None, MUL).then_inc(cn_ready, 1)

            def norm_x1(t):
                dve.wait_ge(n2_root, t + 1)
                own.own(nc.vector.reciprocal(rstd[:, t:t + 1], rstd[:, t:t + 1]))
                TS(XN[:, t, :], X1[:, t, :], rstd[:, t:t + 1], None, MUL).then_inc(xn_ready, 1)

            make_x1(0, 1)
            for t in range(1, NT):
                make_x1(t, 1)
                norm_x1(t - 1)
            norm_x1(NT - 1)

            def head_dst(i):
                name, c = ITEMS[i]
                return {"q": QT[:, c, :], "kk": KTP[:, c, HD:HD + T], "ck": CK[:, c, :]}[name]

            def scale_heads(i):
                n = CTX if ITEMS[i][0] == "ck" else T
                stored(dve, ("ss", i))
                r = DROOT[i % 2][:, 0:n]
                own.own(nc.vector.reciprocal(r, r))
                stored(dve, ITEMS[i])
                TT(head_dst(i), head_dst(i), r, MUL).then_inc(qk_done, 1)

            for i, key in enumerate(ITEMS):
                n = CTX if key[0] == "ck" else T
                dve.wait_ge(qk_squared, i + 1)
                g = VECS[:, VEC["q_gain"]:VEC["q_gain"] + 1] if key[0] == "q" else \
                    VECS[:, VEC["k_gain"]:VEC["k_gain"] + 1]
                free(TS(head_dst(i), arrived(dve, key)[:, 0:n], g, None, MUL), key)
                if i:
                    scale_heads(i - 1)
            scale_heads(len(ITEMS) - 1)
            for c in range(8):
                dve.wait_ge(gate2_tanh, c + 1)
                free(STT(GATE[:, c, :], GATE[:, c, :], 1.0, arrived(dve, ("g2", c))[:, :], ADD, MUL), ("g2", c))
            arrived(dve, ("yf", 3))
            for h in range(2):
                TT(GDIAG[h].rearrange("p (c n) -> p c n", c=4), ident.unsqueeze(1).broadcast_to([P, 4, P]),
                   MODS[:, 16 + 4 * h:20 + 4 * h, 0:1].broadcast_to([P, 4, P]), MUL).then_inc(gdiag_ready, 1)
            for n in range(4):
                stored(dve, ("g2", n))
                o = arrived(dve, ("fo", n)).rearrange("p (col r) -> p col r", r=GH)
                free(STT(MIX[:, n, :].rearrange("p (r col) -> p col r", r=GH), o, 0.5,
                         GATE[:, n, :].rearrange("p (col r) -> p col r", r=GH), MUL, MUL), ("fo", n))
            for h in range(2):
                free(nc.vector.tensor_copy(GX[:, 512 * h:512 * h + 512], arrived(dve, ("gx", h))[:, :]), ("gx", h))

            def mask_scores(n):
                qt, h = divmod(n, NAH)
                o = arrived(dve, ("s", n))
                if n >= 4:
                    arrived(dve, ("pt", n - 4))
                if n >= 4:
                    stored(dve, ("s", n - 4))
                m = MXN[:, 2 * (n % 4):2 * (n % 4) + 1]
                m2 = MXN[:, 2 * (n % 4) + 1:2 * (n % 4) + 2]
                own.own(nc.vector.tensor_reduce(m, o[:, WIN:512], AX.X, MAX))
                own.own(nc.vector.tensor_tensor_reduce(
                    out=PB[n % 4][:, 0:WIN], in0=o[:, 0:WIN], in1=BM[:, (0, 1, 1, 2)[qt], h, :], scale=1.0, scalar=m,
                    op0=ADD, op1=MAX, accum_out=m2))
                TS(MXN2[:, n % 4:n % 4 + 1], m2, -1.0, None, MUL).then_inc(masked, 1)

            def copy_turned_probs(n):
                o = arrived(dve, ("pt", n))
                if n >= 3:
                    k = n - 3
                    if k % NAH == NAH - 1:
                        arrived(dve, ("at", k // NAH))
                    else:
                        dve.wait_ge(pv_done, (k // NAH) * (NAH - 1) + k % NAH + 1)
                free(nc.vector.tensor_copy(PT[n % 3], o[:, :]), ("pt", n))

            def scale_out(qt):
                s1, s2 = SUMS[:, 8 + 8 * qt:16 + 8 * qt], SUMS[:, 40 + 8 * qt:48 + 8 * qt]
                own.own(TT(s1, s1, s2, ADD))
                own.own(nc.vector.reciprocal(s1, s1))
                o = arrived(dve, ("at", qt)).rearrange("p (h n) -> p h n", h=NAH)
                if qt:
                    arrived(dve, ("oT", qt - 1))
                free(TT(ON.rearrange("p (h n) -> p h n", h=NAH), o, s1.unsqueeze(2).broadcast_to([P, NAH, HD]), MUL),
                     ("at", qt))

            def gate_out(qt):
                o = arrived(dve, ("oT", qt)).rearrange("p (c col r) -> p c col r", c=4, r=GH)
                g = GATE[:, 4:8, qt * P:(qt + 1) * P].rearrange("p c (col r) -> p c col r", r=GH)
                dst = MIX[:, 4:8, :].rearrange("p c (r col) -> p c col r", r=GH)[:, :, 16 * qt:16 * qt + 16, :]
                for i in range(4):
                    ins = STT(dst[:, i], o[:, i], 0.5, g[:, i], MUL, MUL)
                    if i < 3:
                        own.did(ins)
                free(ins, ("oT", qt))

            dve.wait_ge(bm_ready, 1)
            NU = NT * NAH
            for n in range(NU + 7):
                if n < NU:
                    mask_scores(n)
                if 2 <= n < NU + 2:
                    copy_turned_probs(n - 2)
                if n >= NAH + 3 and (n - NAH - 3) % NAH == 0:
                    scale_out((n - NAH - 3) // NAH)
                if n >= NAH + 6 and (n - NAH - 6) % NAH == 0:
                    gate_out((n - NAH - 6) // NAH)
            for i in range(8):
                nb, th = divmod(i, 2)
                o = arrived(dve, ("z", nb, th)).rearrange("p (j n) -> p j n", j=2)
                if i >= 4:
                    dve.wait_ge(out_stored[i % 4], 16)
                free(TT(OUTB[i % 4], o, GX[:, nb * 256:(nb + 1) * 256].unsqueeze(1).broadcast_to([P, 2, 256]), MUL),
                     ("z", nb, th))

        @block.gpsimd
        def _(pool):
            TT, TS = nc.gpsimd.tensor_tensor, nc.gpsimd.tensor_scalar
            own = Steps(pool, pool_steps)
            pool.wait_ge(vectors_ready, 1)
            for c in range(KT):
                pool.wait_ge(a_ready, c + 1)
                TS(KMOD, AB[:, c, :], vec("k_a", c), NKA[:, c:c + 1], MUL, ADD).then_inc(kmod_ready, 1)
                pool.wait_ge(kmod_ready, c + 1)
                stored(pool, ("k", c))
                own.own(TT(KB[:, c, :], KB[:, c, :], KMOD, MUL))
                stored(pool, ("r", c))
                if c:
                    pool.wait_ge(bonus_done, c)
                TT(RKT, KB[:, c, :], AR[:, 1, c, :], MUL).then_inc(rk_ready, 1)
                pool.wait_ge(decays_ready, c + 1)
                pool.wait_ge(rk_ready, c + 1)
                TT(KB[:, c, :], KB[:, c, :], E2, MUL).then_inc(kappa_ready, 1)
            pool.wait_ge(kappa_ready, KT)
            TT(CST[:, 3:4], CST[:, 6:7], CST[:, 6:7], ADD).then_inc(pool_phase, 1)
            others_done(pool, 1, pool_phase)
            arrived(pool, "bonus")
            nc.gpsimd.memset(YL, 0.0).then_inc(y_zeroed, 1)
            blocks = con("blocks").rearrange("p (m n) -> p m n", n=BLK).unsqueeze(1).broadcast_to([P, 2, P // BLK, BLK])

            def expand(g):
                j, cc = divmod(g, 4)
                if g < BATCHES:
                    pool.wait_ge(inv_back[cc], 32)
                if g >= 2:
                    for q in range(2):
                        pool.wait_ge(sa_ready[q], g - 1)
                for u in range(4):
                    ins = TT(XS[:, g % 2, u].rearrange("p s (m n) -> p s m n", n=BLK),
                             XST[:, cc, :, u * NT + j, :].unsqueeze(2).broadcast_to([P, 2, P // BLK, BLK]), blocks, MUL)
                ins.then_inc(expanded, 1)

            def bonus_v(j):
                for q in range(2):
                    pool.wait_ge(ys_ready[q], 4 * (j + 1))
                v = V[:, j, :].rearrange("p (h n) -> p h n", n=HD)
                TT(v, v, BON[:, 16 * j:16 * j + 16].unsqueeze(2).broadcast_to([P, HEADS, HD]), MUL).then_inc(bv_ready, 1)

            for g in range(GROUPS):
                expand(g)
                if g >= 6 and g % 4 == 2:
                    bonus_v(g // 4 - 1)
            bonus_v(NT - 1)
            own.did(nc.gpsimd.memset(XNP[:, :, 0:HD], 0.0))
            own.did(nc.gpsimd.memset(XNP[:, :, HD + T:PADT], 0.0))
            stored(pool, ("o", 3, 1))
            own.did(nc.gpsimd.memset(KTP[:, :, 0:HD], 0.0))
            nc.gpsimd.memset(KTP[:, :, HD + T:PADT], 0.0).then_inc(pads_ready, 1)
            pool.wait_ge(rel_here, 16 * 17)
            near_v = NEAR.rearrange("p (v a b) -> p v a b", v=3, b=GH)
            for v in range(3):
                for h in range(NAH):
                    r = REL[:, h * RBW:h * RBW + 1]
                    bias = bass.AP(r.tensor, r.offset + 7 * 31, [list(r.ap[0]), [1, 32], [-31, GH]])
                    ins = TT(BM[:, v, h, :].rearrange("p (a b) -> p a b", b=GH), bias, near_v[:, v], ADD)
                    if (v, h) != (2, NAH - 1):
                        own.did(ins)
            ins.then_inc(bm_ready, 1)
            for i in range(8):
                nb, th = divmod(i, 2)
                stored(pool, ("z", nb, th))
                at = slice(nb * 256, (nb + 1) * 256)
                TT(OUTB[i % 4], OUTB[i % 4], X1[:, 2 * th:2 * th + 2, at], ADD).then_inc(out_ready, 1)


_OUT = (1, T, D)


def kernel(**inputs):
    import concourse.bacc as bacc
    from concourse.bass_utils import run_bass_kernel_spmd as run

    g = {k: np.ascontiguousarray(v) for k, v in inputs.items()}
    f = np.float32

    def rows(a):
        return a.reshape(-1, P).T

    mu = g["l0_mu"]
    parts = [rows(g["l0_norm"])] + [rows(mu[i]) for i in range(6)]
    parts += [rows(g["l0_" + n]) for n in ("w0", "a0", "k_k", "k_a", "r_k", "gn_w", "gn_b")]
    parts += [rows(g["c_2"]), rows(g["c_ctx_2"]), rows(g["norm_g_2"]), rows(g["b_ada_2"][0])]
    parts += [np.tile(g["q_norm_g_2"][0], 2)[:, None], np.tile(g["k_norm_g_2"][0], 2)[:, None]]
    consts, cos_t, nsin_t, near = shape_constants()
    arrays = {
        "x": g["x"][0], "vecs": np.concatenate(parts, 1), "consts": consts, "cos_t": cos_t, "nsin_t": nsin_t,
        "near": near,
        "w_in": g["l0_w_in"], "w_up": g["l0_w_up"], "a_up": g["l0_a_up"], "w_out": g["l0_w_out"],
        "ctx_x": g["ctx_2"][0], "w_ada": g["w_ada_2"][0],
        "w_in2": g["w_in_2"][0], "w_four": g["w_four_2"][0],
        "rel_bias": np.pad(g["rel_bias_2"][0][:, ::-1].reshape(NAH, RB), ((0, 0), (RBPAD, RBPAD))),
        "w_out2": g["w_out_2"][0],
    }
    arrays = {k: np.ascontiguousarray(v) for k, v in arrays.items()}
    nc = bacc.Bacc("TRN2", target_bir_lowering=False, num_devices=1)
    args = [nc.dram_tensor(k, v.shape, mybir.dt.from_np(v.dtype), kind="ExternalInput").ap()
            for k, v in arrays.items()]
    out = nc.dram_tensor("out", (T, D), mybir.dt.float32, kind="ExternalOutput").ap()
    lt_dram = nc.dram_tensor("lt_dram", (HEADS * NT * (P + 1), P), mybir.dt.float32, kind="Internal").ap()
    inv_dram = nc.dram_tensor("inv_dram", (BATCHES * 2 * P, BLK * BLK), mybir.dt.float32, kind="Internal").ap()
    rwkv_then_grid_block(nc, *args, out, lt_dram, inv_dram)
    r = run(nc, [arrays], core_ids=[0])
    return r.results[0]["out"].reshape(_OUT)
```

```python
import math
from contextlib import ExitStack

import numpy as np

import concourse.bass as bass
from concourse import mybir

T, D, P = 512, 1024, 128
KT, NT = D // P, T // P
PAIRS, HEADS, HD = 8, 16, 64
BLK = 16
LEVELS = 3
BATCHES, UNITS = 4, 16
GROUPS = NT * 4
CTX, NAH, GW, GH = 256, 8, 64, 8
WIN = 256
PADT = T + 2 * HD
KAPPA = math.exp(-0.5)
NORM_EPS, GN_EPS = 1e-6, 64e-5
RB = 15 * 31
RBW = 7 * 31 + 32
RBPAD = 8

CONST = {}
_at = 0
for _n, _w in [("ident", P), ("heads", P), ("gram", 2 * P), ("level", LEVELS * HD), ("ones", P), ("blocks", P),
               ("dft128", 2 * P), ("eps", 3)]:
    CONST[_n] = (_at, _w)
    _at += _w
CONST_W = _at
VEC = {n: KT * i for i, n in enumerate(
    ["norm", "mu_r", "mu_w", "mu_k", "mu_v", "mu_a", "mu_g", "w0", "a0", "k_k", "k_a", "r_k", "gn_w", "gn_b",
     "c", "c_ctx", "norm2", "b_shift", "b_scale",
     "b_gate"])}
VEC["q_gain"] = KT * len(VEC)
VEC["k_gain"] = VEC["q_gain"] + 1
VEC_W = VEC["k_gain"] + 1


def shape_constants():
    f = np.float32
    i, j = np.arange(P)[:, None], np.arange(P)[None, :]
    strict, incl = (i < j).astype(f), (i <= j).astype(f)
    c = np.zeros((P, CONST_W), f)

    def put(name, a):
        at, w = CONST[name]
        c[:, at:at + w] = a

    put("ident", np.eye(P, dtype=f))
    put("heads", (i // HD == j // HD).astype(f))
    put("gram", np.concatenate([strict, incl], 1))
    levels = []
    for l in range(LEVELS):
        b = BLK << l
        even = np.concatenate([np.arange(s, s + b) for s in range(0, P, 2 * b)])
        levels.append((i // b == even[None, :] // b + 1).astype(f))
    put("level", np.concatenate(levels, 1))
    put("ones", 1.0)
    put("blocks", (i // BLK == j // BLK).astype(f))
    cl, key = np.arange(P)[:, None] // GH, np.arange(WIN)[None, :] // GH
    near = []
    for tile in (0, 1, 3):
        q, k = 16 * tile + cl, 16 * tile - 8 + key
        first = np.clip(q - 8, 0, GW - 16)
        near.append(np.where((k >= first) & (k < first + 16), 0.0, -1e30).astype(f))
    w = 2 * np.pi * ((i * j) % P) / P
    put("dft128", np.concatenate([np.cos(w), np.sin(w)], 1) / 256.0)
    put("eps", np.array([[NORM_EPS, GN_EPS, HD * NORM_EPS]], f))
    order = np.array([r * GW + col for col in range(GW) for r in range(GH)])
    w = 2 * np.pi * ((order[:, None] * order[None, :]) % T) / T
    return c, np.cos(w).astype(f), (-np.sin(w)).astype(f), np.concatenate(near, 1)


def rwkv_then_grid_block(nc, x, vecs, consts, cos_t, nsin_t, near, w_in, w_up, a_up, w_out,
                         ctx_x, w_ada, w_in2, w_four, rel_bias, w_out2, out, lt_dram, inv_dram):
    f32, f32r = mybir.dt.float32, mybir.dt.float32r
    ALU, ACT, AX = mybir.AluOpType, mybir.ActivationFunctionType, mybir.AxisListType
    MUL, ADD, SUB, MAX = ALU.mult, ALU.add, ALU.subtract, ALU.max

    stack = ExitStack()
    with stack:
        def sem(name):
            return stack.enter_context(nc.semaphore(name))

        END, SMALL_W = 53208, 604
        arena_byte = (nc.sbuf_base + 31) // 32 * 32
        arena = stack.enter_context(nc.sbuf_tensor("arena", [P, END], f32))
        banks = [stack.enter_context(nc.psum_tensor(f"bank{b}", [P, 512], f32)) for b in range(8)]

        class Room:
            def __init__(self, at, end):
                self.at, self.end = at, end

            def take(self, width, parts=P):
                at = self.at
                self.at += width
                assert self.at <= self.end, (self.at, self.end)
                return arena[0:parts, at:at + width]

        def rounded(name, at, width):
            return nc.alloc_sbuf_tensor_at(name, [P, width], f32r, offset=arena_byte + 4 * at)

        fixed = Room(0, END)
        wr_at = fixed.at
        WR = [fixed.take(2048) for _ in range(3)]
        WLO, WHI = [[rounded(f"w_{n}{i}", wr_at + 2048 * i + 1024 * h, 1024) for i in range(3)]
                    for h, n in enumerate(("lo", "hi"))]

        CON = fixed.take(CONST_W)
        VECS = fixed.take(VEC_W)
        MROW = fixed.take(256, 2)
        SMALL = fixed.take(SMALL_W)

        def con(name):
            at, w = CONST[name]
            return CON[:, at:at + w]

        def vec(name, c, n=1):
            return VECS[:, VEC[name] + c:VEC[name] + c + n]

        def half_vec(name, c, n=1):
            at = {"w0": 0, "a0": KT}[name] + c
            return HVEC[:, at:at + n]

        ident, heads1, gram_mask = con("ident"), con("heads"), con("gram")
        sm = Room(0, SMALL_W)

        def small(w):
            at = sm.at
            sm.at += w
            assert sm.at <= SMALL_W
            return SMALL[:, at:at + w]

        rstd = small(4)
        ssq = small(4)
        F = small(32).rearrange("p (c j) -> p c j", j=4)
        BON = small(64)
        RKB = small(16).rearrange("p (c h) -> p c h", h=2)
        MID = small(12)
        GST = small(64 * 3)
        SILC = small(16).rearrange("p (c k) -> p c k", k=2)
        SILT = small(32)
        MODS = small(48).rearrange("p (c k) -> p c k", k=2)
        GSC = small(16).rearrange("p (c k) -> p c k", k=2)
        CST = small(8)
        MXN = small(32)
        SUMS = small(80)
        HVEC = small(2 * KT)
        NKA = small(KT)
        MXN2 = small(4)

        base = (fixed.at + 7) // 8 * 8
        roomA = Room(base, END)
        AR = roomA.take(8192).rearrange("p (s c t) -> p s c t", s=2, c=KT)
        KB = roomA.take(4096).rearrange("p (c t) -> p c t", c=KT)
        ab_at = roomA.at
        AB = roomA.take(4096).rearrange("p (c t) -> p c t", c=KT)
        v_at = roomA.at
        V = roomA.take(4096).rearrange("p (t n) -> p t n", t=NT)
        ht_at = roomA.at
        HT_ = roomA.take(KT * 513)
        HT = HT_.rearrange("p (c t) -> p c t", c=KT)
        b0 = roomA.at
        DX = roomA.take(4096).rearrange("p (c t) -> p c t", c=KT)
        XI = [roomA.take(4096).rearrange("p (c t) -> p c t", c=KT) for _ in range(2)]
        GT = XI[1]
        as_mix = lambda at: arena[:, at:at + 4096].rearrange("p (c t) -> p c t", c=KT)
        MIXES = [AB, as_mix(v_at), XI[1], as_mix(v_at), XI[0], DX]
        XHI, XLO = [{m: [rounded(f"{n}{m}_{c}", at + c * T, T) for c in range(KT)] for m, at in places}
                    for n, places in (("x_hi", ((2, b0 + 4096), (3, ab_at), (5, ht_at))),
                                      ("x_lo", ((2, b0 + 8192), (3, v_at), (5, b0))))]
        nth_split = {2: 0, 3: 1, 5: 2}
        b1 = roomA.at
        LOW = roomA.take(1024, 64).rearrange("p (s t) -> p s t", s=2)
        UPS = roomA.take(2048, 64).rearrange("p (s n) -> p s n", s=2)
        SIGW, CSUM, E2, KMOD = [roomA.take(512) for _ in range(4)]
        SQ2 = [roomA.take(512) for _ in range(2)]
        root_b = roomA.take(516)
        ROOT = [roomA.take(512), root_b[:, 0:512]]
        E1 = root_b.rearrange("p (j t) -> p j t", j=4)
        RKT = ROOT[0]

        xi0 = b0 + 4096
        XST = arena[:, xi0:xi0 + 2048].rearrange("p (q s u n) -> p q s u n", q=BATCHES, s=2, u=UNITS)
        LTS = [arena[:, xi0 + 2048 + 512 * i:xi0 + 2560 + 512 * i] for i in range(2)]
        LTB = arena[:, xi0 + 3072:xi0 + 3328].rearrange("p (a b) -> p a b", a=BLK)
        XO = arena[:, xi0 + 3328:xi0 + 3840].rearrange("p (s a b) -> p s a b", s=2, a=BLK)
        XTMP = arena[:, xi0 + 3840:xi0 + 4096]
        SQ = arena[:, xi0 + 3072:xi0 + 4096]
        GM = [arena[:, at:at + 2048].rearrange("p (u n) -> p u n", u=4) for at in (b0, b0 + 2048, ht_at)]
        XS = arena[:, ht_at + 2048:ht_at + 4096].rearrange("p (g u s n) -> p g u s n", g=2, u=4, s=2)
        roomB2 = Room(b1, END)
        yt3 = roomB2.take(3072)
        YT = [yt3[:, 1024 * i:1024 * i + 1024] for i in range(3)] + [arena[:, xi0 + 2048:xi0 + 3072]]
        YG = [y.rearrange("p (c t) -> p c t", c=KT) for y in YT]
        BK = roomB2.take(1536).rearrange("p (g q n) -> p g q n", g=3, q=2)
        RH = roomB2.take(256).rearrange("p (q n) -> p q n", q=2)
        SA = roomB2.take(256).rearrange("p (q n) -> p q n", q=2)
        ST = roomB2.take(1024).rearrange("p (c n) -> p c n", c=PAIRS)
        STMP = roomB2.take(256).rearrange("p (q n) -> p q n", q=2)
        YL_ = roomB2.take(LEVELS * 512)
        YL = YL_.rearrange("p (l u n) -> p l u n", l=LEVELS, u=4)

        def corner(hf, w):
            return banks[hf][:, 2 * P:4 * P].rearrange("p (u w n) -> p u w n", u=2, w=2)[:, :, w, :]

        dlo = Room(base, base + 16384)
        XNP = dlo.take(KT * PADT).rearrange("p (c t) -> p c t", c=KT)
        MIX = XNP[:, :, 0:T]
        xn_at = dlo.at
        xn_flat = dlo.take(4096)
        XN = xn_flat.rearrange("p (t n) -> p t n", t=NT)
        UC = xn_flat.rearrange("p (t s n) -> p t s n", t=NT, s=2)
        OUTB = [xn_flat[:, 512 * i:512 * i + 512].rearrange("p (j n) -> p j n", j=2) for i in range(4)]
        xr_at = dlo.at
        XR = arena[:, xr_at:xr_at + 4096].rearrange("p (t n) -> p t n", t=NT)
        WX = arena[:, xr_at + 4096:xr_at + 6144].rearrange("p (k n) -> p k n", k=KT)
        QT = dlo.take(2048).rearrange("p (c t) -> p c t", c=4)
        CK = dlo.take(1024).rearrange("p (c t) -> p c t", c=4)
        KTP = dlo.take(4 * PADT).rearrange("p (c t) -> p c t", c=4)
        GX = dlo.take(1024)
        gate_flat = HT_[:, 0:4096]
        GATE = gate_flat.rearrange("p (c t) -> p c t", c=8)
        CX = gate_flat[:, 0:2048].rearrange("p (t n) -> p t n", t=2)
        CNT = gate_flat[:, 2048:4096].rearrange("p (c t) -> p c t", c=KT)
        CNJ = gate_flat[:, 2048:3072]
        X1 = arena[:, b0:b0 + 4096].rearrange("p (t n) -> p t n", t=NT)
        dhi = Room(b0 + 4096, END)
        VP = dhi.take(7 * 512).rearrange("p (t n) -> p t n", t=7)
        XNHI, XNLO = [[rounded(f"{n}{c}", at + c * T, T) for c in range(KT)]
                      for n, at in (("xn_hi", xn_at), ("xn_lo", v_at))]
        ut_at = dhi.at
        UT = dhi.take(2048).rearrange("p (c t) -> p c t", c=4)
        YF = UT
        BM = dhi.take(3 * NAH * WIN).rearrange("p (v h n) -> p v h n", v=3, h=NAH)
        MXHI, MXLO = [[rounded(f"{n}{c}", (v_at if c < 4 else ut_at + 2048) + 2048 * lo + c % 4 * T, T)
                       for c in range(KT)] for n, lo in (("mix_hi", 0), ("mix_lo", 1))]
        W2LO = [rounded(f"w_out2_lo{i}", wr_at + 2048 * i, 2048) for i in range(3)]
        w2hi = [rounded(f"w_out2_hi{i}", at, 2048) for i, at in enumerate((ut_at, xn_at + 2048, ht_at))]
        W2HI = w2hi + w2hi[:1]
        pr = dhi.at
        REL = dhi.take(NAH * RBW)
        NEAR = dhi.take(3 * WIN)
        GDIAG = [xn_flat[:, 512 * i:512 * i + 512] for i in range(2)]
        DTMP = [dhi.take(512) for _ in range(2)]
        DROOT = [GX[:, 0:512], dlo.take(512)]
        datt = Room(pr, END)
        PB = [datt.take(512) for _ in range(4)]
        PT = [datt.take(512) for _ in range(3)]
        ON = datt.take(512)

        bank_full = [sem(f"bank_full{b}") for b in range(8)]
        bank_free = [sem(f"bank_free{b}") for b in range(8)]
        weights_here = [sem(f"weights_here{s}") for s in range(3)]
        consts_here, ups_here, x_again, ctx_here, rel_here, wx_here = [
            sem(n) for n in ("consts_here", "ups_here", "x_again", "ctx_here", "rel_here", "wx_here")]
        x_here = [sem(f"x_here{t}") for t in range(NT)]
        out_stored = [sem(f"out_stored{i}") for i in range(4)]
        act_steps, dve_steps, pool_steps = sem("act_steps"), sem("dve_steps"), sem("pool_steps")
        act_phase, dve_phase, pool_phase = sem("act_phase"), sem("dve_phase"), sem("pool_phase")
        x_squared, x_scaled, mixed = sem("x_squared"), sem("x_scaled"), sem("mixed")
        k_scaled, k_squared, kk_done = sem("k_scaled"), sem("k_squared"), sem("kk_done")
        csum_ready, decays_ready, a_ready, kmod_ready, rk_ready, kappa_ready, bonus_done = [
            sem(n) for n in ("csum_ready", "decays_ready", "a_ready", "kmod_ready", "rk_ready", "kappa_ready",
                             "bonus_done")]
        xn_rounded, xn_split, weights_split_d = sem("xn_rounded"), sem("xn_split"), sem("weights_split_d")
        mx_rounded, mx_split, mx_split_d, w2_rounded, w2_split = [
            sem(n) for n in ("mx_rounded", "mx_split", "mx_split_d", "w2_rounded", "w2_split")]
        weights_rounded, weights_split, mix_rough, mix_rounded = [
            sem(n) for n in ("weights_rounded", "weights_split", "mix_rough", "mix_rounded")]
        vectors_ready, gate_tanh, c_tanh = [sem(n) for n in ("vectors_ready", "gate_tanh", "c_tanh")]
        y_zeroed, ab_ready, inverted, expanded = [sem(n) for n in ("y_zeroed", "ab_ready", "inverted", "expanded")]
        lt_back, inv_out = sem("lt_back"), sem("inv_out")
        lt_out = [sem(f"lt_out{i}") for i in range(2)]
        inv_back = [sem(f"inv_back{q}") for q in range(BATCHES)]
        mods_block, pv_done = sem("mods_block"), sem("pv_done")
        mods_copied = sem("mods_copied")
        z_ready, y_ready, x_grown, x_added = [[sem(f"{n}{h}") for h in range(2)] for n in
                                              ("z_ready", "y_ready", "x_grown", "x_added")]
        rhs_ready, rhs_copied, sa_ready, sa_copied, ys_ready, s_updated, y_copied = [
            [sem(f"{n}{h}") for h in range(2)] for n in
            ("rhs_ready", "rhs_copied", "sa_ready", "sa_copied", "ys_ready", "s_updated", "y_copied")]
        centred, gn_squared, gn_sums, gn_root, y_normed, bv_ready, y_gated = [
            sem(n) for n in ("centred", "gn_squared", "gn_sums", "gn_root", "y_normed", "bv_ready", "y_gated")]
        n2_root, cn_root, cn_ready, xn_ready, mods_ready, pads_ready, gdiag_ready = [
            sem(n) for n in ("n2_root", "cn_root", "cn_ready", "xn_ready", "mods_ready", "pads_ready", "gdiag_ready")]
        qk_squared, qk_done = sem("qk_squared"), sem("qk_done")
        gate2_tanh, bm_ready, masked, out_ready = [sem(n) for n in ("gate2_tanh", "bm_ready", "masked", "out_ready")]

        def cols(w, a, n):
            return w.rearrange("(k p) n -> p k n", p=P)[:, :, a:a + n], w.shape[0] // P, n

        stream = [cols(w_in, 4 * D, P)]
        for first in (D, 0):
            stream += [cols(w_in, first + P * b, P) for b in range(KT)]
        stream += [cols(w_in, 2 * D + 256 * b, 256) for b in range(4)]
        split_g = len(stream)
        stream += [cols(w_in, 3 * D + P * b, P) for b in range(KT)]
        stream += [cols(w_ada, 256 * b, 256) for b in range(12)]
        stream += [cols(w_out, 256 * b, 256) for b in range(3)]
        stream += [cols(w_in2, a + 256 * b, 256) for a in (1536, 2048) for b in range(2)]
        split_d = len(stream)
        stream += [cols(w_in2, a + P * b, P) for a in (1536, 1024, 0, 512, 2560) for b in range(4)]
        stream += [cols(cos_t, 0, 512), cols(nsin_t, 0, 512), cols(w_four, 0, 512)]
        stream += [cols(w_out2, 256 * b, 256) for b in range(4)]

        SPLIT_A = list(range(1, 1 + 2 * KT)) + list(range(split_g, split_g + KT))
        SPLIT_D = list(range(split_d, split_d + 20))

        def block_view(n):
            _, k, w = stream[n]
            return WR[n % 3][:, 0:k * w].rearrange("p (k n) -> p k n", k=k)

        class Steps:

            def __init__(self, eng, s):
                self.eng, self.s, self.n = eng, s, 0

            def did(self, ins):
                ins.then_inc(self.s, 1)
                self.n += 1

            def wait(self):
                self.eng.wait_ge(self.s, self.n)

            def own(self, ins):
                self.did(ins)
                self.wait()

        where, uses = {}, [0] * 8
        block_key = {}

        def arrived(eng, key):
            b, n = where[key]
            eng.wait_ge(bank_full[b], n)
            return banks[b]

        def free(ins, key):
            ins.then_inc(bank_free[where[key][0]], 1)

        def stored(eng, key):
            b, n = where[key]
            eng.wait_ge(bank_free[b], n)

        def others_done(eng, n, mine):
            for s in (act_phase, dve_phase, pool_phase):
                if s is not mine:
                    eng.wait_ge(s, n)

        def halves(ap, b, s):
            v = ap.rearrange("p (m s b) -> p m s b", s=2, b=b)
            return v[:, :, s, :]

        def halves2(ap, b, s):
            v = ap.rearrange("p u (m s b) -> p u m s b", s=2, b=b)
            return v[:, :, :, s, :]

        ITEMS = [("ck", c) for c in range(4)] + [("kk", c) for c in range(4)] + [("q", c) for c in range(4)]
        block = stack.enter_context(nc.Block())

        @block.tensor
        def _(pe):
            mm = nc.tensor.matmul
            taken = [0]

            def weights():
                n = taken[0]
                taken[0] += 1
                pe.wait_ge(weights_here[n % 3], 16 * (n // 3 + 1))
                return block_view(n)

            def out_bank(key, b):
                if uses[b]:
                    pe.wait_ge(bank_free[b], uses[b])
                uses[b] += 1
                where[key] = (b, uses[b])
                return banks[b]

            turn = [0]

            def next_bank(key, n=6):
                turn[0] = (turn[0] + 1) % n
                return out_bank(key, turn[0])

            def full(ins, key):
                ins.then_inc(bank_full[where[key][0]], 1)
                block_key[taken[0] - 1] = key

            def split_weights():
                if taken[0] in SPLIT_A:
                    pe.wait_ge(weights_split, SPLIT_A.index(taken[0]) + 1)
                else:
                    pe.wait_ge(weights_split_d, SPLIT_D.index(taken[0]) + 1)
                weights()
                i = (taken[0] - 1) % 3
                return WLO[i], WHI[i]

            def split_product(o, w_lo, w_hi, x_lo, x_hi, k):
                wk = slice(k * P, (k + 1) * P)
                mm(o[:, :], w_hi[:, wk], x_hi, start=(k == 0), stop=False)
                mm(o[:, :], w_hi[:, wk], x_lo, start=False, stop=False)
                return mm(o[:, :], w_lo[:, wk], x_hi, start=False, stop=(k == KT - 1))

            def accumulate(o, lhs, rhs, n=KT):
                for k in range(n):
                    last = mm(o, lhs(k), rhs(k), start=(k == 0), stop=(k == n - 1))
                return last

            pe.wait_ge(consts_here, 32)
            pe.wait_ge(x_scaled, NT)
            for c in range(KT):
                o = next_bank(("hT", c))
                for t in range(NT):
                    last = nc.tensor.transpose(o[:, t * P:(t + 1) * P], V[:, t, c * P:(c + 1) * P], ident)
                full(last, ("hT", c))
            w = weights()
            for m in range(2):
                o = next_bank(("low", m))
                for k in range(KT):
                    pe.wait_ge(mixed, KT * m + k + 1)
                    last = mm(o[0:64, :], w[:, k, 64 * m:64 * m + 64], MIXES[m][:, k, :], start=(k == 0), stop=(k == KT - 1))
                full(last, ("low", m))
            for m, name in ((2, "k"), (3, "r")):
                for c in range(KT):
                    lo, hi = split_weights()
                    o = next_bank((name, c))
                    for k in range(KT):
                        if c == 0:
                            pe.wait_ge(mixed, KT * m + k + 1)
                        last = split_product(o, lo, hi, XLO[m][k][:, :], XHI[m][k][:, :], k)
                    full(last, (name, c))
                    if m == 3:
                        pe.wait_ge(k_squared, c + 1)
                        o = next_bank(("kss", c))
                        ins = mm(o[:, :], heads1, SQ2[c % 2], start=True, stop=True)
                        ins.then_inc(bank_full[where["kss", c][0]], 1)
            stored(pe, ("low", 0))
            stored(pe, ("low", 1))
            pe.wait_ge(ups_here, 32)
            pe.wait_ge(vectors_ready, 1)
            bonus_bank = out_bank("bonus", 7)

            def bonus(c):
                pe.wait_ge(rk_ready, c + 1)
                for t in range(NT):
                    last = mm(bonus_bank[:, t * 16 + 2 * c:t * 16 + 2 * c + 2], RKT[:, t * P:(t + 1) * P],
                              RKB[:, c, :], start=True, stop=True, skip_group_check=True)
                if c < KT - 1:
                    last.then_inc(bonus_done, 1)
                else:
                    full(last, "bonus")

            def first_l(c):
                pe.wait_ge(ab_ready, c + 1)
                for h in range(2):
                    o = next_bank(("lt", c, h))
                    lo = HD * h
                    for j in range(NT):
                        at = slice(j * P, (j + 1) * P)
                        last = mm(o[:, at], AB[lo:lo + HD, c, at], AR[lo:lo + HD, 0, c, at], start=True, stop=True,
                                  skip_group_check=True)
                    last.then_inc(bank_full[where["lt", c, h][0]], 1)

            for c in range(KT):
                for s, name in ((0, "w"), (1, "a")):
                    o = next_bank((name, c))
                    mm(o[:, :], UPS[:, s, c * P:(c + 1) * P], LOW[:, s, :], start=True, stop=True)\
                        .then_inc(bank_full[where[name, c][0]], 1)
                if c < 4:
                    w = weights()
                pe.wait_ge(mixed, KT * (5 if c < 4 else 6))
                for h in range(2):
                    if c < 4:
                        o = next_bank(("v", c, h))
                        for i in range(2):
                            t = 2 * h + i
                            last = accumulate(o[:, i * 256:(i + 1) * 256], lambda k: XI[0][:, k, t * P:(t + 1) * P],
                                              lambda k: w[:, k, :])
                        full(last, ("v", c, h))
                    else:
                        cc = 2 * (c - 4) + h
                        lo, hi = split_weights()
                        o = next_bank(("g", cc))
                        for k in range(KT):
                            last = split_product(o, lo, hi, XLO[5][k][:, :], XHI[5][k][:, :], k)
                        full(last, ("g", cc))
                if c >= 1:
                    bonus(c - 1)
                if c == KT - 1:
                    bonus(c)
                if c >= 4:
                    first_l(2 * (c - 4))
                    first_l(2 * (c - 4) + 1)
            for b in range(8):
                if uses[b]:
                    pe.wait_ge(bank_free[b], uses[b])
            others_done(pe, 1, None)

            gram_n = [0]

            def gram_bank(key):
                b = 4 + gram_n[0] % 2
                gram_n[0] += 1
                return out_bank(key, b)

            def gram(g, u):
                j, cc = divmod(g, 4)
                c, lo = 2 * cc + u // 2, HD * (u % 2)
                o = gram_bank(("gram", g, u))
                at = slice(j * P, (j + 1) * P)
                mm(o[:, 0:256], AB[lo:lo + HD, c, at], AR[lo:lo + HD, :, c, at], start=True, stop=True,
                   skip_group_check=True)
                mm(o[:, 256:512], KB[lo:lo + HD, c, at], AR[lo:lo + HD, :, c, at], start=True, stop=True,
                   skip_group_check=True).then_inc(bank_full[where["gram", g, u][0]], 1)

            def turned(g):
                j, cc = divmod(g, 4)
                o = gram_bank(("turn", g))
                for q in range(2):
                    for s, src in enumerate((AB, KB)):
                        last = nc.tensor.transpose(o[:, (2 * q + s) * P:(2 * q + s + 1) * P],
                                                   src[:, 2 * cc + q, j * P:(j + 1) * P], ident)
                last.then_inc(bank_full[where["turn", g][0]], 1)

            def off_product(g, l, hf):
                n = LEVELS * g + l
                if l == 0:
                    pe.wait_ge(expanded, g + 1)
                if n:
                    pe.wait_ge(x_added[hf], n)
                for i in range(2):
                    u = 2 * hf + i
                    if l == 0:
                        stored(pe, ("gram", g, u))
                    last = mm(banks[hf][:, i * P:(i + 1) * P], GM[g % 3][:, u, 0:P], XS[:, g % 2, u, 0, :],
                              start=True, stop=True, skip_group_check=True)
                last.then_inc(z_ready[hf], 1)

            def grow(g, l, hf):
                pe.wait_ge(y_ready[hf], LEVELS * g + l + 1)
                for i in range(2):
                    u = 2 * hf + i
                    xt = XS[:, g % 2, u, 1, :]
                    o = banks[hf][:, (2 + i) * P:(3 + i) * P]
                    y = YL[:, l, u, :]
                    if l < LEVELS - 1:
                        mm(o[:, 0:HD], xt, halves(y, BLK << l, 0), start=True, stop=True, skip_group_check=True)
                    last = mm(o[:, HD:P], y, halves(xt, BLK << l, 1), start=True, stop=True, skip_group_check=True)
                last.then_inc(x_grown[hf], 1)

            def scan_rhs(g, q):
                j, cc = divmod(g, 4)
                c = 2 * cc + q
                o = banks[6 + q][:, 0:P]
                if g:
                    pe.wait_ge(y_copied[q], g)
                    pe.wait_ge(s_updated[q], min(g, GROUPS - 4))
                for i in range(2):
                    stored(pe, ("gram", g, 2 * q + i))
                if j:
                    mm(o, AR[:, 0, c, j * P:(j + 1) * P], ST[:, c, :], start=True, stop=False, skip_group_check=True)
                for i in range(2):
                    last = mm(o[:, i * HD:(i + 1) * HD], GM[g % 3][:, 2 * q + i, 2 * P:3 * P],
                              V[:, j, c * P + i * HD:c * P + (i + 1) * HD], start=(j == 0 and i == 0), stop=(i == 1),
                              skip_group_check=True)
                last.then_inc(rhs_ready[q], 1)

            def scan_sa(g, q):
                pe.wait_ge(rhs_copied[q], g + 1)
                pe.wait_ge(x_added[q], LEVELS * (g + 1))
                for i in range(2):
                    last = mm(banks[6 + q][:, P + i * HD:P + (i + 1) * HD], XS[:, g % 2, 2 * q + i, 1, :],
                              RH[:, q, i * HD:(i + 1) * HD], start=True, stop=True, skip_group_check=True)
                last.then_inc(sa_ready[q], 1)

            def scan_out(g, q):
                j, cc = divmod(g, 4)
                c = 2 * cc + q
                pe.wait_ge(sa_copied[q], g + 1)
                o = banks[6 + q][:, 2 * P:3 * P]
                if j:
                    mm(o, AR[:, 1, c, j * P:(j + 1) * P], ST[:, c, :], start=True, stop=False, skip_group_check=True)
                for i in range(2):
                    gm = GM[g % 3][:, 2 * q + i, :]
                    mm(o[:, i * HD:(i + 1) * HD], gm[:, P:2 * P], SA[:, q, i * HD:(i + 1) * HD],
                       start=(j == 0 and i == 0), stop=False, skip_group_check=True)
                    last = mm(o[:, i * HD:(i + 1) * HD], gm[:, 3 * P:4 * P],
                              V[:, j, c * P + i * HD:c * P + (i + 1) * HD], start=False, stop=(i == 1),
                              skip_group_check=True)
                if j < NT - 1:
                    stored(pe, ("turn", g))
                    s = banks[6 + q][:, 3 * P:4 * P]
                    mm(s, BK[:, g % 3, q, 0:P], SA[:, q, :], start=True, stop=False, skip_group_check=True)
                    last = mm(s, BK[:, g % 3, q, P:2 * P], V[:, j, c * P:(c + 1) * P], start=False, stop=True,
                              skip_group_check=True)
                last.then_inc(ys_ready[q], 1)

            def modulation(n):
                w = weights()
                if n == 0:
                    out_bank("mods", 2)
                last = accumulate(banks[2][0:2, 0:256], lambda k: SILC[:, k, :], lambda k: w[:, k, :])
                last.then_inc(mods_block, 1)
                block_key[taken[0] - 1] = n + 1

            def turn_mods(n):
                pe.wait_ge(mods_copied, n + 1)
                for h in range(2):
                    at = 256 + 4 * n + 2 * h
                    last = nc.tensor.transpose(banks[2][:, at:at + 2], MROW[:, h * P:(h + 1) * P], ident[0:2, 0:2])
                if n == 11:
                    last.then_inc(bank_full[2], 1)

            def turn_y(j, piece):
                h = piece // 2
                if piece == 0:
                    pe.wait_ge(y_normed, j + 1)
                    pe.wait_ge(bv_ready, j + 1)
                name, src = ("yT", YT[j]) if piece % 2 == 0 else ("bT", V[:, j, :])
                o = out_bank((name, j, h), 3) if j < NT - 1 else next_bank((name, j, h))
                for i in range(4):
                    last = nc.tensor.transpose(o[:, i * P:(i + 1) * P], src[:, (4 * h + i) * P:(4 * h + i + 1) * P],
                                               ident)
                last.then_inc(bank_full[where[name, j, h][0]], 1)

            for u in range(4):
                gram(0, u)
            turned(0)
            pe.wait_ge(y_zeroed, 1)
            for g in range(GROUPS + 4):
                now, nxt, old = g < GROUPS, g + 1 < GROUPS, 0 < g <= GROUPS
                mod = g - 1 if 1 <= g <= 12 else None
                turning = g in (8, 12, 16)
                if g == 13:
                    turn_mods(11)
                for l in range(LEVELS):
                    if now:
                        off_product(g, l, 0)
                        off_product(g, l, 1)
                    if nxt:
                        gram(g + 1, l)
                    if old and l == 0:
                        scan_rhs(g - 1, 0)
                        scan_rhs(g - 1, 1)
                    if old and l == 1:
                        scan_out(g - 1, 0)
                    if old and l == 2:
                        scan_out(g - 1, 1)
                    if mod is not None and l == 0:
                        if mod:
                            turn_mods(mod - 1)
                        modulation(mod)
                    if now:
                        grow(g, l, 0)
                        grow(g, l, 1)
                    if old and l == 0:
                        scan_sa(g - 1, 0)
                        scan_sa(g - 1, 1)
                    if nxt and l == 1:
                        gram(g + 1, 3)
                    if nxt and l == 2:
                        turned(g + 1)
                    if turning:
                        turn_y(g // 4 - 2, l)
                if turning:
                    turn_y(g // 4 - 2, 3)

            wo = [weights(), weights()]

            def project_y(t, h):
                pe.wait_ge(y_gated, 2 * (t + 1))
                if (t, h) == (0, 1):
                    wo.extend([weights(), WX])
                    pe.wait_ge(wx_here, 16)
                o = next_bank(("o", t, h))
                for i in range(2):
                    last = accumulate(o[:, i * 256:(i + 1) * 256], lambda k: YG[t][:, k, :],
                                      lambda k: wo[2 * h + i][:, k, :])
                last.then_inc(bank_full[where["o", t, h][0]], 1)

            def turn_x1(t):
                pe.wait_ge(xn_ready, t + 1)
                for h in range(2):
                    o = next_bank(("xT", t, h))
                    for i in range(4):
                        last = nc.tensor.transpose(o[:, i * P:(i + 1) * P], XN[:, t, (4 * h + i) * P:(4 * h + i + 1) * P],
                                                   ident)
                    last.then_inc(bank_full[where["xT", t, h][0]], 1)

            for t in range(3):
                project_y(t, 0)
            for piece in range(4):
                turn_y(3, piece)
            project_y(3, 0)
            block_key[taken[0] - 2] = block_key[taken[0] - 1] = ("o", 3, 0)
            project_y(0, 1)
            pe.wait_ge(cn_ready, 2)
            for h in range(4):
                o = next_bank(("cT", h))
                for i in range(2):
                    for t in range(2):
                        c = 2 * h + i
                        last = nc.tensor.transpose(o[:, i * 256 + t * P:i * 256 + (t + 1) * P],
                                                   CX[:, t, c * P:(c + 1) * P], ident)
                last.then_inc(bank_full[where["cT", h][0]], 1)
            items = []

            def head_norm(i):
                n = CTX if ITEMS[i][0] == "ck" else T
                pe.wait_ge(qk_squared, i + 1)
                o = next_bank(("ss", i))
                mm(o[:, 0:n], heads1, DTMP[i % 2][:, 0:n], start=True, stop=True)\
                    .then_inc(bank_full[where["ss", i][0]], 1)

            def xn_output(name, c):
                lo, hi = split_weights()
                o = next_bank((name, c))
                for k in range(KT):
                    if (name, c) == ("kk", 0):
                        pe.wait_ge(xn_split, k + 1)
                    last = split_product(o, lo, hi, XNLO[k][:, :], XNHI[k][:, :], k)
                full(last, (name, c))

            def qk_output(name, c, w, h):
                if name == "ck":
                    o = next_bank((name, c))
                    full(accumulate(o[:, 0:CTX], lambda k: w[:, k, h * P:(h + 1) * P], lambda k: CNT[:, k, :]),
                         (name, c))
                else:
                    xn_output(name, c)
                items.append((name, c))
                if len(items) > 1:
                    head_norm(len(items) - 2)

            project_y(1, 1)
            project_y(2, 1)
            turn_x1(0)
            project_y(3, 1)
            block_key[taken[0] - 1] = ("o", 3, 1)
            turn_x1(1)
            for h in range(4):
                stored(pe, ("cT", h))
            for nb in range(2):
                w = weights()
                for h in range(2):
                    qk_output("ck", 2 * nb + h, w, h)
                    if nb != h:
                        turn_x1(2 + nb)
            for t in range(NT):
                stored(pe, ("xT", t, 0))
                stored(pe, ("xT", t, 1))
            pe.wait_ge(pads_ready, 1)
            for nb in range(2):
                w = weights()
                for b4 in range(4):
                    o = next_bank(("vv", nb, b4))
                    for i in range(2):
                        t = 2 * b4 + i
                        if t < 7:
                            last = accumulate(o[:, i * 256:(i + 1) * 256],
                                              (lambda k: XNP[:, k, t * P:(t + 1) * P]) if t < 5 else
                                              (lambda k: CNT[:, k, (t - 5) * P:(t - 4) * P]), lambda k: w[:, k, :])
                    full(last, ("vv", nb, b4))
            for name in ("kk", "q"):
                for c in range(4):
                    qk_output(name, c, None, None)
            head_norm(len(items) - 1)
            for name, n0 in (("f", 0), ("g2", 0), ("g2", 4)):
                for c in range(4):
                    xn_output(name, n0 + c)
            for t in range(NT):
                for gp in range(2):
                    stored(pe, ("f", 2 * gp))
                    stored(pe, ("f", 2 * gp + 1))
                    o = next_bank(("uc", t, gp))
                    for i in range(2):
                        last = mm(o[:, i * 256:(i + 1) * 256], UT[:, 2 * gp + i, t * P:(t + 1) * P], con("dft128"),
                                  start=True, stop=True)
                    last.then_inc(bank_full[where["uc", t, gp][0]], 1)
            dft = [weights(), weights()]
            for g in range(4):
                o = next_bank(("yf", g))
                for s in range(2):
                    for t in range(NT):
                        stored(pe, ("uc", t, g // 2))
                        last = mm(o[:, :], UC[:, t, s, g * P:(g + 1) * P], dft[s][:, t, :], start=(s == 0 and t == 0),
                                  stop=(s == 1 and t == NT - 1))
                full(last, ("yf", g))
            block_key[taken[0] - 2] = ("yf", 3)
            w = weights()
            for n in range(4):
                o = next_bank(("fo", n))
                for k in range(4):
                    stored(pe, ("yf", k))
                full(accumulate(o[:, :], lambda k: w[:, k, n * P:(n + 1) * P], lambda k: YF[:, k, :], 4), ("fo", n))

            for h in range(2):
                pe.wait_ge(gdiag_ready, h + 1)
                o = next_bank(("gx", h))
                full_ins = mm(o[:, :], con("ones"), GDIAG[h], start=True, stop=True)
                full_ins.then_inc(bank_full[where["gx", h][0]], 1)

            def scores(n):
                qt, h = divmod(n, NAH)
                lo = HD * (h % 2)
                o = out_bank(("s", n), (0, 1, 6)[n % 3])
                q = QT[lo:lo + HD, h // 2, qt * P:(qt + 1) * P]
                mm(o[:, 0:WIN], q, KTP[lo:lo + HD, h // 2, qt * P:qt * P + WIN], start=True, stop=True,
                   skip_group_check=True)
                mm(o[:, WIN:WIN + CTX], q, CK[lo:lo + HD, h // 2, :], start=True, stop=True, skip_group_check=True)\
                    .then_inc(bank_full[where["s", n][0]], 1)

            def turn_probs(n):
                stored(pe, ("s", n))
                o = out_bank(("pt", n), 2 + n % 2)
                for i in range(4):
                    last = nc.tensor.transpose(o[:, i * P:(i + 1) * P], PB[n % 4][:, i * P:(i + 1) * P], ident)
                last.then_inc(bank_full[2 + n % 2], 1)

            def take_values(n):
                qt, h = divmod(n, NAH)
                stored(pe, ("pt", n))
                b = 4 if qt % 2 == 0 else 7
                o = out_bank(("at", qt), b) if h == 0 else banks[b]
                for i in range(4):
                    v = VP[:, qt + i if i < 2 else 3 + i, h * HD:(h + 1) * HD]
                    last = mm(o[:, h * HD:(h + 1) * HD], PT[n % 3][:, i * P:(i + 1) * P], v, start=(i == 0),
                              stop=(i == 3), skip_group_check=True)
                last.then_inc(bank_full[b], 1) if h == NAH - 1 else last.then_inc(pv_done, 1)

            def turn_out(qt):
                stored(pe, ("at", qt))
                o = out_bank(("oT", qt), 5)
                for i in range(4):
                    last = nc.tensor.transpose(o[:, i * P:(i + 1) * P], ON[:, i * P:(i + 1) * P], ident)
                last.then_inc(bank_full[5], 1)

            pe.wait_ge(qk_done, len(ITEMS))
            for nb in range(2):
                for b4 in range(4):
                    stored(pe, ("vv", nb, b4))
            NU = NT * NAH
            for n in range(NU + 6):
                if n < NU:
                    scores(n)
                if 2 <= n < NU + 2:
                    turn_probs(n - 2)
                if 3 <= n < NU + 3:
                    take_values(n - 3)
                if n >= NAH + 5 and (n - NAH - 5) % NAH == 0:
                    turn_out((n - NAH - 5) // NAH)
            for nb in range(4):
                weights()
                slot = (taken[0] - 1) % 3
                for th in range(2):
                    o = next_bank(("z", nb, th))
                    if nb == 0 and th == 0:
                        for n in range(4):
                            stored(pe, ("fo", n))
                            stored(pe, ("oT", n))
                        pe.wait_ge(mx_split, 4)
                    if th == 0:
                        pe.wait_ge(w2_split, nb + 1)
                    for i in range(2):
                        at = slice((2 * th + i) * P, (2 * th + i + 1) * P)
                        for k in range(KT):
                            if (nb, th, i) == (0, 0, 0) and k >= 4:
                                pe.wait_ge(mx_split_d, k - 3)
                            wk = slice(k * 256, (k + 1) * 256)
                            oi = o[:, i * 256:(i + 1) * 256]
                            mm(oi, MXHI[k][:, at], W2HI[nb][:, wk], start=(k == 0), stop=False)
                            mm(oi, MXHI[k][:, at], W2LO[slot][:, wk], start=False, stop=False)
                            last = mm(oi, MXLO[k][:, at], W2HI[nb][:, wk], start=False, stop=(k == KT - 1))
                    full(last, ("z", nb, th))

        @block.sync
        def _(sp):
            x_t = x.rearrange("(t p) n -> p t n", p=P)
            for t in range(NT):
                sp.dma_start(V[:, t, :], x_t[:, t, :]).then_inc(x_here[t], 16)
            for n, (src, k, w) in enumerate(stream):
                if n >= 3:
                    key = block_key[n - 3]
                    if isinstance(key, int):
                        sp.wait_ge(mods_block, key)
                    else:
                        arrived(sp, key)
                sp.dma_start(block_view(n), src).then_inc(weights_here[n % 3], 16)
                if n == 0:
                    sp.dma_start(UPS[:, 0, :], w_up).then_inc(ups_here, 16)
                    sp.dma_start(UPS[:, 1, :], a_up).then_inc(ups_here, 16)
                if n == 43:
                    sp.wait_ge(ys_ready[0], GROUPS)
                    sp.wait_ge(ys_ready[1], GROUPS)
                    sp.dma_start(XR, x_t).then_inc(x_again, 16)
                    sp.dma_start(WX, cols(w_out, 768, 256)[0]).then_inc(wx_here, 16)
                    sp.wait_ge(y_gated, 2 * NT)
                    sp.dma_start(CX, ctx_x.rearrange("(t p) n -> p t n", p=P)).then_inc(ctx_here, 16)
                if n == 46:
                    sp.dma_start(NEAR, near).then_inc(rel_here, 16)
                    for cl in range(16):
                        src = bass.AP(rel_bias.tensor, RBPAD + 7 - cl, [[31, GH], [RB + 2 * RBPAD, NAH], [1, RBW]])
                        sp.dma_start(REL[cl * GH:(cl + 1) * GH, :], src).then_inc(rel_here, 16)
            for i in range(8):
                nb, th = divmod(i, 2)
                sp.wait_ge(out_ready, i + 1)
                sp.dma_start(out.rearrange("(t p) n -> p t n", p=P)[:, 2 * th:2 * th + 2, 256 * nb:256 * nb + 256],
                             OUTB[i % 4]).then_inc(out_stored[i % 4], 16)
            for s in out_stored:
                sp.wait_ge(s, 32)

        @block.scalar
        def _(act):
            A = nc.scalar.activation
            own = Steps(act, act_steps)
            eps, gn_eps, eps64 = [con("eps")[:, i:i + 1] for i in range(3)]
            act.dma_start(CON, consts).then_inc(consts_here, 16)
            act.dma_start(VECS, vecs).then_inc(consts_here, 16)
            for t in range(NT):
                act.wait_ge(x_here[t], 16)
                own.own(A(XI[0][:, 2 * t:2 * t + 2, :], V[:, t, :].rearrange("p (a b) -> p a b", a=2), ACT.Square,
                          accum_out=ssq[:, t:t + 1]))
                if t == 0:
                    act.wait_ge(consts_here, 32)
                A(rstd[:, t:t + 1], ssq[:, t:t + 1], ACT.Sqrt, bias=eps, scale=1.0 / D).then_inc(x_squared, 1)
            act.wait_ge(vectors_ready, 1)
            A(SILT[:, 0:16], VECS[:, VEC["c"]:VEC["c"] + 16], ACT.Tanh, scale=0.5).then_inc(c_tanh, 1)
            for c in range(KT):
                o = arrived(act, ("hT", c))
                free(A(HT[:, c, 1:T + 1], o[:, :], ACT.Copy, scale=vec("norm", c)), ("hT", c))
            def round_weights(i):
                n = (SPLIT_A + SPLIT_D)[i]
                act.wait_ge(weights_here[n % 3], 16 * (n // 3 + 1))
                A(WHI[n % 3][:, :], WR[n % 3][:, 0:1024], ACT.Copy).then_inc(weights_rounded, 1)

            def round_mix(m, c):
                act.wait_ge(mix_rough, KT * nth_split[m] + c + 1)
                A(XHI[m][c][:, :], MIXES[m][:, c, :], ACT.Copy).then_inc(mix_rounded, 1)

            round_weights(0)
            for c in range(KT):
                round_mix(2, c)
            round_weights(1)
            free(A(LOW[:, 0, :], arrived(act, ("low", 0))[0:64, :], ACT.Tanh), ("low", 0))
            free(A(LOW[:, 1, :], arrived(act, ("low", 1))[0:64, :], ACT.Copy), ("low", 1))
            for c in range(KT):
                round_weights(c + 2)
                free(A(KB[:, c, :], arrived(act, ("k", c))[:, :], ACT.Copy), ("k", c))
                round_mix(3, c)

            def square_k(c):
                act.wait_ge(k_scaled, c + 1)
                if c >= 2:
                    arrived(act, ("kss", c - 2))
                A(SQ2[c % 2], AR[:, 0, c, :], ACT.Square).then_inc(k_squared, 1)

            square_k(0)
            for c in range(KT):
                if c + 1 < KT:
                    square_k(c + 1)
                if c + 10 < 2 * KT:
                    round_weights(c + 10)
                free(A(AR[:, 1, c, :], arrived(act, ("r", c))[:, :], ACT.Copy), ("r", c))
                o = arrived(act, ("kss", c))
                if c >= 2:
                    act.wait_ge(kk_done, c - 1)
                free(A(ROOT[c % 2], o[:, :], ACT.Sqrt), ("kss", c))
            def copy_l(q):
                for i in range(4):
                    k, (c, h) = 4 * q + i, (2 * q + i // 2, i % 2)
                    o = arrived(act, ("lt", c, h))
                    if k >= 2:
                        act.wait_ge(lt_out[k % 2], 16 * (k // 2))
                    free(A(LTS[k % 2], o[:, :], ACT.Copy), ("lt", c, h))
                    stored(act, ("lt", c, h))
                    dst = bass.AP(lt_dram.tensor, k * NT * P * (P + 1), [[P, P], [P * (P + 1), NT], [1, P]])
                    act.dma_start(dst, LTS[k % 2].rearrange("p (j t) -> p j t", j=NT)).then_inc(lt_out[k % 2], 16)

            def fetch_blocks(q):
                for i in range(2):
                    act.wait_ge(lt_out[i], 32 * (q + 1))
                if q:
                    act.wait_ge(inverted, q)
                src = bass.AP(lt_dram.tensor, q * UNITS * P * (P + 1), [[BLK * (P + 1), P], [P, BLK], [1, BLK]])
                act.dma_start(LTB, src).then_inc(lt_back, 16)

            def store_inverse(q):
                act.wait_ge(inverted, q + 1)
                dst = bass.AP(inv_dram.tensor, q * 2 * P * BLK * BLK, [[BLK * BLK, P], [P * BLK * BLK, 2], [1, BLK * BLK]])
                act.dma_start(dst, XO.rearrange("p s a b -> p s (a b)")).then_inc(inv_out, 16)

            def fetch_inverse(q):
                act.wait_ge(inv_out, 16 * (q + 1))
                for s in range(2):
                    src = bass.AP(inv_dram.tensor, (2 * q + s) * P * BLK * BLK, [[BLK, P], [P * BLK, UNITS], [1, BLK]])
                    act.dma_start(XST[:, q, s], src).then_inc(inv_back[q], 16)

            for c in range(KT):
                o = arrived(act, ("w", c))
                if c:
                    act.wait_ge(csum_ready, c)
                free(A(SIGW, o[:, :], ACT.Tanh, scale=0.5, bias=half_vec("w0", c)), ("w", c))
                free(A(AB[:, c, :], arrived(act, ("a", c))[:, :], ACT.Tanh, scale=0.5, bias=half_vec("a0", c)), ("a", c))
                act.wait_ge(csum_ready, c + 1)
                if c:
                    act.wait_ge(kappa_ready, c)
                csum = CSUM.rearrange("p (j t) -> p j t", j=4)
                A(E1[:, :, 1:P + 1], csum, ACT.Exp, scale=-KAPPA)
                A(E2, CSUM, ACT.Exp, scale=KAPPA)
                A(E1[:, :, 0], MID[:, 0:4], ACT.Exp, scale=KAPPA)
                A(MID[:, 4:8], MID[:, 0:4], ACT.Exp, scale=-KAPPA).then_inc(decays_ready, 1)
                for h in range(2):
                    if c < 4:
                        o = arrived(act, ("v", c, h))
                        free(A(V[:, 2 * h:2 * h + 2, c * 256:(c + 1) * 256], o.rearrange("p (i n) -> p i n", i=2),
                               ACT.Copy), ("v", c, h))
                    else:
                        cc = 2 * (c - 4) + h
                        o = arrived(act, ("g", cc))
                        if cc >= 2:
                            stored(act, ("g", cc - 2))
                        A(SQ2[cc % 2], o[:, :], ACT.Tanh, scale=0.5).then_inc(gate_tanh, 1)
                if c < 4:
                    round_mix(5, 2 * c)
                    round_mix(5, 2 * c + 1)
                if 3 <= c < 7:
                    round_weights(2 * KT + 2 * (c - 3))
                    round_weights(2 * KT + 2 * (c - 3) + 1)
                if c >= 7:
                    fetch_inverse(c - 7)
                if c >= 6:
                    store_inverse(c - 6)
                if c >= 5:
                    fetch_blocks(c - 5)
                if c >= 4:
                    copy_l(c - 4)
            A(CST[:, 0:1], CST[:, 4:5], ACT.Copy).then_inc(act_phase, 1)
            fetch_inverse(1)
            others_done(act, 1, act_phase)
            arrived(act, "bonus")

            def copy_turned(g):
                free(A(BK[:, g % 3, :, :], arrived(act, ("turn", g)).rearrange("p (q n) -> p q n", q=2), ACT.Copy),
                     ("turn", g))

            def copy_rhs(g, q):
                act.wait_ge(rhs_ready[q], g + 1)
                A(RH[:, q, :], banks[6 + q][:, 0:P], ACT.Copy).then_inc(rhs_copied[q], 1)

            def copy_sa(g, q):
                act.wait_ge(sa_ready[q], g + 1)
                A(SA[:, q, :], banks[6 + q][:, P:2 * P], ACT.Copy).then_inc(sa_copied[q], 1)

            def copy_y(g, q):
                j, cc = divmod(g, 4)
                c = 2 * cc + q
                act.wait_ge(ys_ready[q], g + 1)
                if j < NT - 1:
                    act.wait_ge(s_updated[q], g + 1)
                A(YT[j][:, c * P:(c + 1) * P], banks[6 + q][:, 2 * P:3 * P], ACT.Copy).then_inc(y_copied[q], 1)

            def take_y(j, h):
                o = arrived(act, ("yT", j, h))
                for i in range(4):
                    c = 4 * h + i
                    ins = A(YG[j][:, c, :], o[:, i * P:(i + 1) * P], ACT.Identity, bias=vec("gn_b", c),
                            scale=vec("gn_w", c))
                free(ins, ("yT", j, h))

            copy_turned(0)
            for g in range(GROUPS + 4):
                nxt, old = g + 1 < GROUPS, 0 < g <= GROUPS
                turning = g in (8, 12, 16)
                if old:
                    for q in range(2):
                        copy_rhs(g - 1, q)
                mod = g - 1 if 1 <= g <= 12 else None
                if mod is not None:
                    act.wait_ge(mods_block, mod + 1)
                    A(MROW, banks[2][0:2, 0:256], ACT.Copy).then_inc(mods_copied, 1)
                if old:
                    for q in range(2):
                        copy_sa(g - 1, q)
                if turning:
                    take_y(g // 4 - 2, 0)
                if old:
                    for q in range(2):
                        copy_y(g - 1, q)
                if nxt:
                    copy_turned(g + 1)
                if turning:
                    take_y(g // 4 - 2, 1)
                j = g // 4 - 1
                if g >= 5 and g % 4 == 1:
                    act.wait_ge(centred, j + 1)
                    if j:
                        act.wait_ge(gn_sums, j)
                    A(SQ, YT[j], ACT.Square).then_inc(gn_squared, 1)
                if g >= 6 and g % 4 == 2:
                    act.wait_ge(gn_sums, j + 1)
                    A(GST[:, 128 + 16 * j:144 + 16 * j], GST[:, 64 + 16 * j:80 + 16 * j], ACT.Sqrt, bias=gn_eps,
                      scale=1.0 / HD).then_inc(gn_root, 1)
                if g < 2:
                    store_inverse(2 + g)
                if g == 0:
                    fetch_blocks(3)
                if g < 2:
                    fetch_inverse(2 + g)
            take_y(3, 0)
            take_y(3, 1)
            act.wait_ge(ctx_here, 16)
            for t in range(2):
                own.own(A(CNJ, CX[:, t, :], ACT.Square, accum_out=SUMS[:, t:t + 1]))
            A(SUMS[:, 2:4], SUMS[:, 0:2], ACT.Sqrt, bias=eps, scale=1.0 / D).then_inc(cn_root, 1)

            def square_x1(t):
                for h in range(2):
                    stored(act, ("o", t, h))
                own.own(A(XN[:, t, :], X1[:, t, :], ACT.Square, accum_out=ssq[:, t:t + 1]))
                A(rstd[:, t:t + 1], ssq[:, t:t + 1], ACT.Sqrt, bias=eps, scale=1.0 / D).then_inc(n2_root, 1)

            def take_x1(t):
                for h in range(2):
                    o = arrived(act, ("xT", t, h))
                    for i in range(4):
                        c = 4 * h + i
                        dst = XNP[:, c, HD:HD + T].rearrange("p (col r) -> p r col", r=GH)[:, 2 * t:2 * t + 2, :]
                        ins = A(dst, o[:, i * P:(i + 1) * P].rearrange("p (r col) -> p r col", r=2), ACT.Identity,
                                bias=MODS[:, c, 0:1], scale=GSC[:, c, 0:1])
                    free(ins, ("xT", t, h))

            act.wait_ge(mods_ready, 1)
            square_x1(0)
            for h in range(4):
                o = arrived(act, ("cT", h))
                for i in range(2):
                    c = 2 * h + i
                    ins = A(CNT[:, c, :], o[:, i * 256:(i + 1) * 256], ACT.Identity, bias=MODS[:, c, 1:2],
                            scale=GSC[:, c, 1:2])
                free(ins, ("cT", h))
            square_x1(1)
            square_x1(2)
            take_x1(0)
            square_x1(3)
            take_x1(1)

            def root(i):
                n = CTX if ITEMS[i][0] == "ck" else T
                o = arrived(act, ("ss", i))
                if i >= 2:
                    act.wait_ge(qk_done, i - 1)
                q = ITEMS[i][0] == "q"
                free(A(DROOT[i % 2][:, 0:n], o[:, 0:n], ACT.Sqrt, bias=eps64 if q else eps,
                       scale=1.0 if q else 1.0 / HD), ("ss", i))

            def take_v():
                for nb in range(2):
                    for b4 in range(4):
                        o = arrived(act, ("vv", nb, b4)).rearrange("p (i n) -> p i n", i=2)
                        w = 2 if b4 < 3 else 1
                        free(A(VP[:, 2 * b4:2 * b4 + w, nb * 256:(nb + 1) * 256], o[:, 0:w, :], ACT.Copy), ("vv", nb, b4))

            def round_xn():
                stored(act, ("xT", 3, 1))
                for c in range(KT):
                    A(XNHI[c][:, :], XNP[:, c, HD:HD + T], ACT.Copy).then_inc(xn_rounded, 1)

            for i, key in enumerate(ITEMS):
                if i in (2, 3):
                    take_x1(i)
                if i == 4:
                    round_xn()
                    round_weights(len(SPLIT_A))
                    round_weights(len(SPLIT_A) + 1)
                    take_v()
                if i >= 4:
                    round_weights(len(SPLIT_A) + i - 4 + 2)
                n = CTX if key[0] == "ck" else T
                o = arrived(act, key)
                if i >= 2:
                    arrived(act, ("ss", i - 2))
                A(DTMP[i % 2][:, 0:n], o[:, 0:n], ACT.Square).then_inc(qk_squared, 1)
                if i:
                    root(i - 1)
            root(len(ITEMS) - 1)
            for c in range(4):
                round_weights(len(SPLIT_A) + c + 10)
                free(A(UT[:, c, :], arrived(act, ("f", c))[:, :], ACT.Copy), ("f", c))
            for c in range(8):
                if c < 6:
                    round_weights(len(SPLIT_A) + c + 14)
                A(GATE[:, c, :], arrived(act, ("g2", c))[:, :], ACT.Tanh, scale=0.5).then_inc(gate2_tanh, 1)
            for t in range(NT):
                for gp in range(2):
                    o = arrived(act, ("uc", t, gp)).rearrange("p (g s n) -> p g s n", g=2, s=2)
                    dst = UC[:, t, :, gp * 256:(gp + 1) * 256].rearrange("p s (g n) -> p g s n", g=2)
                    free(A(dst, o, ACT.Copy), ("uc", t, gp))
            for g in range(4):
                free(A(YF[:, g, :], arrived(act, ("yf", g))[:, :], ACT.Copy), ("yf", g))
            def round_mx(c):
                A(MXHI[c][:, :], MIX[:, c, :], ACT.Copy).then_inc(mx_rounded, 1)

            def round_w2(i):
                n = len(stream) - 4 + i
                act.wait_ge(weights_here[n % 3], 16 * (n // 3 + 1))
                A(W2HI[i][:, :], WR[n % 3], ACT.Copy).then_inc(w2_rounded, 1)

            for c in range(4):
                stored(act, ("fo", c))
                round_mx(c)
            for n in range(NT * NAH):
                if n in (4, 8, 12):
                    round_w2(n // 4 - 1)
                act.wait_ge(masked, n + 1)
                nm = MXN2[:, n % 4:n % 4 + 1]
                A(PB[n % 4][:, 0:WIN], PB[n % 4][:, 0:WIN], ACT.Exp, bias=nm, accum_out=SUMS[:, 8 + n:9 + n])
                free(A(PB[n % 4][:, WIN:512], banks[where["s", n][0]][:, WIN:512], ACT.Exp, bias=nm,
                       accum_out=SUMS[:, 40 + n:41 + n]), ("s", n))
            stored(act, ("oT", 3))
            for c in range(4, KT):
                round_mx(c)
            arrived(act, ("z", 0, 1))
            round_w2(3)

        @block.vector
        def _(dve):
            TT, TS, STT = nc.vector.tensor_tensor, nc.vector.tensor_scalar, nc.vector.scalar_tensor_tensor
            own = Steps(dve, dve_steps)
            own.did(nc.vector.memset(CST, 0.0))
            own.did(nc.vector.memset(HT[:, :, 0:1], 0.0))
            dve.wait_ge(consts_here, 32)
            own.did(TS(HVEC, VECS[:, VEC["w0"]:VEC["w0"] + 2 * KT], 0.5, None, MUL))
            own.did(TS(NKA, VECS[:, VEC["k_a"]:VEC["k_a"] + KT], -1.0, 1.0, MUL, ADD))
            TT(RKB, VECS[:, VEC["r_k"]:VEC["r_k"] + KT].unsqueeze(2).broadcast_to([P, KT, 2]),
               heads1[:, 0:P:HD].unsqueeze(1).broadcast_to([P, KT, 2]), MUL).then_inc(vectors_ready, 1)
            for t in range(NT):
                dve.wait_ge(x_squared, t + 1)
                own.own(nc.vector.reciprocal(rstd[:, t:t + 1], rstd[:, t:t + 1]))
                TS(V[:, t, :], V[:, t, :], rstd[:, t:t + 1], None, MUL).then_inc(x_scaled, 1)
            dve.wait_ge(c_tanh, 1)
            own.own(TS(SILT[:, 16:32], SILT[:, 0:16], 0.5, 0.5, MUL, ADD))
            own.did(TT(SILC.rearrange("p c k -> p k c"), SILT[:, 16:32].rearrange("p (k c) -> p k c", k=2),
                       VECS[:, VEC["c"]:VEC["c"] + 16].rearrange("p (k c) -> p k c", k=2), MUL))
            for c in range(KT):
                stored(dve, ("hT", c))
                own.did(TT(DX[:, c, :], HT[:, c, 0:T], HT[:, c, 1:T + 1], SUB))
            own.wait()

            def mix(m):
                for c in range(KT):
                    ins = STT(MIXES[m][:, c, :], DX[:, c, :], vec("mu_" + "wakrvg"[m], c), HT[:, c, 1:T + 1], MUL, ADD)
                    ins.then_inc(mix_rough if m in XHI else mixed, 1)

            def split_mix(m, c):
                dve.wait_ge(mix_rounded, KT * nth_split[m] + c + 1)
                TT(XLO[m][c][:, :], MIXES[m][:, c, :], XHI[m][c][:, :].bitcast(f32), SUB).then_inc(mixed, 1)

            for m in range(3):
                mix(m)
            for c in range(KT):
                split_mix(2, c)
            arrived(dve, ("low", 1))
            mix(3)
            for c in range(KT):
                split_mix(3, c)
                stored(dve, ("k", c))
                TS(AR[:, 0, c, :], KB[:, c, :], vec("k_k", c), None, MUL).then_inc(k_scaled, 1)
            arrived(dve, ("k", 7))
            mix(4)
            for c in range(KT):
                stored(dve, ("kss", c))
                own.own(TS(ROOT[c % 2], ROOT[c % 2], 1e-12, None, MAX))
                own.own(nc.vector.reciprocal(ROOT[c % 2], ROOT[c % 2]))
                TT(AR[:, 0, c, :], AR[:, 0, c, :], ROOT[c % 2], MUL).then_inc(kk_done, 1)
            mix(5)

            def gate(cc):
                dve.wait_ge(gate_tanh, cc + 1)
                free(STT(GT[:, cc, :], SQ2[cc % 2], 1.0, arrived(dve, ("g", cc))[:, :], ADD, MUL), ("g", cc))

            PARTS = [(1, 5), (5, 8), (8, 11), (11, 13), (13, 15), (15, 16)]

            def solve(q, part):
                if part == 0:
                    if q:
                        dve.wait_ge(inv_out, 16 * q)
                    own.own(nc.vector.memset(XO[:, 0], 0.0))
                    own.did(nc.vector.memset(XO[:, 0].rearrange("p a b -> p (a b)")[:, 0:BLK * BLK:BLK + 1], 1.0))
                    dve.wait_ge(lt_back, 16 * (q + 1))
                    own.wait()
                for i in range(*PARTS[part]):
                    tmp = XTMP[:, 0:i * i].rearrange("p (k j) -> p k j", k=i)
                    own.own(TT(tmp, XO[:, 0, 0:i, 0:i].rearrange("p j k -> p k j"),
                               LTB[:, 0:i, i].unsqueeze(1).broadcast_to([P, i, i]), MUL))
                    own.own(nc.vector.tensor_reduce(XO[:, 0, i, 0:i], tmp, AX.X, ADD))
                if part == 5:
                    nc.vector.tensor_copy(XO[:, 1], XO[:, 0].rearrange("p a b -> p b a")).then_inc(inverted, 1)

            dve.wait_ge(kk_done, KT)
            for c in range(KT):
                stored(dve, ("w", c))
                own.own(TS(SIGW, SIGW, 0.5, 0.5, MUL, ADD))
                for j in range(4):
                    at = slice(j * P, (j + 1) * P)
                    own.did(nc.vector.tensor_tensor_scan(CSUM[:, at], con("ones"), SIGW[:, at], 0.0, MUL, ADD))
                own.wait()
                csum = CSUM.rearrange("p (j t) -> p j t", j=4)
                if c:
                    dve.wait_ge(decays_ready, c)
                own.own(nc.vector.tensor_copy(MID[:, 0:4], csum[:, :, HD - 1]))
                TT(csum, csum, MID[:, 0:4].unsqueeze(2).broadcast_to([P, 4, P]), SUB).then_inc(csum_ready, 1)
                stored(dve, ("a", c))
                TS(AB[:, c, :], AB[:, c, :], 0.5, 0.5, MUL, ADD).then_inc(a_ready, 1)
                dve.wait_ge(a_ready, c + 1)
                dve.wait_ge(kmod_ready, c + 1)
                own.own(TT(AB[:, c, :], AB[:, c, :], AR[:, 0, c, :], MUL))
                dve.wait_ge(decays_ready, c + 1)
                own.did(TT(AB[:, c, :], AB[:, c, :], E2, MUL))
                a4 = AR[:, 0, c, :].rearrange("p (j t) -> p j t", j=4)
                own.did(STT(a4, a4, -1.0, E1[:, :, 0:P], MUL, MUL))
                own.did(TT(F[:, c, 0:3], E1[:, 0:3, P], MID[:, 5:8], MUL))
                dve.wait_ge(rk_ready, c + 1)
                r4 = AR[:, 1, c, :].rearrange("p (j t) -> p j t", j=4)
                TT(r4, r4, E1[:, :, 1:P + 1], MUL).then_inc(ab_ready, 1)
                if c >= 4:
                    gate(2 * (c - 4))
                    gate(2 * (c - 4) + 1)
                if c < 4:
                    split_mix(5, 2 * c)
                    split_mix(5, 2 * c + 1)
                if c in (5, 6):
                    for part in range(6):
                        solve(c - 5, part)
            free(nc.vector.tensor_copy(BON, arrived(dve, "bonus")[:, 0:64]), "bonus")
            nc.vector.tensor_copy(CST[:, 1:2], CST[:, 5:6]).then_inc(dve_phase, 1)
            others_done(dve, 1, dve_phase)

            def mask_gram(g, u):
                o = arrived(dve, ("gram", g, u)).rearrange("p (s n) -> p s n", s=2)
                free(TT(GM[g % 3][:, u, :].rearrange("p (s n) -> p s n", s=2), o,
                        gram_mask.unsqueeze(1).broadcast_to([P, 2, 2 * P]), MUL), ("gram", g, u))

            def mask_z(g, l, hf):
                dve.wait_ge(z_ready[hf], LEVELS * g + l + 1)
                b = BLK << l
                m = con("level")[:, l * HD:(l + 1) * HD].rearrange("p (m b) -> p m b", b=b)
                z = halves2(banks[hf][:, 0:2 * P].rearrange("p (u n) -> p u n", u=2), b, 0)
                TT(halves2(YL[:, l, 2 * hf:2 * hf + 2, :], b, 0), z, m.unsqueeze(1).broadcast_to([P, 2, HD // b, b]),
                   MUL).then_inc(y_ready[hf], 1)

            def add_x(g, l, hf):
                dve.wait_ge(x_grown[hf], LEVELS * g + l + 1)
                b = BLK << l
                for w in range(0 if l < LEVELS - 1 else 1, 2):
                    x = halves2(XS[:, g % 2, 2 * hf:2 * hf + 2, w, :], b, w)
                    ins = TT(x, x, corner(hf, w).rearrange("p u (m b) -> p u m b", b=b), ADD)
                ins.then_inc(x_added[hf], 1)

            def update(g, q):
                j, cc = divmod(g, 4)
                c = 2 * cc + q
                if j == NT - 1:
                    return
                dve.wait_ge(ys_ready[q], g + 1)
                s = banks[6 + q][:, 3 * P:4 * P]
                if j == 0:
                    STT(ST[:, c, :], s, F[:, c, j:j + 1], heads1, MUL, MUL).then_inc(s_updated[q], 1)
                else:
                    own.own(STT(STMP[:, q, :], s, F[:, c, j:j + 1], heads1, MUL, MUL))
                    STT(ST[:, c, :], ST[:, c, :], F[:, c, j:j + 1], STMP[:, q, :], MUL, ADD).then_inc(s_updated[q], 1)

            arrived(dve, "bonus")
            for u in range(4):
                mask_gram(0, u)
            dve.wait_ge(y_zeroed, 1)
            def centre(j):
                for q in range(2):
                    dve.wait_ge(y_copied[q], 4 * (j + 1))
                own.own(nc.vector.tensor_reduce(stat(0, j), heads_of(YT[j]), AX.X, ADD))
                own.own(TS(stat(0, j), stat(0, j), 1.0 / HD, None, MUL))
                TT(heads_of(YT[j]), heads_of(YT[j]), bc(stat(0, j)), SUB).then_inc(centred, 1)

            def finish_y(j, h):
                stored(dve, ("yT", j, h))
                o = arrived(dve, ("bT", j, h))
                y = YG[j][:, 4 * h:4 * h + 4, :]
                free(TT(y, y, o.rearrange("p (c n) -> p c n", c=4), ADD), ("bT", j, h))
                stored(dve, ("bT", j, h))
                STT(y, y, 0.5, GT[:, 4 * h:4 * h + 4, j * P:(j + 1) * P], MUL, MUL).then_inc(y_gated, 1)

            def take_mods():
                o = arrived(dve, "mods")
                b2 = VECS[:, VEC["b_shift"]:VEC["b_shift"] + 24].unsqueeze(2).broadcast_to([P, 24, 2])
                free(TT(MODS, o[:, 256:304].rearrange("p (c k) -> p c k", k=2), b2, ADD), "mods")
                stored(dve, "mods")
                own.own(TS(GSC, MODS[:, 8:16, :], 1.0, None, ADD))
                TT(GSC, GSC, VECS[:, VEC["norm2"]:VEC["norm2"] + 8].unsqueeze(2).broadcast_to([P, 8, 2]), MUL)\
                    .then_inc(mods_ready, 1)

            stat = lambda i, j: GST[:, 64 * i + 16 * j:64 * i + 16 * j + 16]
            bc = lambda a: a.unsqueeze(2).broadcast_to([P, HEADS, HD])
            heads_of = lambda a: a.rearrange("p (h n) -> p h n", n=HD)
            for g in range(GROUPS + 4):
                now, nxt, old = g < GROUPS, g + 1 < GROUPS, 0 < g <= GROUPS
                turning = g in (8, 12, 16)
                for l in range(LEVELS):
                    if now:
                        mask_z(g, l, 0)
                        mask_z(g, l, 1)
                    if nxt:
                        mask_gram(g + 1, l)
                    if g < 2:
                        solve(2 + g, 2 * l)
                    if now:
                        add_x(g, l, 0)
                        add_x(g, l, 1)
                    if g < 2:
                        solve(2 + g, 2 * l + 1)
                    if old and l == 1:
                        update(g - 1, 0)
                    if nxt and l == 1:
                        mask_gram(g + 1, 3)
                    if turning and l == 1:
                        finish_y(g // 4 - 2, 0)
                    if old and l == 2:
                        update(g - 1, 1)
                if turning:
                    finish_y(g // 4 - 2, 1)
                j = g // 4 - 1
                if g >= 5 and g % 4 == 1:
                    centre(j)
                if g >= 6 and g % 4 == 2:
                    dve.wait_ge(gn_squared, j + 1)
                    nc.vector.tensor_reduce(stat(1, j), heads_of(SQ), AX.X, ADD).then_inc(gn_sums, 1)
                if g >= 7 and g % 4 == 3:
                    dve.wait_ge(gn_root, j + 1)
                    own.own(nc.vector.reciprocal(stat(2, j), stat(2, j)))
                    TT(heads_of(YT[j]), heads_of(YT[j]), bc(stat(2, j)), MUL).then_inc(y_normed, 1)
                if g == 13:
                    take_mods()
            dve.wait_ge(x_again, 16)

            def make_x1(t, h):
                at = slice(512 * h, 512 * h + 512)
                free(TT(X1[:, t, at], arrived(dve, ("o", t, h))[:, :], XR[:, t, at], ADD), ("o", t, h))

            for t in range(3):
                make_x1(t, 0)
            finish_y(3, 0)
            finish_y(3, 1)
            make_x1(3, 0)
            dve.wait_ge(cn_root, 1)
            own.own(nc.vector.reciprocal(SUMS[:, 2:4], SUMS[:, 2:4]))
            for t in range(2):
                TS(CX[:, t, :], CX[:, t, :], SUMS[:, 2 + t:3 + t], None, MUL).then_inc(cn_ready, 1)

            def norm_x1(t):
                dve.wait_ge(n2_root, t + 1)
                own.own(nc.vector.reciprocal(rstd[:, t:t + 1], rstd[:, t:t + 1]))
                TS(XN[:, t, :], X1[:, t, :], rstd[:, t:t + 1], None, MUL).then_inc(xn_ready, 1)

            make_x1(0, 1)
            for t in range(1, NT):
                make_x1(t, 1)
                norm_x1(t - 1)
            norm_x1(NT - 1)

            def head_dst(i):
                name, c = ITEMS[i]
                return {"q": QT[:, c, :], "kk": KTP[:, c, HD:HD + T], "ck": CK[:, c, :]}[name]

            def scale_heads(i):
                n = CTX if ITEMS[i][0] == "ck" else T
                stored(dve, ("ss", i))
                r = DROOT[i % 2][:, 0:n]
                own.own(nc.vector.reciprocal(r, r))
                stored(dve, ITEMS[i])
                TT(head_dst(i), head_dst(i), r, MUL).then_inc(qk_done, 1)

            def split_w(i):
                n = SPLIT_D[i]
                dve.wait_ge(weights_rounded, len(SPLIT_A) + i + 1)
                TT(WLO[n % 3][:, :], WR[n % 3][:, 0:1024], WHI[n % 3][:, :].bitcast(f32), SUB)\
                    .then_inc(weights_split_d, 1)

            for i, key in enumerate(ITEMS):
                n = CTX if key[0] == "ck" else T
                if i == 4:
                    for c in range(KT):
                        dve.wait_ge(xn_rounded, c + 1)
                        TT(XNLO[c][:, :], XNP[:, c, HD:HD + T], XNHI[c][:, :].bitcast(f32), SUB).then_inc(xn_split, 1)
                    split_w(0)
                    split_w(1)
                if i >= 4:
                    split_w(i - 4 + 2)
                dve.wait_ge(qk_squared, i + 1)
                g = VECS[:, VEC["q_gain"]:VEC["q_gain"] + 1] if key[0] == "q" else \
                    VECS[:, VEC["k_gain"]:VEC["k_gain"] + 1]
                free(TS(head_dst(i), arrived(dve, key)[:, 0:n], g, None, MUL), key)
                if i:
                    scale_heads(i - 1)
            scale_heads(len(ITEMS) - 1)
            for c in range(4):
                split_w(c + 10)
            for c in range(8):
                if c < 6:
                    split_w(c + 14)
                dve.wait_ge(gate2_tanh, c + 1)
                free(STT(GATE[:, c, :], GATE[:, c, :], 1.0, arrived(dve, ("g2", c))[:, :], ADD, MUL), ("g2", c))
            arrived(dve, ("yf", 3))
            for h in range(2):
                TT(GDIAG[h].rearrange("p (c n) -> p c n", c=4), ident.unsqueeze(1).broadcast_to([P, 4, P]),
                   MODS[:, 16 + 4 * h:20 + 4 * h, 0:1].broadcast_to([P, 4, P]), MUL).then_inc(gdiag_ready, 1)
            for n in range(4):
                stored(dve, ("g2", n))
                o = arrived(dve, ("fo", n)).rearrange("p (col r) -> p col r", r=GH)
                free(STT(MIX[:, n, :].rearrange("p (r col) -> p col r", r=GH), o, 0.5,
                         GATE[:, n, :].rearrange("p (col r) -> p col r", r=GH), MUL, MUL), ("fo", n))
            for h in range(2):
                free(nc.vector.tensor_copy(GX[:, 512 * h:512 * h + 512], arrived(dve, ("gx", h))[:, :]), ("gx", h))

            def mask_scores(n):
                qt, h = divmod(n, NAH)
                o = arrived(dve, ("s", n))
                if n >= 4:
                    arrived(dve, ("pt", n - 4))
                if n >= 4:
                    stored(dve, ("s", n - 4))
                m = MXN[:, 2 * (n % 4):2 * (n % 4) + 1]
                m2 = MXN[:, 2 * (n % 4) + 1:2 * (n % 4) + 2]
                own.own(nc.vector.tensor_reduce(m, o[:, WIN:512], AX.X, MAX))
                own.own(nc.vector.tensor_tensor_reduce(
                    out=PB[n % 4][:, 0:WIN], in0=o[:, 0:WIN], in1=BM[:, (0, 1, 1, 2)[qt], h, :], scale=1.0, scalar=m,
                    op0=ADD, op1=MAX, accum_out=m2))
                TS(MXN2[:, n % 4:n % 4 + 1], m2, -1.0, None, MUL).then_inc(masked, 1)

            def copy_turned_probs(n):
                o = arrived(dve, ("pt", n))
                if n >= 3:
                    k = n - 3
                    if k % NAH == NAH - 1:
                        arrived(dve, ("at", k // NAH))
                    else:
                        dve.wait_ge(pv_done, (k // NAH) * (NAH - 1) + k % NAH + 1)
                free(nc.vector.tensor_copy(PT[n % 3], o[:, :]), ("pt", n))

            def scale_out(qt):
                s1, s2 = SUMS[:, 8 + 8 * qt:16 + 8 * qt], SUMS[:, 40 + 8 * qt:48 + 8 * qt]
                own.own(TT(s1, s1, s2, ADD))
                own.own(nc.vector.reciprocal(s1, s1))
                o = arrived(dve, ("at", qt)).rearrange("p (h n) -> p h n", h=NAH)
                if qt:
                    arrived(dve, ("oT", qt - 1))
                free(TT(ON.rearrange("p (h n) -> p h n", h=NAH), o, s1.unsqueeze(2).broadcast_to([P, NAH, HD]), MUL),
                     ("at", qt))

            def gate_out(qt):
                o = arrived(dve, ("oT", qt)).rearrange("p (c col r) -> p c col r", c=4, r=GH)
                g = GATE[:, 4:8, qt * P:(qt + 1) * P].rearrange("p c (col r) -> p c col r", r=GH)
                dst = MIX[:, 4:8, :].rearrange("p c (r col) -> p c col r", r=GH)[:, :, 16 * qt:16 * qt + 16, :]
                for i in range(4):
                    ins = STT(dst[:, i], o[:, i], 0.5, g[:, i], MUL, MUL)
                    if i < 3:
                        own.did(ins)
                free(ins, ("oT", qt))

            dve.wait_ge(bm_ready, 1)
            NU = NT * NAH
            for n in range(NU + 7):
                if n < NU:
                    mask_scores(n)
                if 2 <= n < NU + 2:
                    copy_turned_probs(n - 2)
                if n >= NAH + 3 and (n - NAH - 3) % NAH == 0:
                    scale_out((n - NAH - 3) // NAH)
                if n >= NAH + 6 and (n - NAH - 6) % NAH == 0:
                    gate_out((n - NAH - 6) // NAH)
            for c in range(4, KT):
                dve.wait_ge(mx_rounded, c + 1)
                TT(MXLO[c][:, :], MIX[:, c, :], MXHI[c][:, :].bitcast(f32), SUB).then_inc(mx_split_d, 1)
            for i in range(8):
                nb, th = divmod(i, 2)
                o = arrived(dve, ("z", nb, th)).rearrange("p (j n) -> p j n", j=2)
                if i >= 4:
                    dve.wait_ge(out_stored[i % 4], 16)
                free(TT(OUTB[i % 4], o, GX[:, nb * 256:(nb + 1) * 256].unsqueeze(1).broadcast_to([P, 2, 256]), MUL),
                     ("z", nb, th))

        @block.gpsimd
        def _(pool):
            TT, TS = nc.gpsimd.tensor_tensor, nc.gpsimd.tensor_scalar
            own = Steps(pool, pool_steps)
            def split_w(i):
                n = SPLIT_A[i]
                pool.wait_ge(weights_rounded, i + 1)
                TT(WLO[n % 3][:, :], WR[n % 3][:, 0:1024], WHI[n % 3][:, :].bitcast(f32), SUB)\
                    .then_inc(weights_split, 1)

            for i in range(2 * KT):
                split_w(i)
            pool.wait_ge(vectors_ready, 1)
            for c in range(KT):
                pool.wait_ge(a_ready, c + 1)
                TS(KMOD, AB[:, c, :], vec("k_a", c), NKA[:, c:c + 1], MUL, ADD).then_inc(kmod_ready, 1)
                pool.wait_ge(kmod_ready, c + 1)
                stored(pool, ("k", c))
                own.own(TT(KB[:, c, :], KB[:, c, :], KMOD, MUL))
                stored(pool, ("r", c))
                if c:
                    pool.wait_ge(bonus_done, c)
                TT(RKT, KB[:, c, :], AR[:, 1, c, :], MUL).then_inc(rk_ready, 1)
                pool.wait_ge(decays_ready, c + 1)
                pool.wait_ge(rk_ready, c + 1)
                TT(KB[:, c, :], KB[:, c, :], E2, MUL).then_inc(kappa_ready, 1)
                if 3 <= c < 7:
                    split_w(2 * KT + 2 * (c - 3))
                    split_w(2 * KT + 2 * (c - 3) + 1)
            pool.wait_ge(kappa_ready, KT)
            TT(CST[:, 3:4], CST[:, 6:7], CST[:, 6:7], ADD).then_inc(pool_phase, 1)
            others_done(pool, 1, pool_phase)
            arrived(pool, "bonus")
            nc.gpsimd.memset(YL, 0.0).then_inc(y_zeroed, 1)
            blocks = con("blocks").rearrange("p (m n) -> p m n", n=BLK).unsqueeze(1).broadcast_to([P, 2, P // BLK, BLK])

            def expand(g):
                j, cc = divmod(g, 4)
                if g < BATCHES:
                    pool.wait_ge(inv_back[cc], 32)
                if g >= 2:
                    for q in range(2):
                        pool.wait_ge(sa_ready[q], g - 1)
                for u in range(4):
                    ins = TT(XS[:, g % 2, u].rearrange("p s (m n) -> p s m n", n=BLK),
                             XST[:, cc, :, u * NT + j, :].unsqueeze(2).broadcast_to([P, 2, P // BLK, BLK]), blocks, MUL)
                ins.then_inc(expanded, 1)

            def bonus_v(j):
                for q in range(2):
                    pool.wait_ge(ys_ready[q], 4 * (j + 1))
                v = V[:, j, :].rearrange("p (h n) -> p h n", n=HD)
                TT(v, v, BON[:, 16 * j:16 * j + 16].unsqueeze(2).broadcast_to([P, HEADS, HD]), MUL).then_inc(bv_ready, 1)

            for g in range(GROUPS):
                expand(g)
                if g >= 6 and g % 4 == 2:
                    bonus_v(g // 4 - 1)
            bonus_v(NT - 1)
            own.did(nc.gpsimd.memset(XNP[:, :, 0:HD], 0.0))
            own.did(nc.gpsimd.memset(XNP[:, :, HD + T:PADT], 0.0))
            stored(pool, ("o", 3, 1))
            own.did(nc.gpsimd.memset(KTP[:, :, 0:HD], 0.0))
            nc.gpsimd.memset(KTP[:, :, HD + T:PADT], 0.0).then_inc(pads_ready, 1)
            pool.wait_ge(rel_here, 16 * 17)
            near_v = NEAR.rearrange("p (v a b) -> p v a b", v=3, b=GH)
            for v in range(3):
                for h in range(NAH):
                    r = REL[:, h * RBW:h * RBW + 1]
                    bias = bass.AP(r.tensor, r.offset + 7 * 31, [list(r.ap[0]), [1, 32], [-31, GH]])
                    ins = TT(BM[:, v, h, :].rearrange("p (a b) -> p a b", b=GH), bias, near_v[:, v], ADD)
                    if (v, h) != (2, NAH - 1):
                        own.did(ins)
            ins.then_inc(bm_ready, 1)

            def split_w2(i):
                slot = (len(stream) - 4 + i) % 3
                pool.wait_ge(w2_rounded, i + 1)
                TT(W2LO[slot][:, :], WR[slot], W2HI[i][:, :].bitcast(f32), SUB).then_inc(w2_split, 1)

            for c in range(4):
                pool.wait_ge(mx_rounded, c + 1)
                TT(MXLO[c][:, :], MIX[:, c, :], MXHI[c][:, :].bitcast(f32), SUB).then_inc(mx_split, 1)
            for i in range(3):
                split_w2(i)
            for i in range(8):
                nb, th = divmod(i, 2)
                if i == 2:
                    split_w2(3)
                stored(pool, ("z", nb, th))
                at = slice(nb * 256, (nb + 1) * 256)
                TT(OUTB[i % 4], OUTB[i % 4], X1[:, 2 * th:2 * th + 2, at], ADD).then_inc(out_ready, 1)


_OUT = (1, T, D)


def kernel(**inputs):
    import concourse.bacc as bacc
    from concourse.bass_utils import run_bass_kernel_spmd as run

    g = {k: np.ascontiguousarray(v) for k, v in inputs.items()}
    f = np.float32

    def rows(a):
        return a.reshape(-1, P).T

    mu = g["l0_mu"]
    parts = [rows(g["l0_norm"])] + [rows(mu[i]) for i in range(6)]
    parts += [rows(g["l0_" + n]) for n in ("w0", "a0", "k_k", "k_a", "r_k", "gn_w", "gn_b")]
    parts += [rows(g["c_2"]), rows(g["c_ctx_2"]), rows(g["norm_g_2"]), rows(g["b_ada_2"][0])]
    parts += [np.tile(g["q_norm_g_2"][0], 2)[:, None], np.tile(g["k_norm_g_2"][0], 2)[:, None]]
    consts, cos_t, nsin_t, near = shape_constants()
    arrays = {
        "x": g["x"][0], "vecs": np.concatenate(parts, 1), "consts": consts, "cos_t": cos_t, "nsin_t": nsin_t,
        "near": near,
        "w_in": g["l0_w_in"], "w_up": g["l0_w_up"], "a_up": g["l0_a_up"], "w_out": g["l0_w_out"],
        "ctx_x": g["ctx_2"][0], "w_ada": g["w_ada_2"][0],
        "w_in2": g["w_in_2"][0], "w_four": g["w_four_2"][0],
        "rel_bias": np.pad(g["rel_bias_2"][0][:, ::-1].reshape(NAH, RB), ((0, 0), (RBPAD, RBPAD))),
        "w_out2": g["w_out_2"][0],
    }
    arrays = {k: np.ascontiguousarray(v) for k, v in arrays.items()}
    nc = bacc.Bacc("TRN2", target_bir_lowering=False, num_devices=1)
    args = [nc.dram_tensor(k, v.shape, mybir.dt.from_np(v.dtype), kind="ExternalInput").ap()
            for k, v in arrays.items()]
    out = nc.dram_tensor("out", (T, D), mybir.dt.float32, kind="ExternalOutput").ap()
    lt_dram = nc.dram_tensor("lt_dram", (HEADS * NT * (P + 1), P), mybir.dt.float32, kind="Internal").ap()
    inv_dram = nc.dram_tensor("inv_dram", (BATCHES * 2 * P, BLK * BLK), mybir.dt.float32, kind="Internal").ap()
    rwkv_then_grid_block(nc, *args, out, lt_dram, inv_dram)
    r = run(nc, [arrays], core_ids=[0])
    return r.results[0]["out"].reshape(_OUT)
```
